# Optimizing a Trainium2 kernel written in Bass

```python
import jax, jax.numpy as jnp
from jax import lax
import numpy as np
import math

D_MODEL = 1024
BATCH = 1
SEQ = 256
DEPTH = 2

N_A = DEPTH // 2
N_B = DEPTH - N_A
PLE_DIM = 256
EPS = 1e-6
NEG = -1e30
BIG = 1e30

RET_HEADS = D_MODEL // 256
RET_QK_DIM = D_MODEL // RET_HEADS
RET_V_DIM = 2 * RET_QK_DIM
RET_QK_W = RET_HEADS * RET_QK_DIM
RET_V_W = RET_HEADS * RET_V_DIM
RET_CHUNK = 128
ROPE_BASE = 10000.0

NSA_DK = 128
NSA_DV = 128
NSA_W = 2 * D_MODEL
NSA_HEADS = NSA_W // NSA_DV
NSA_GROUPS = 4
NSA_HPG = NSA_HEADS // NSA_GROUPS
NSA_KV_W = NSA_GROUPS * NSA_DK
CMP_LEN = 32
CMP_STRIDE = 16
CMP_HIDDEN = 256
SEL_BLOCK = 64
N_SEL = 16
WIN = 512
Q_BLOCK = 128


def rmsnorm(x, g):
    xf = x.astype(jnp.float32)
    y = xf * lax.rsqrt(jnp.mean(xf * xf, axis=-1, keepdims=True) + EPS)
    return (y * g.astype(jnp.float32)).astype(x.dtype)

def rotary(x, pos):
    half = x.shape[-1] // 2
    inv = ROPE_BASE ** (-jnp.arange(half, dtype=jnp.float32) / half)
    ang = pos.astype(jnp.float32)[:, None] * inv[None, :]
    cos, sin = jnp.cos(ang), jnp.sin(ang)
    x1, x2 = x[..., :half], x[..., half:]
    return jnp.concatenate([x1 * cos - x2 * sin, x1 * sin + x2 * cos], axis=-1)

def retention_chunkwise(q, k, v):
    b, h, t, _ = q.shape
    nc = t // RET_CHUNK
    lg = jnp.log1p(-(2.0 ** (-5.0 - jnp.arange(h, dtype=jnp.float32))))
    pos = jnp.arange(RET_CHUNK, dtype=jnp.float32)
    diff = pos[:, None] - pos[None, :]
    decay = jnp.where(diff[None] >= 0,
                      jnp.exp(jnp.maximum(diff, 0.0)[None] * lg[:, None, None]), 0.0)
    q_dec = jnp.exp((pos + 1.0)[None, :] * lg[:, None])
    k_dec = jnp.exp((RET_CHUNK - 1.0 - pos)[None, :] * lg[:, None])
    chunk_dec = jnp.exp(RET_CHUNK * lg)

    def to_chunks(a):
        return jnp.moveaxis(a.reshape(b, h, nc, RET_CHUNK, a.shape[-1]), 2, 0)

    def step(state, qkv):
        qc, kc, vc = qkv
        s = jnp.einsum('bhnd,bhmd->bhnm', qc, kc) * decay
        o = (jnp.einsum('bhnm,bhmv->bhnv', s, vc)
             + jnp.einsum('bhnd,bhdv->bhnv', qc, state) * q_dec[..., None])
        state = (state * chunk_dec[:, None, None]
                 + jnp.einsum('bhmd,bhmv->bhdv', kc * k_dec[..., None], vc))
        return state, o

    state0 = jnp.zeros((b, h, q.shape[-1], v.shape[-1]), jnp.float32)
    _, o = lax.scan(step, state0, (to_chunks(q), to_chunks(k), to_chunks(v)))
    return jnp.moveaxis(o, 0, 2).reshape(b, h, t, v.shape[-1])

def retention_layer(h, g_norm, w_in, gn_gain, w_out):
    b, t, _ = h.shape
    proj = rmsnorm(h, g_norm) @ w_in
    q, k, v, gate = jnp.split(proj, [RET_QK_W, 2 * RET_QK_W, 2 * RET_QK_W + RET_V_W], axis=-1)

    def heads(a, d):
        return a.reshape(b, t, RET_HEADS, d).transpose(0, 2, 1, 3).astype(jnp.float32)

    pos = jnp.arange(t)
    q = rotary(heads(q, RET_QK_DIM), pos)
    k = rotary(heads(k, RET_QK_DIM), pos) * (RET_QK_DIM ** -0.5)
    o = retention_chunkwise(q, k, heads(v, RET_V_DIM))
    mu = jnp.mean(o, axis=-1, keepdims=True)
    var = jnp.mean(jnp.square(o - mu), axis=-1, keepdims=True)
    o = ((o - mu) * lax.rsqrt(var + EPS)).transpose(0, 2, 1, 3).reshape(b, t, RET_V_W)
    o = o * gn_gain.astype(jnp.float32)
    y = (jax.nn.silu(gate.astype(jnp.float32)) * o).astype(h.dtype) @ w_out
    return h + y

def per_layer_embedding(h, p_i, g, w_gate, w_emb):
    gate = jax.nn.sigmoid(rmsnorm(h, g) @ w_gate)
    return h + gate * (p_i @ w_emb)

def compress_blocks(a, pe, w1, w2):
    b, g, t, d = a.shape
    lc = CMP_LEN // CMP_STRIDE
    n_cmp = (t - CMP_LEN) // CMP_STRIDE + 1
    sub = a.reshape(b, g, t // CMP_STRIDE, CMP_STRIDE, d)
    blocks = jnp.concatenate([sub[:, :, o:o + n_cmp] for o in range(lc)], axis=3)
    blocks = (blocks + pe).reshape(b, g, n_cmp, CMP_LEN * d)
    return jax.nn.gelu(blocks @ w1) @ w2

def nsa_shared_kv(h, g_kv, w_kv, pe_k, w1_k, w2_k, pe_v, w1_v, w2_v):
    b, t, _ = h.shape
    proj = rmsnorm(h, g_kv) @ w_kv
    parts = proj.reshape(b, t, 6, NSA_GROUPS, NSA_DK).transpose(2, 0, 3, 1, 4)
    kc, vc, ks, vs, kw, vw = parts[0], parts[1], parts[2], parts[3], parts[4], parts[5]
    k_cmp = compress_blocks(kc, pe_k, w1_k, w2_k)
    v_cmp = compress_blocks(vc, pe_v, w1_v, w2_v)
    nslc = t // SEL_BLOCK
    k_sel = ks.reshape(b, NSA_GROUPS, nslc, SEL_BLOCK * NSA_DK)
    v_sel = vs.reshape(b, NSA_GROUPS, nslc, SEL_BLOCK * NSA_DV)
    pad = ((0, 0), (0, 0), (WIN, 0), (0, 0))
    return (k_cmp, v_cmp, k_sel, v_sel, jnp.pad(kw, pad), jnp.pad(vw, pad))

def selection_importance(p, nslc):
    f = SEL_BLOCK // CMP_STRIDE
    lc = CMP_LEN // CMP_STRIDE
    left = lc - 1
    right = f * nslc - p.shape[-1]
    pp = jnp.pad(p, ((0, 0), (0, 0), (0, 0), (left, right)))
    terms = []
    for o in range(-(lc - 1), f):
        w = float(min(o + lc, f) - max(o, 0))
        s = left + o
        terms.append(w * pp[..., s:s + f * (nslc - 1) + 1:f])
    return sum(terms[1:], terms[0])

def nsa_query_block(q, gates, blk, k_cmp, v_cmp, k_sel, v_sel, k_win, v_win):
    b = q.shape[0]
    scale = NSA_DK ** -0.5
    t = blk * Q_BLOCK + jnp.arange(Q_BLOCK)

    n_cmp = k_cmp.shape[2]
    cmp_end = jnp.arange(n_cmp) * CMP_STRIDE + CMP_LEN - 1
    valid_c = cmp_end[None, :] <= t[:, None]
    s_c = jnp.einsum('bgrqd,bgnd->bgrqn', q, k_cmp).astype(jnp.float32) * scale
    p_c = jnp.where(valid_c, jax.nn.softmax(jnp.where(valid_c, s_c, NEG), axis=-1), 0.0)
    o_c = jnp.einsum('bgrqn,bgnd->bgrqd', p_c, v_cmp.astype(jnp.float32))

    nslc = k_sel.shape[2]
    n_top = min(N_SEL, nslc)
    imp = selection_importance(jnp.sum(p_c, axis=2), nslc)
    cur = (t // SEL_BLOCK)[:, None]
    j = jnp.arange(nslc)[None, :]
    forced = (j == 0) | (j == cur) | (j == cur - 1)
    score = jnp.where(j <= cur, jnp.where(forced, BIG, imp), -BIG)
    top_v, top_i = lax.top_k(score, n_top)
    sel_ok = top_v > -0.5 * BIG
    idx = top_i.reshape(b, NSA_GROUPS, Q_BLOCK * n_top)
    bi = jnp.arange(b)[:, None, None]
    gi = jnp.arange(NSA_GROUPS)[None, :, None]
    ks = k_sel[bi, gi, idx].reshape(b, NSA_GROUPS, Q_BLOCK, n_top, SEL_BLOCK, NSA_DK)
    vs = v_sel[bi, gi, idx].reshape(b, NSA_GROUPS, Q_BLOCK, n_top, SEL_BLOCK, NSA_DV)
    kpos = top_i[..., None] * SEL_BLOCK + jnp.arange(SEL_BLOCK)
    valid_s = (sel_ok[..., None] & (kpos <= t[:, None, None]))[:, :, None]
    s_s = jnp.einsum('bgrqd,bgqnkd->bgrqnk', q, ks).astype(jnp.float32) * scale
    p_s = jnp.where(valid_s, jax.nn.softmax(jnp.where(valid_s, s_s, NEG), axis=(-2, -1)), 0.0)
    o_s = jnp.einsum('bgrqnk,bgqnkd->bgrqd', p_s, vs.astype(jnp.float32))

    start = blk * Q_BLOCK
    kw = lax.dynamic_slice_in_dim(k_win, start, WIN + Q_BLOCK, axis=2)
    vw = lax.dynamic_slice_in_dim(v_win, start, WIN + Q_BLOCK, axis=2)
    kwpos = start - WIN + jnp.arange(WIN + Q_BLOCK)
    valid_w = ((kwpos[None, :] <= t[:, None]) & (kwpos[None, :] > t[:, None] - WIN)
               & (kwpos[None, :] >= 0))
    s_w = jnp.einsum('bgrqd,bgkd->bgrqk', q, kw).astype(jnp.float32) * scale
    p_w = jax.nn.softmax(jnp.where(valid_w, s_w, NEG), axis=-1)
    o_w = jnp.einsum('bgrqk,bgkd->bgrqd', p_w, vw.astype(jnp.float32))

    return gates[..., 0:1] * o_c + gates[..., 1:2] * o_s + gates[..., 2:3] * o_w

def nsa_layer(h, g_norm, w_in, w_out, k_cmp, v_cmp, k_sel, v_sel, k_win, v_win):
    b, t, _ = h.shape
    proj = rmsnorm(h, g_norm) @ w_in
    q_w = NSA_HEADS * NSA_DK
    q, gate, bgate = jnp.split(proj, [q_w, q_w + NSA_W], axis=-1)
    nqb = t // Q_BLOCK
    qb = q.reshape(b, nqb, Q_BLOCK, NSA_GROUPS, NSA_HPG, NSA_DK).transpose(1, 0, 3, 4, 2, 5)
    gb = jax.nn.sigmoid(bgate.astype(jnp.float32)).reshape(
        b, nqb, Q_BLOCK, NSA_GROUPS, NSA_HPG, 3).transpose(1, 0, 3, 4, 2, 5)

    def body(args):
        q_blk, g_blk, blk = args
        return nsa_query_block(q_blk, g_blk, blk, k_cmp, v_cmp, k_sel, v_sel, k_win, v_win)

    o = lax.map(body, (qb, gb, jnp.arange(nqb)))
    o = o.transpose(1, 0, 4, 2, 3, 5).reshape(b, t, NSA_W)
    y = (jax.nn.silu(gate.astype(jnp.float32)) * o).astype(h.dtype) @ w_out
    return h + y

def first_inputs(seed: int = 0) -> dict:
    key = jax.random.key(seed)
    ks = jax.random.split(key, 24)

    def nrm(k, shape, scale):
        return jax.random.normal(k, shape, jnp.float32) * scale

    def gain(k, shape):
        return 1.0 + 0.02 * jax.random.normal(k, shape, jnp.float32)

    ret_in_w = 2 * RET_QK_W + 2 * RET_V_W
    nsa_in_w = NSA_HEADS * NSA_DK + NSA_W + 3 * NSA_HEADS
    return {
        "x": nrm(ks[0], (BATCH, SEQ, D_MODEL), 1.0),
        "p": nrm(ks[1], (DEPTH, BATCH, SEQ, PLE_DIM), 1.0),
        "ret_norm": gain(ks[2], (N_A, D_MODEL)),
        "ret_w_in": nrm(ks[3], (N_A, D_MODEL, ret_in_w), D_MODEL ** -0.5),
        "ret_gn": gain(ks[4], (N_A, RET_V_W)),
        "ret_w_out": nrm(ks[5], (N_A, RET_V_W, D_MODEL), RET_V_W ** -0.5),
        "kv_norm": gain(ks[6], (D_MODEL,)),
        "kv_w": nrm(ks[7], (D_MODEL, 6 * NSA_KV_W), D_MODEL ** -0.5),
        "cmp_pe_k": nrm(ks[8], (CMP_LEN, NSA_DK), 0.02),
        "cmp_w1_k": nrm(ks[9], (CMP_LEN * NSA_DK, CMP_HIDDEN), (CMP_LEN * NSA_DK) ** -0.5),
        "cmp_w2_k": nrm(ks[10], (CMP_HIDDEN, NSA_DK), CMP_HIDDEN ** -0.5),
        "cmp_pe_v": nrm(ks[11], (CMP_LEN, NSA_DV), 0.02),
        "cmp_w1_v": nrm(ks[12], (CMP_LEN * NSA_DV, CMP_HIDDEN), (CMP_LEN * NSA_DV) ** -0.5),
        "cmp_w2_v": nrm(ks[13], (CMP_HIDDEN, NSA_DV), CMP_HIDDEN ** -0.5),
        "nsa_norm": gain(ks[14], (N_B, D_MODEL)),
        "nsa_w_in": nrm(ks[15], (N_B, D_MODEL, nsa_in_w), D_MODEL ** -0.5),
        "nsa_w_out": nrm(ks[16], (N_B, NSA_W, D_MODEL), NSA_W ** -0.5),
        "ple_norm": gain(ks[17], (DEPTH, D_MODEL)),
        "ple_w_gate": nrm(ks[18], (DEPTH, D_MODEL, D_MODEL), D_MODEL ** -0.5),
        "ple_w_emb": nrm(ks[19], (DEPTH, PLE_DIM, D_MODEL), PLE_DIM ** -0.5),
        "final_norm": gain(ks[20], (D_MODEL,)),
    }

def first_block(x, p, ret_norm, ret_w_in, ret_gn, ret_w_out, kv_norm, kv_w,
              cmp_pe_k, cmp_w1_k, cmp_w2_k, cmp_pe_v, cmp_w1_v, cmp_w2_v,
              nsa_norm, nsa_w_in, nsa_w_out, ple_norm, ple_w_gate, ple_w_emb, final_norm):
    h = x
    shared = None
    for i in range(DEPTH):
        if i < N_A:
            h = retention_layer(h, ret_norm[i], ret_w_in[i], ret_gn[i], ret_w_out[i])
        else:
            if i == N_A:
                shared = nsa_shared_kv(h, kv_norm, kv_w, cmp_pe_k, cmp_w1_k, cmp_w2_k,
                                       cmp_pe_v, cmp_w1_v, cmp_w2_v)
            j = i - N_A
            h = nsa_layer(h, nsa_norm[j], nsa_w_in[j], nsa_w_out[j], *shared)
        h = per_layer_embedding(h, p[i], ple_norm[i], ple_w_gate[i], ple_w_emb[i])
    return rmsnorm(h, final_norm)


DEPTH_2 = 1

N_META = 16
GDN_HEADS = D_MODEL // 256
GDN_DK = 128
GDN_DV = 128
FOX_HEADS = D_MODEL // 128
FOX_DH = 64
D_MIX = GDN_HEADS * GDN_DV + FOX_HEADS * FOX_DH
CONV_K = 4
CHUNK = 64
BLOCK_Q = 128
D_FF = -(-8 * D_MODEL // (3 * 256)) * 256
MASK_VALUE = -1e30
GDN_QKV = 2 * GDN_HEADS * GDN_DK + GDN_HEADS * GDN_DV
IN_SIZES = (GDN_HEADS * GDN_DK, GDN_HEADS * GDN_DK, GDN_HEADS * GDN_DV, GDN_HEADS * GDN_DV,
            GDN_HEADS, GDN_HEADS,
            FOX_HEADS * FOX_DH, FOX_HEADS * FOX_DH, FOX_HEADS * FOX_DH, FOX_HEADS)
D_IN = sum(IN_SIZES)
IN_SPLITS = tuple(int(s) for s in np.cumsum(IN_SIZES)[:-1])


def rmsnorm_2(x, w):
    x32 = x.astype(jnp.float32)
    y = x32 * lax.rsqrt(jnp.mean(x32 * x32, axis=-1, keepdims=True) + EPS)
    return (y * w.astype(jnp.float32)).astype(x.dtype)

def l2norm(x):
    return x * lax.rsqrt(jnp.sum(x * x, axis=-1, keepdims=True) + EPS)

def causal_dwconv(x, w):
    k = w.shape[0]
    return lax.conv_general_dilated(x, w[:, None, :], window_strides=(1,), padding=[(k - 1, 0)],
                                    dimension_numbers=("NWC", "WIO", "NWC"),
                                    feature_group_count=x.shape[-1])

def chunk_gated_delta_rule(q, k, v, beta, g, s0, chunk):
    b, h, t, _ = q.shape
    dv = v.shape[-1]
    n = t // chunk
    q, k, v = (a.reshape(b, h, n, chunk, a.shape[-1]) for a in (q, k, v))
    beta = beta.reshape(b, h, n, chunk)
    gc = jnp.cumsum(g.reshape(b, h, n, chunk), axis=-1)
    incl = jnp.tril(jnp.ones((chunk, chunk), dtype=bool))
    strict = jnp.tril(jnp.ones((chunk, chunk), dtype=bool), -1)
    diff = gc[..., :, None] - gc[..., None, :]
    decay = jnp.where(incl, jnp.exp(jnp.where(incl, diff, 0.0)), 0.0)
    a_mat = jnp.where(strict, jnp.einsum("bhncd,bhnsd->bhncs", k, k) * decay * beta[..., :, None], 0.0)
    rhs = jnp.concatenate([v * beta[..., None], k * (beta * jnp.exp(gc))[..., None]], axis=-1)
    sol = lax.linalg.triangular_solve(a_mat + jnp.eye(chunk, dtype=a_mat.dtype), rhs,
                                      left_side=True, lower=True, unit_diagonal=True)
    u, w = sol[..., :dv], sol[..., dv:]
    qk = jnp.einsum("bhncd,bhnsd->bhncs", q, k) * decay
    xs = tuple(jnp.moveaxis(a, 2, 0) for a in (q, k, u, w, gc, qk))

    def step(state, inp):
        q_c, k_c, u_c, w_c, g_c, qk_c = inp
        v_new = u_c - jnp.einsum("bhcd,bhde->bhce", w_c, state)
        o_c = (jnp.einsum("bhcd,bhde->bhce", q_c * jnp.exp(g_c)[..., None], state)
               + jnp.einsum("bhcs,bhse->bhce", qk_c, v_new))
        g_last = g_c[..., -1:]
        state = (state * jnp.exp(g_last)[..., None]
                 + jnp.einsum("bhcd,bhce->bhde", k_c * jnp.exp(g_last - g_c)[..., None], v_new))
        return state, o_c

    s_final, o = lax.scan(step, s0, xs)
    o = jnp.moveaxis(o, 0, 2).reshape(b, h, t, dv)
    return o, s_final

def gated_deltanet_group(qkv, z, b_raw, a_raw, conv_w, a_log, dt_bias, norm_w):
    bsz, t, _ = qkv.shape
    f32 = jnp.float32
    qkv = jax.nn.silu(causal_dwconv(qkv, conv_w)).astype(f32)
    q, k, v = jnp.split(qkv, [GDN_HEADS * GDN_DK, 2 * GDN_HEADS * GDN_DK], axis=-1)
    q = l2norm(q.reshape(bsz, t, GDN_HEADS, GDN_DK)).transpose(0, 2, 1, 3) * (GDN_DK ** -0.5)
    k = l2norm(k.reshape(bsz, t, GDN_HEADS, GDN_DK)).transpose(0, 2, 1, 3)
    v = v.reshape(bsz, t, GDN_HEADS, GDN_DV).transpose(0, 2, 1, 3)
    beta = jax.nn.sigmoid(b_raw.astype(f32)).transpose(0, 2, 1)
    g = (-jnp.exp(a_log.astype(f32))
         * jax.nn.softplus(a_raw.astype(f32) + dt_bias.astype(f32))).transpose(0, 2, 1)
    s0 = jnp.zeros((bsz, GDN_HEADS, GDN_DK, GDN_DV), f32)
    o_meta, s_meta = chunk_gated_delta_rule(q[:, :, :N_META], k[:, :, :N_META], v[:, :, :N_META],
                                            beta[:, :, :N_META], g[:, :, :N_META], s0, N_META)
    o_real, _ = chunk_gated_delta_rule(q[:, :, N_META:], k[:, :, N_META:], v[:, :, N_META:],
                                       beta[:, :, N_META:], g[:, :, N_META:], s_meta, CHUNK)
    o = jnp.concatenate([o_meta, o_real], axis=2).transpose(0, 2, 1, 3)
    zg = jax.nn.silu(z.astype(f32).reshape(bsz, t, GDN_HEADS, GDN_DV))
    o = o * lax.rsqrt(jnp.mean(o * o, axis=-1, keepdims=True) + EPS) * norm_w.astype(f32) * zg
    return o.reshape(bsz, t, GDN_HEADS * GDN_DV).astype(qkv.dtype)

def forgetting_attention_group(q, k, v, f_raw, f_bias):
    bsz, t, _ = q.shape
    f32 = jnp.float32
    q, k, v = (a.astype(f32).reshape(bsz, t, FOX_HEADS, FOX_DH) for a in (q, k, v))
    logf = jax.nn.log_sigmoid(f_raw.astype(f32) + f_bias.astype(f32))
    c = jnp.cumsum(logf, axis=1).transpose(0, 2, 1)
    scale = FOX_DH ** -0.5
    n_blocks = (t - N_META) // BLOCK_Q
    bounds = [0, N_META] + [N_META + (i + 1) * BLOCK_Q for i in range(n_blocks)]
    outs = []
    for s, e in zip(bounds[:-1], bounds[1:]):
        sc = (jnp.einsum("bqhd,bkhd->bhqk", q[:, s:e], k[:, :e]) * scale
              + c[:, :, s:e, None] - c[:, :, None, :e])
        causal = jnp.arange(s, e)[:, None] >= jnp.arange(e)[None, :]
        p = jax.nn.softmax(jnp.where(causal, sc, MASK_VALUE), axis=-1)
        outs.append(jnp.einsum("bhqk,bkhd->bqhd", p, v[:, :e]))
    return jnp.concatenate(outs, axis=1).reshape(bsz, t, FOX_HEADS * FOX_DH)

def swiglu(x, w_gate, w_up, w_down):
    return (jax.nn.silu(x @ w_gate) * (x @ w_up)) @ w_down

def second_inputs(seed: int = 0) -> dict:
    key = jax.random.key(seed)
    ks = jax.random.split(key, 15)
    nrm = jax.random.normal
    dt = jnp.exp(jax.random.uniform(ks[6], (DEPTH_2, GDN_HEADS), minval=math.log(1e-3), maxval=math.log(1e-1)))
    return {
        "x": nrm(ks[0], (BATCH, SEQ, D_MODEL), jnp.float32),
        "meta_tokens": nrm(ks[1], (N_META, D_MODEL), jnp.float32),
        "attn_norm_w": 1.0 + 0.02 * nrm(ks[2], (DEPTH_2, D_MODEL), jnp.float32),
        "w_in": nrm(ks[3], (DEPTH_2, D_MODEL, D_IN), jnp.float32) * D_MODEL ** -0.5,
        "conv_w": nrm(ks[4], (DEPTH_2, CONV_K, GDN_QKV), jnp.float32) * CONV_K ** -0.5,
        "a_log": jnp.log(jax.random.uniform(ks[5], (DEPTH_2, GDN_HEADS), minval=1.0, maxval=16.0)),
        "dt_bias": dt + jnp.log(-jnp.expm1(-dt)),
        "gdn_norm_w": 1.0 + 0.02 * nrm(ks[7], (DEPTH_2, GDN_DV), jnp.float32),
        "fgate_b": 2.0 + 0.5 * nrm(ks[8], (DEPTH_2, FOX_HEADS), jnp.float32),
        "w_out": nrm(ks[9], (DEPTH_2, D_MIX, D_MODEL), jnp.float32) * D_MIX ** -0.5,
        "ffn_norm_w": 1.0 + 0.02 * nrm(ks[10], (DEPTH_2, D_MODEL), jnp.float32),
        "w_gate": nrm(ks[11], (DEPTH_2, D_MODEL, D_FF), jnp.float32) * D_MODEL ** -0.5,
        "w_up": nrm(ks[12], (DEPTH_2, D_MODEL, D_FF), jnp.float32) * D_MODEL ** -0.5,
        "w_down": nrm(ks[13], (DEPTH_2, D_FF, D_MODEL), jnp.float32) * D_FF ** -0.5,
        "final_norm_w": 1.0 + 0.02 * nrm(ks[14], (D_MODEL,), jnp.float32),
    }

def second_block(x, meta_tokens, attn_norm_w, w_in, conv_w, a_log, dt_bias, gdn_norm_w, fgate_b,
              w_out, ffn_norm_w, w_gate, w_up, w_down, final_norm_w):
    bsz = x.shape[0]
    meta = jnp.broadcast_to(meta_tokens[None].astype(x.dtype), (bsz, N_META, D_MODEL))
    h = jnp.concatenate([meta, x], axis=1)
    for l in range(DEPTH_2):
        u = rmsnorm_2(h, attn_norm_w[l])
        proj = u @ w_in[l]
        gq, gk, gv, gz, gb, ga, fq, fk, fv, ff = jnp.split(proj, IN_SPLITS, axis=-1)
        o_gdn = gated_deltanet_group(jnp.concatenate([gq, gk, gv], axis=-1), gz, gb, ga,
                                     conv_w[l], a_log[l], dt_bias[l], gdn_norm_w[l])
        o_fox = forgetting_attention_group(fq, fk, fv, ff, fgate_b[l]).astype(h.dtype)
        h = h + jnp.concatenate([o_gdn, o_fox], axis=-1) @ w_out[l]
        h = h + swiglu(rmsnorm_2(h, ffn_norm_w[l]), w_gate[l], w_up[l], w_down[l])
    h = rmsnorm_2(h, final_norm_w)
    return h[:, N_META:]


def setup_inputs(seed=0):
    out = dict(first_inputs(seed))
    for name, value in second_inputs(seed + 1).items():
        if name != "x":
            out[name + "_2"] = value
    return out


def reference(
    x, p, ret_norm, ret_w_in, ret_gn, ret_w_out, kv_norm, kv_w, cmp_pe_k, cmp_w1_k, cmp_w2_k,
    cmp_pe_v, cmp_w1_v, cmp_w2_v, nsa_norm, nsa_w_in, nsa_w_out, ple_norm, ple_w_gate,
    ple_w_emb, final_norm, meta_tokens_2, attn_norm_w_2, w_in_2, conv_w_2, a_log_2, dt_bias_2,
    gdn_norm_w_2, fgate_b_2, w_out_2, ffn_norm_w_2, w_gate_2, w_up_2, w_down_2, final_norm_w_2,
):
    x = first_block(
        x, p, ret_norm, ret_w_in, ret_gn, ret_w_out, kv_norm, kv_w, cmp_pe_k, cmp_w1_k,
        cmp_w2_k, cmp_pe_v, cmp_w1_v, cmp_w2_v, nsa_norm, nsa_w_in, nsa_w_out, ple_norm,
        ple_w_gate, ple_w_emb, final_norm,
    )
    return second_block(
        x, meta_tokens_2, attn_norm_w_2, w_in_2, conv_w_2, a_log_2, dt_bias_2, gdn_norm_w_2,
        fgate_b_2, w_out_2, ffn_norm_w_2, w_gate_2, w_up_2, w_down_2, final_norm_w_2,
    )


_drawn_inputs = setup_inputs


def setup_inputs(seed=0):
    import zlib

    import numpy as np

    out = dict(_drawn_inputs(seed))
    spreads = {}
    factors = {'ret_gn': 5.041,
     'kv_norm': 8.0,
     'cmp_pe_k': 8.0,
     'cmp_pe_v': 24.01,
     'nsa_norm': 8.0,
     'ple_norm': 8.0,
     'attn_norm_w_2': 3.575,
     'gdn_norm_w_2': 20.46,
     'ffn_norm_w_2': 12.301,
     'final_norm_w_2': 23.008,
     'fgate_b_2': 2.686}
    for name, (base, spread) in spreads.items():
        noise = np.random.default_rng([zlib.crc32(name.encode()), seed]).standard_normal(out[name].shape)
        drawn = base * np.exp(spread * noise) if base else spread * noise
        out[name] = __import__('jax').numpy.asarray(drawn.astype(out[name].dtype))
    for name, factor in factors.items():
        out[name] = (out[name] * factor).astype(out[name].dtype)
    return out
```

```python
from contextlib import ExitStack

import numpy as np

import concourse.bass as bass
from concourse import mybir

F32 = mybir.dt.float32
ALU = mybir.AluOpType
ACT = mybir.ActivationFunctionType
AX = mybir.AxisListType.X

P = 128
D = 1024
KD = D // P
T = 256
TT = T // P
M = 16
TM = T + M
EPS = 1e-6
NEG = -1e30

RH = 4
NSA_H, NSA_G, NSA_HPG = 16, 4, 4
CMP_L, CMP_STRIDE = 32, 16
CMP_N = (T - CMP_L) // CMP_STRIDE + 1
CMP_ROWS = NSA_G * CMP_N
GH = 4
FH, FD = 8, 64
FF = 2816
CHUNKS = [(0, M), (M, P), (M + P, P)]
LEVELS = [1, 2, 4, 8, 16, 32, 64]

UNIT = 2048
RING = 6



def weight_units():
    units = []

    def a(name, c0, n):
        units.extend((name, "A", 0, c0 + 256 * i) for i in range(n // 256))

    def b(name, c0, n, kt=KD):
        for c in range(n // 512):
            units.extend((name, "B", k0, c0 + 512 * c) for k0 in range(0, kt, 4))

    a("ret_w_in", 0, 2048)
    b("ret_w_in", 2048, 4096)
    b("ret_w_out", 0, D, 16)
    units.append(("ple_w_emb0", "E", 0, 0))
    b("ple_w_gate0", 0, D)
    a("kv_w", 0, 1024)
    a("kv_w", 1024, 512)
    a("kv_w", 2048, 512)
    b("kv_w", 1536, 512)
    b("kv_w", 2560, 512)
    units.extend(("cmp_w1_k", "C", k0, 0) for k0 in range(0, CMP_L, 8))
    units.extend(("cmp_w1_v", "C", k0, 0) for k0 in range(0, CMP_L, 8))
    a("nsa_w_in", 0, 2048)
    b("nsa_w_in", 2048, 2048)
    b("nsa_w_out", 0, D, 16)
    units.append(("ple_w_emb1", "E", 0, 0))
    b("ple_w_gate1", 0, D)
    a("w_in_2", 512, 512)
    a("w_in_2", 0, 512)
    a("w_in_2", 1024, 512)
    a("w_in_2", 2056, 1024)
    b("w_in_2", 3080, 512)
    b("w_in_2", 1536, 512)
    b("w_out_2", 0, D)
    for c in range(0, FF, 256):
        units.append(("w_gate_2", "A", 0, c))
        units.append(("w_up_2", "A", 0, c))
    for c in range(2):
        units.extend(("w_down_2", "B", k0, 512 * c) for k0 in range(0, 20, 4))
    units.append(("w_down_2", "E", 20, 0))
    return units


UNITS = weight_units()
NU = len(UNITS)

PARAM = {}
_at = 0
for _name, _n in [("ret_norm", 8), ("kv_norm", 8), ("nsa_norm", 8), ("ple_norm0", 8), ("ple_norm1", 8),
                  ("attn_norm_w_2", 8), ("ffn_norm_w_2", 8), ("ret_gn", 16), ("gdn_norm_w_2", 1),
                  ("cmp_pe_k", CMP_L), ("cmp_pe_v", CMP_L), ("conv_w_2", 48), ("a_log_2", 1),
                  ("dt_bias_2", 1), ("fgate_b_2", 1)]:
    PARAM[_name] = _at
    _at += _n
NPARAM = _at
SIDE_BG, SIDE_G2, SIDE_W2K, SIDE_W2V = 0, KD * 48, KD * 64, KD * 64 + 256
NSIDE = KD * 64 + 512
TB_ID, TB_CAUSAL, TB_CMP, TB_ROW, TB_STRICT, TB_INCL, TB_LEVEL = 0, 128, 256, 286, 288, 416, 544
TB_ONE = TB_LEVEL + 128 * len(LEVELS)
NTAB = TB_ONE + 15
RT_COS, RT_SIN, RT_DECAY = 0, 256, 512
NRT = 512 + RH * 256


def tables():
    i = np.arange(P)
    t = np.zeros((P, NTAB), np.float32)
    t[:, TB_ID:TB_ID + P] = np.eye(P)
    t[:, TB_CAUSAL:TB_CAUSAL + P] = np.where(i[None] <= i[:, None], 0.0, NEG)
    end = np.arange(CMP_N) * CMP_STRIDE + CMP_L - 1
    for b in range(TT):
        t[:, TB_CMP + b * CMP_N:TB_CMP + (b + 1) * CMP_N] = np.where(end[None] <= (b * P + i)[:, None], 0.0, NEG)
        t[:, TB_ROW + b] = (b * P + i >= CMP_L - 1)
    t[:, TB_STRICT:TB_STRICT + P] = np.where(i[None] < i[:, None], 0.0, -NEG)
    t[:, TB_INCL:TB_INCL + P] = np.where(i[None] >= i[:, None], 0.0, NEG)
    for n, m in enumerate(LEVELS):
        same = (i[:, None] // (2 * m)) == (i[None] // (2 * m))
        t[:, TB_LEVEL + n * P:TB_LEVEL + (n + 1) * P] = same & (i[:, None] // m % 2 == 1) & (i[None] // m % 2 == 0)
    t[:, TB_ONE + 7] = 1.0
    r = np.zeros((P, NRT), np.float32)
    inv = (np.float32(10000.0) ** (-np.arange(P, dtype=np.float32) / np.float32(P))).astype(np.float32)
    ang = (np.arange(T, dtype=np.float32)[None] * inv[:, None]).astype(np.float32)
    r[:, RT_COS:RT_COS + T] = np.cos(ang)
    r[:, RT_SIN:RT_SIN + T] = np.sin(ang)
    lg = np.log1p(-(2.0 ** (-5.0 - np.arange(RH))))
    diff = (np.arange(T)[None] - i[:, None]).astype(np.float64)
    for h in range(RH):
        r[:, RT_DECAY + h * T:RT_DECAY + (h + 1) * T] = np.where(
            diff >= 0, np.exp(np.maximum(diff, 0) * lg[h]), 0.0) * 256.0 ** -0.5
    return t, r


class Banks:

    def __init__(self, tensor, first, uses, full, freed):
        self.tensor, self.first, self.uses, self.full_sem, self.freed = tensor, first, uses, full, freed
        self.index = {key: n for n, (key, _) in enumerate(uses)}
        assert len(self.index) == len(uses)
        self.rank, counts = [], {}
        for _, engine in uses:
            counts[engine] = counts.get(engine, 0) + 1
            self.rank.append(counts[engine])
        self.filled, self.released = 0, {}

    def at(self, key):
        return self.tensor[:, self.first + self.index[key] % 4, :]

    def open(self, pe, key):
        n = self.index[key] - 4
        if n >= 0:
            pe.wait_ge(self.freed[self.uses[n][1]], self.rank[n])
        return self.at(key)

    def full(self, ins, key):
        assert self.index[key] == self.filled, (key, self.uses[self.filled])
        self.filled += 1
        ins.then_inc(self.full_sem, 1)

    def wait(self, engine, key):
        engine.wait_ge(self.full_sem, self.index[key] + 1)
        return self.at(key)

    def free(self, ins, key):
        n = self.index[key]
        engine = self.uses[n][1]
        self.released[engine] = self.released.get(engine, 0) + 1
        assert self.released[engine] == self.rank[n], (key, engine)
        ins.then_inc(self.freed[engine], 1)


STEPS = [(0, 4 * g, 4) for g in range(4)] + [(1, 2 * n, 2) for n in range(8)]
NORMS = ["ret", "ple0", "kv", "ple1", "final", "attn", "ffn", "last"]


def main_uses():
    u = [(("rqk", n), "dve") for n in range(8)]
    u += [(("rv", c, t), "act") for c in range(4) for t in range(TT)]
    u += [(("rg", c, t), "dve") for c in range(4) for t in range(TT)]
    u += [(("ro", c, t), "dve") for c in range(2) for t in range(TT)]

    def ple(n):
        return [(("emb", n, c, t), "act") for c in range(2) for t in range(TT)] + \
               [(("pg", n, c, t), "act") for c in range(2) for t in range(TT)]

    u += ple(0)
    u += [(("kvA", n), "act") for n in range(8)]
    u += [(("kvB", n, t), "act") for n in range(2) for t in range(TT)]
    u += [(("cmp", n), "dve") for n in range(2)]
    u += [(("nq", n), "act") for n in range(8)]
    u += [(("bg", t), "act") for t in range(TT)]
    u += [(("ng", c, t), "dve") for c in range(4) for t in range(TT)]
    u += [(("no", c, t), "dve") for c in range(2) for t in range(TT)]
    u += ple(1)
    u += [("gb", "act"), ("ga", "dve"), ("ff", "dve")]
    u += [(("gin", j), "act") for j in range(12)]
    u += [(("fin", j), "act") for j in range(8)]
    u += [(("fv", c), "act") for c in range(3)]
    u += [(("gz", t), "dve") for t in range(TT)]
    u += [(("mo", c, t), "dve") for c in range(2) for t in range(TT)]
    for n in range(11):
        u += [(("fg", n), "dve"), (("fu", n), "dve")]
    u += [(("dn", c, t), "dve") for c in range(2) for t in range(TT)]
    return u


def tr_uses(name, n):
    return [((name, f), "dve" if f % 2 == 0 else "act") for f in range(n)]


def nsa_order():
    order = [("S", 0), ("S", 1)]
    for i in range(len(STEPS)):
        order += [("G", i)] * (i < 4) + [("O", i)]
        if i + 2 < len(STEPS):
            order.append(("S", i + 2))
    return order


def aux_uses():
    u = [("meta", "dve")] + tr_uses("xT_ret", 4)
    u += [(("rs", h), "dve") for h in range(RH)]
    for h in range(RH):
        u += [(("rpv", h, t), "act") for t in range(TT)]
    u += tr_uses("yT", 8)
    u += tr_uses("xT_ple0", 4)
    u += tr_uses("xT_kv", 4)
    u += [(("hT", n), "dve") for n in range(2)] + [(("c2", n), "dve") for n in range(2)]
    u += [(("cs", b), "dve") for b in range(TT)]
    for kind, i in nsa_order():
        if kind == "S":
            u += [(("s", i), "act"), (("w", i), "act")]
        if kind == "O":
            u += [(("sT", i), "dve"), (("wT", i), "act"), (("cT", i), "dve"), (("o", i), "dve")]
    u += tr_uses("oT", 8)
    u += tr_uses("xT_ple1", 4)
    u += tr_uses("xT_attn", 4)
    u += [("ss", "act")] + [(("rb", j), "dve") for j in range(8)]
    u += [("tok", "dve")]
    for c in range(3):
        u += [(("bc", c), "act" if c else "dve"), (("kk", c), "dve")]
        if c:
            u += [(("qk", c), "dve")]
        u += [(("kt", c), "dve"), (("vt", c), "dve")]
    u += gdn_fox_uses()
    u += tr_uses("mT", 4)
    u += tr_uses("xT_ffn", 4)
    return u


def level_chunks(n):
    return [c for c in (1, 2, 0) if 2 * LEVELS[n] <= CHUNKS[c][1]]


def last_level(n, c):
    return 2 * LEVELS[n] == CHUNKS[c][1]


def gdn_fox_order():
    order = [("Fs", 0)]
    for n in range(len(LEVELS)):
        order += [("Lz", n, c) for c in level_chunks(n)] + [("Ft", n)]
        order += [("Lx", n, c) for c in level_chunks(n)] + [("Fo", n), ("Fs", n + 1)]
    order += [("W", 1), ("W", 2), ("V", 0), ("Ft", 7), ("V", 1), ("Fo", 7), ("V", 2)]
    return order


def gdn_fox_uses():
    u = []
    for kind, *at in gdn_fox_order():
        n = at[0]
        if kind == "Lz":
            u += [(("z", *at), "act")]
        elif kind == "Lx":
            u += ([] if last_level(*at) else [(("x", *at), "dve")]) + [(("y", *at), "dve")]
        elif kind == "Fs":
            u += [(("fs", n), "act")]
        elif kind == "Ft":
            u += [(("fT", n), "act"), (("fm", n), "dve")]
        elif kind == "Fo":
            u += [(("fo", n), "act")]
        elif kind == "W":
            u += [(("gw", n), "act")]
        else:
            u += [(("vn", n), "act")] + [(("go", n), "dve")] * (n > 0) + [(("st", n), "dve")] * (n < 2)
    return u


R1, R2, R3, R4 = 0, 4096, 8192, 12288
GIN_TILES = [4, 5, 6, 7, 0, 1, 2, 3, 8, 9, 10, 11]
RAW_W = TM + 3
C_OFF = [0, 4 * M, 4 * M + 4 * P]
C_ALL = 4 * M + 8 * P
CMP_K, CMP_V = 4 * CMP_ROWS, 5 * CMP_ROWS
LEVEL_LIST = [(n, c) for n in range(len(LEVELS)) for c in level_chunks(n)]


def two_models_kernel(nc, x, meta, weights, side, params, tabs, ret_tabs, p_t, gains, out):
    ctx = ExitStack()
    with ctx:
        def sb(name, cols):
            return ctx.enter_context(nc.sbuf_tensor(name, [P, cols], F32))

        sems = {}

        def sem(name):
            if name not in sems:
                sems[name] = ctx.enter_context(nc.semaphore(name))
            return sems[name]

        ring = sb("ring", RING * UNIT)
        side_sb = sb("side_sb", NSIDE)
        tab = sb("tab", NTAB)
        par = sb("par", NPARAM)
        h = sb("h", TT * D)
        xn = sb("xn", TT * D)
        xT = sb("xT", KD * TM)
        xT2 = sb("xT2", KD * TM)
        R = sb("R", 4 * 4096)
        PTb = sb("PTb", 4096)
        gfin2 = sb("gfin2", D)
        G1 = sb("G1", 2 * D)
        tmp = sb("tmp", 1024)
        nw = sb("nw", 1088)
        Pf = sb("Pf", 1088)
        PfT = sb("PfT", 1536)
        small = sb("small", 560)
        psum = ctx.enter_context(nc.psum_tensor("psum", [P, 8, 512], F32))

        freed = {e: sem(f"main_read_by_{e}") for e in ("act", "dve")}
        main = Banks(psum, 0, main_uses(), sem("main_filled"), freed)
        freed = {e: sem(f"aux_read_by_{e}") for e in ("act", "dve")}
        aux = Banks(psum, 4, aux_uses(), sem("aux_filled"), freed)

        at = [0]

        def cols(n):
            at[0] += n
            assert at[0] <= 560
            return small[:, at[0] - n:at[0]]

        sumsq, std, rstd = cols(16), cols(16), cols(16)
        msum = cols(3)
        eps = cols(1)
        bn, mv, rsd, rrs, nmr = cols(24), cols(16), cols(8), cols(8), cols(8)
        half_gn = cols(17)
        bgt = cols(96)
        nmx, esum, esc = cols(96), cols(96), cols(96)
        tk, g3, e3, be = nmx[:, 0:24], nmx[:, 24:60], esum[:, 0:36], esum[:, 36:48]
        hb, fnm, fsum, frs = esum[:, 48:60], esc[:, 0:16], esc[:, 16:32], esc[:, 32:48]
        gss, gsd, grs = esc[:, 48:56], esc[:, 56:64], esc[:, 64:72]
        cst = cols(32)

        ident = tab[:, TB_ID:TB_ID + P]
        causal = tab[:, TB_CAUSAL:TB_CAUSAL + P]

        def param(name, n=0, rows=P):
            return par[0:rows, PARAM[name] + n:PARAM[name] + n + 1]

        def hrow(t, c=0, n=D):
            return h[:, t * D + c:t * D + c + n]

        def xnrow(t):
            return xn[:, t * D:(t + 1) * D]

        def spread(ap, inner):
            return ap.unsqueeze(2).to_broadcast([ap.shape[0], ap.shape[1], inner])

        def over(ap, outer):
            return ap.unsqueeze(1).to_broadcast([ap.shape[0], outer, ap.shape[1]])

        def kt_cols(buf, kt, c0, n, width=TM, base=0):
            return buf[:, base + kt * width + c0:base + kt * width + c0 + n]

        def into_xT(kt):
            return kt_cols(xT, kt, M, T)

        def into_R1(kt):
            return R[:, R1 + kt * T:R1 + (kt + 1) * T]

        class Marks:

            def __init__(self, engine, name):
                self.engine, self.sem, self.n = engine, sem(name), 0

            def then_wait(self, ins):
                self.n += 1
                ins.then_inc(self.sem, 1)
                self.engine.wait_ge(self.sem, self.n)

        def wait_read(engine, banks, key):
            n = banks.index[key]
            engine.wait_ge(banks.freed[banks.uses[n][1]], banks.rank[n])

        def evacuate(engine, is_act, name, f, dst, gain, imm=None):
            key = (name, f)
            bank = aux.wait(engine, key)
            for k in range(2):
                kt = 2 * f + k
                src = bank[:, k * T:(k + 1) * T]
                g = gain(kt) if gain else imm
                if is_act:
                    ins = engine.activation(dst(kt), src, ACT.Copy, scale=g)
                else:
                    ins = engine.tensor_scalar(dst(kt), src, g, None, ALU.mult)
            aux.free(ins, key)

        def gain_of(name):
            return lambda kt: param(name, kt)

        def mix_gain(kt):
            return half_gn[:, 16:17] if kt < 4 else 1.0

        def two_gains(engine, is_act, f):
            key = ("xT_kv", f)
            bank = aux.wait(engine, key)
            for k in range(2):
                kt = 2 * f + k
                src = bank[:, k * T:(k + 1) * T]
                for dst, name in ((xT, "kv_norm"), (xT2, "nsa_norm")):
                    if is_act:
                        ins = engine.activation(kt_cols(dst, kt, M, T), src, ACT.Copy, scale=param(name, kt))
                    else:
                        ins = engine.tensor_scalar(kt_cols(dst, kt, M, T), src, param(name, kt), None, ALU.mult)
            aux.free(ins, key)

        RV, RK, KDEC = (R, R1), (R, R1 + 1536), (G1, 0)
        SM = {}
        for n, (name, rows) in enumerate([("ga", 4), ("la", 4), ("gc", 4), ("beta", 4), ("ff", 8), ("lf", 8), ("ones", 8)]):
            SM[name] = R[0:rows, R4 + 1024 + n * TM:R4 + 1024 + (n + 1) * TM]
        SM["negc"] = R[0:8, R3 + 8 * TM + 1536:R3 + 9 * TM + 1536]
        SM["r8"] = xn[0:8, 0:TM]

        block = ctx.enter_context(nc.Block())

        @block.sync
        def _(sp):
            def load(name, dst, src):
                sp.dma_start(dst, src).then_inc(sem(name), 16)

            for t in range(TT):
                load(f"x_in{t}", hrow(t), x[t * P:(t + 1) * P, :])
            load("par_in", par[:, :], params)
            load("tab_in", tab[:, :], tabs)
            load("meta_in", R[0:M, R3:R3 + D], meta)

            def unit(u):
                if u >= RING:
                    sp.wait_ge(sem("units_used"), u - RING + 1)
                sp.dma_start(ring[:, u % RING * UNIT:(u % RING + 1) * UNIT], weights[u]).then_inc(
                    sem(f"unit_in{u % RING}"), 16)

            for u in range(2):
                unit(u)
            load("ret_in", R[:, R4:R4 + NRT], ret_tabs)
            for u in range(2, RING):
                unit(u)
            load("pT_in", G1[:, D:2 * D], p_t)
            load("side_in", side_sb[:, :], side)
            load("gain1_in", G1[:, 0:D], gains[0:1, :].to_broadcast([P, D]))
            load("gain2_in", gfin2[:, :], gains[1:2, :].to_broadcast([P, D]))
            for u in range(RING, NU):
                unit(u)
            for t in range(TT):
                sp.wait_ge(sem("out_rows"), t + 1)
                sp.dma_start(out[t * P:(t + 1) * P, :], xnrow(t)).then_inc(sem("stored"), 16)
            sp.wait_ge(sem("stored"), 16 * TT)

        @block.tensor
        def _(pe):
            begun = [0]

            def mm(out, lhsT, rhs, first, last):
                return pe.matmul(out, lhsT, rhs, start=first, stop=last, skip_group_check=True)

            def next_unit():
                u = begun[0]
                begun[0] += 1
                pe.wait_ge(sem(f"unit_in{u % RING}"), 16 * (u // RING + 1))
                first = [u > 0]

                def product(*args):
                    ins = mm(*args)
                    if first[0]:
                        ins.then_inc(sem("units_used"), 1)
                    first[0] = False
                    return ins

                return ring[:, u % RING * UNIT:(u % RING + 1) * UNIT], product

            def project_a(keys, src, c0, n):
                w, product = next_unit()
                w = w.rearrange("p (k c) -> p k c", k=KD)
                for f in range(2):
                    key = keys[f * (len(keys) - 1)]
                    base = f * n if len(keys) == 1 else 0
                    if f == 0 or len(keys) == 2:
                        bank = main.open(pe, key)
                    for k in range(KD):
                        ins = product(bank[:, base:base + n], w[:, k, f * P:(f + 1) * P], src(k, c0, n),
                                      k == 0, k == KD - 1)
                    if f == 1 or len(keys) == 2:
                        main.full(ins, key)

            def project_b(keys, src, rows, kt, ready=None):
                banks = [main.open(pe, key) for key in keys]
                for k0 in range(0, kt, 4):
                    if ready:
                        ready(k0)
                    w, product = next_unit()
                    w = w.rearrange("p (k c) -> p k c", k=4)
                    for n, bank in enumerate(banks):
                        c0, m = rows[n]
                        for k in range(4):
                            ins = product(bank[0:m, :], src(k0 + k, c0, m), w[:, k, :], k0 + k == 0, k0 + k == kt - 1)
                        if k0 + 4 == kt:
                            main.full(ins, keys[n])

            def turn(name, f, src):
                bank = aux.open(pe, (name, f))
                for k in range(2):
                    for t in range(TT):
                        ins = pe.transpose(bank[:, k * T + t * P:k * T + (t + 1) * P], src(2 * f + k, t), ident)
                aux.full(ins, (name, f))

            def from_xn(kt, t):
                return xn[:, t * D + kt * P:t * D + (kt + 1) * P]

            def turn_norm(name, n):
                pe.wait_ge(sem("xn_ready"), 2 * (n + 1))
                for f in range(4):
                    turn(name, f, from_xn)

            def wait_turned(name, fs):
                for f in fs:
                    wait_read(pe, aux, (name, f))

            def x_src(k, c0, n):
                return kt_cols(xT, k, c0, n)

            def x2_src(k, c0, n):
                return kt_cols(xT2, k, c0, n)

            def r1_src(k, c0, n):
                return kt_cols(R, k, c0, n, T, R1)

            rows = [(M, P), (M + P, P)]
            rows0 = [(0, P), (P, P)]

            pe.wait_ge(sem("tab_in"), 16)
            pe.wait_ge(sem("meta_rows"), 1)
            bank = aux.open(pe, "meta")
            for kt in range(KD):
                ins = pe.transpose(bank[:, kt * M:(kt + 1) * M], R[0:M, R3 + kt * P:R3 + (kt + 1) * P], ident[0:M, 0:M])
            aux.full(ins, "meta")
            turn_norm("xT_ret", 0)
            wait_turned("xT_ret", range(4))
            for n in range(8):
                project_a([("rqk", n)], x_src, M, T)
            project_b([("rv", 0, t) for t in range(TT)], x_src, rows, KD)

            def qk_tile(which, hd, half, c0, n):
                return kt_cols(R, which * 8 + hd * 2 + half, c0, n, T, R1)

            pe.wait_ge(sem("rotated"), 8)
            for hd in range(RH):
                bank = aux.open(pe, ("rs", hd))
                for half in range(2):
                    mm(bank[:, 0:T], qk_tile(1, hd, half, 0, P), qk_tile(0, hd, half, 0, T), half == 0, half == 1)
                for half in range(2):
                    ins = mm(bank[:, T:T + P], qk_tile(1, hd, half, P, P), qk_tile(0, hd, half, P, P),
                             half == 0, half == 1)
                aux.full(ins, ("rs", hd))
            for c in range(1, 4):
                project_b([("rv", c, t) for t in range(TT)], x_src, rows, KD)

            def retention_values(hd):
                wait_read(pe, aux, ("rs", hd))
                for t in range(TT):
                    wait_read(pe, main, ("rv", hd, t))
                st = PTb[:, hd * 384:(hd + 1) * 384]
                v0 = R[:, R2 + hd * 512:R2 + (hd + 1) * 512]
                v1 = R[:, R2 + 2048 + hd * 512:R2 + 2048 + (hd + 1) * 512]
                bank = aux.open(pe, ("rpv", hd, 0))
                aux.full(mm(bank, st[:, 0:P], v0, True, True), ("rpv", hd, 0))
                bank = aux.open(pe, ("rpv", hd, 1))
                mm(bank, st[:, P:T], v0, True, False)
                aux.full(mm(bank, st[:, T:T + P], v1, False, True), ("rpv", hd, 1))

            for half in range(2):
                for c in (2 * half, 2 * half + 1):
                    project_b([("rg", c, t) for t in range(TT)], x_src, rows, KD)
                for hd in (2 * half, 2 * half + 1):
                    retention_values(hd)

            def y_src(base):
                return lambda kt, t: R[:, base + t * 2048 + kt * P:base + t * 2048 + (kt + 1) * P]

            def turn_before(name, src, need):
                def ready(k0):
                    if k0 % 8 == 0:
                        need(k0 // 8)
                        for f in range(k0 // 2, k0 // 2 + 4):
                            turn(name, f, src)
                        wait_turned(name, range(k0 // 2, k0 // 2 + 4))
                return ready

            project_b([("ro", 0, t) for t in range(TT)], r1_src, rows0, 16,
                      turn_before("yT", y_src(R3), lambda half: pe.wait_ge(sem("ret_y"), 4 * (half + 1))))
            project_b([("ro", 1, t) for t in range(TT)], r1_src, rows0, 16)

            def ple(n, norm):
                pe.wait_ge(sem("pT_in"), 16)
                w, product = next_unit()
                w = w.rearrange("p (k c) -> p k c", k=2)
                for c in range(2):
                    for t in range(TT):
                        bank = main.open(pe, ("emb", n, c, t))
                        for k in range(2):
                            c0 = D + (n * 2 + k) * T + t * P
                            ins = product(bank, G1[:, c0:c0 + P], w[:, k, c * 512:(c + 1) * 512], k == 0, k == 1)
                        main.full(ins, ("emb", n, c, t))
                turn_norm(f"xT_ple{n}", norm)
                wait_turned(f"xT_ple{n}", range(4))
                for c in range(2):
                    project_b([("pg", n, c, t) for t in range(TT)], x_src, rows, KD)

            ple(0, 1)

            turn_norm("xT_kv", 2)
            wait_turned("xT_kv", range(4))
            for n in range(8):
                project_a([("kvA", n)], x_src, M, T)
            for n in range(2):
                project_b([("kvB", n, t) for t in range(TT)], x_src, rows, KD)
            for n in range(2):
                pe.wait_ge(sem("blocks_ready"), n + 1)
                bank = main.open(pe, ("cmp", n))
                for k0 in range(0, CMP_L, 8):
                    w, product = next_unit()
                    w = w.rearrange("p (k c) -> p k c", k=8)
                    for k in range(8):
                        c0 = R3 + n * CMP_L * CMP_ROWS + (k0 + k) * CMP_ROWS
                        ins = product(bank[0:CMP_ROWS, 0:256], R[:, c0:c0 + CMP_ROWS], w[:, k, :],
                                      k0 + k == 0, k0 + k == CMP_L - 1)
                main.full(ins, ("cmp", n))
            for n in range(4):
                project_a([("nq", n)], x2_src, M, T)
            pe.wait_ge(sem("side_in"), 16)
            for n in range(2):
                wait_read(pe, main, ("cmp", n))
                bank = aux.open(pe, ("hT", n))
                for k in range(2):
                    c0 = n * 512 + 256 + k * P
                    ins = pe.transpose(bank[:, k * CMP_ROWS:(k + 1) * CMP_ROWS], tmp[0:CMP_ROWS, c0:c0 + P],
                                       ident[0:CMP_ROWS, 0:CMP_ROWS])
                aux.full(ins, ("hT", n))
            wait_read(pe, aux, ("hT", 0))
            bank = aux.open(pe, ("c2", 0))
            for k in range(2):
                ins = mm(bank[:, 0:CMP_ROWS], side_sb[:, SIDE_W2K + k * P:SIDE_W2K + (k + 1) * P],
                         Pf[:, k * CMP_ROWS:(k + 1) * CMP_ROWS], k == 0, k == 1)
            aux.full(ins, ("c2", 0))
            wait_read(pe, aux, ("hT", 1))
            bank = aux.open(pe, ("c2", 1))
            for g in range(NSA_G):
                for k in range(2):
                    c0 = 2 * CMP_ROWS + k * CMP_ROWS + g * CMP_N
                    ins = mm(bank[0:CMP_N, g * P:(g + 1) * P], Pf[:, c0:c0 + CMP_N],
                             side_sb[:, SIDE_W2V + k * P:SIDE_W2V + (k + 1) * P], k == 0, k == 1)
            aux.full(ins, ("c2", 1))
            for n in range(4, 8):
                project_a([("nq", n)], x2_src, M, T)
            for t in range(TT):
                bank = main.open(pe, ("bg", t))
                for k in range(KD):
                    ins = mm(bank[:, 0:48], x2_src(k, *rows[t]), side_sb[:, SIDE_BG + k * 48:SIDE_BG + (k + 1) * 48],
                             k == 0, k == KD - 1)
                main.full(ins, ("bg", t))

            def q_tile(hd, b):
                return kt_cols(R, hd, b * P, P, T, R3)

            wait_read(pe, aux, ("c2", 1))
            wait_read(pe, main, ("nq", 7))
            for b in range(TT):
                bank = aux.open(pe, ("cs", b))
                for hd in range(NSA_H):
                    c0 = CMP_K + hd // NSA_HPG * CMP_N
                    ins = mm(bank[:, hd * CMP_N:(hd + 1) * CMP_N], q_tile(hd, b), Pf[:, c0:c0 + CMP_N], True, True)
                aux.full(ins, ("cs", b))
            wait_read(pe, main, ("kvB", 1, 1))

            def nsa_scores(i):
                b, h0, nh = STEPS[i]
                kt = b + 1
                for key, base in ((("s", i), R1 + 2048), (("w", i), R1 + 3072)):
                    bank = aux.open(pe, key)
                    for n in range(nh):
                        k0 = base + (h0 + n) // NSA_HPG * T
                        c0 = n * kt * P
                        mm(bank[:, c0:c0 + kt * P], q_tile(h0 + n, b), R[:, k0:k0 + kt * P], True, False)
                        ins = mm(bank[:, c0 + b * P:c0 + kt * P], ident, causal, False, True)
                    aux.full(ins, key)

            def nsa_values(i):
                b, h0, nh = STEPS[i]
                kt = b + 1
                slot = i % 2
                pe.wait_ge(sem("nsa_p"), i + 1)
                for key, base in ((("sT", i), 0), (("wT", i), 512)):
                    bank = aux.open(pe, key)
                    for n in range(4):
                        c0 = R2 + 2048 + slot * 1024 + base + n * P
                        ins = pe.transpose(bank[:, n * P:(n + 1) * P], R[:, c0:c0 + P], ident)
                    aux.full(ins, key)
                pe.wait_ge(sem("cmp_p"), b + 1)
                bank = aux.open(pe, ("cT", i))
                for n in range(nh):
                    c0 = b * 240 + (h0 + n) * CMP_N
                    ins = pe.transpose(bank[0:CMP_N, n * P:(n + 1) * P], xn[:, c0:c0 + CMP_N], ident)
                aux.full(ins, ("cT", i))
                bank = aux.open(pe, ("o", i))
                for key in ("sT", "wT", "cT"):
                    wait_read(pe, aux, (key, i))
                for n in range(nh):
                    g = (h0 + n) // NSA_HPG
                    o = bank[:, n * P:(n + 1) * P]
                    mm(o, nw[0:CMP_N, slot * 512 + n * P:slot * 512 + (n + 1) * P],
                       Pf[0:CMP_N, CMP_V + g * P:CMP_V + (g + 1) * P], True, False)
                    for br in range(2):
                        for k in range(kt):
                            c0 = slot * 1024 + br * 512 + (n * kt + k) * P
                            v0 = R2 + br * 1024 + k * 512 + g * P
                            ins = mm(o, PTb[:, c0:c0 + P], R[:, v0:v0 + P], False, br == 1 and k == kt - 1)
                aux.full(ins, ("o", i))

            for kind, i in nsa_order():
                if kind == "S":
                    nsa_scores(i)
                elif kind == "G":
                    project_b([("ng", i, t) for t in range(TT)], x2_src, rows, KD)
                else:
                    nsa_values(i)
            project_b([("no", 0, t) for t in range(TT)], r1_src, rows0, 16,
                      turn_before("oT", y_src(R4), lambda half: wait_read(pe, aux, ("o", len(STEPS) - 1))))
            project_b([("no", 1, t) for t in range(TT)], r1_src, rows0, 16)
            ple(1, 3)

            turn_norm("xT_attn", 4)
            wait_turned("xT_attn", range(4))
            wait_read(pe, aux, "meta")
            for key, c0, n in (("gb", 0, 4), ("ga", 4, 4), ("ff", 8, 8)):
                bank = main.open(pe, key)
                for k in range(KD):
                    w0 = SIDE_G2 + k * 16 + c0
                    ins = mm(bank[0:n, 0:TM], side_sb[:, w0:w0 + n], x_src(k, 0, TM), k == 0, k == KD - 1)
                main.full(ins, key)
            for u in range(6):
                project_a([("gin", 2 * u), ("gin", 2 * u + 1)], x_src, 0, TM)
            for u in range(4):
                project_a([("fin", 2 * u), ("fin", 2 * u + 1)], x_src, 0, TM)

            def ch(j, c0, n):
                return kt_cols(R, j, c0, n, TM, R2)

            pe.wait_ge(sem("squares"), 1)
            bank = aux.open(pe, "ss")
            for j in range(8):
                ins = mm(bank[0:8, 0:TM], tab[:, TB_ONE + 7 - j:TB_ONE + 15 - j], xT2[:, j * TM:(j + 1) * TM],
                         j == 0, j == 7)
            aux.full(ins, "ss")
            project_b([("fv", c) for c in range(3)], x_src, [(0, M)] + rows, KD)
            pe.wait_ge(sem("qk_factor"), 1)
            for j in range(8):
                bank = aux.open(pe, ("rb", j))
                aux.full(mm(bank[:, 0:TM], ident[0:8, j:j + 1].to_broadcast([8, P]), SM["r8"], True, True), ("rb", j))
            pe.wait_ge(sem("scans"), 4)
            bank = aux.open(pe, "tok")
            for c, (t0, n) in enumerate(CHUNKS):
                for i, src in enumerate(("gc", "beta")):
                    ins = pe.transpose(bank[0:n, c * 8 + i * 4:c * 8 + i * 4 + 4], SM[src][:, t0:t0 + n],
                                       ident[0:4, 0:4])
            aux.full(ins, "tok")
            project_b([("gz", t) for t in range(TT)], x_src, rows, KD)

            wait_read(pe, aux, ("rb", 7))
            pe.wait_ge(sem("conv_silu"), 12)
            for c, (t0, n) in enumerate(CHUNKS):
                bank = aux.open(pe, ("bc", c))
                for hd in range(GH):
                    ins = mm(bank[:, hd * n:(hd + 1) * n], ident[0:4, hd:hd + 1].to_broadcast([4, P]),
                             SM["gc"][:, t0:t0 + n], True, True)
                aux.full(ins, ("bc", c))
                bank = aux.open(pe, ("kk", c))
                for hd in range(GH):
                    ins = mm(bank[0:n, hd * n:(hd + 1) * n], ch(4 + hd, t0, n), ch(4 + hd, t0, n), True, True)
                aux.full(ins, ("kk", c))
                if c:
                    bank = aux.open(pe, ("qk", c))
                    for hd in range(GH):
                        ins = mm(bank[0:n, hd * n:(hd + 1) * n], ch(4 + hd, t0, n), ch(hd, t0, n), True, True)
                    aux.full(ins, ("qk", c))
                for key, j0 in (("kt", 4), ("vt", 8)):
                    bank = aux.open(pe, (key, c))
                    for hd in range(GH):
                        ins = pe.transpose(bank[0:n, hd * P:(hd + 1) * P], ch(j0 + hd, t0, n), ident)
                    aux.full(ins, (key, c))

            def mat(buf, base, c, hd):
                n = CHUNKS[c][1]
                return buf[0:n, base + C_OFF[c] + hd * n:base + C_OFF[c] + (hd + 1) * n]

            def chunk_rows(base, c, hd):
                buf, b0 = base
                return buf[0:CHUNKS[c][1], b0 + c * 512 + hd * P:b0 + c * 512 + (hd + 1) * P]

            def fox_scores(hd):
                bank = aux.open(pe, ("fs", hd))
                p0, c0 = hd % 2 * FD, hd // 2 * TM
                at_ = 0
                for b in range(TT):
                    n = M + (b + 1) * P
                    o = bank[:, at_:at_ + n]
                    q0 = R3 + c0 + M + b * P
                    mm(o, R[p0:p0 + FD, q0:q0 + P], R[p0:p0 + FD, R3 + 4 * TM + c0:R3 + 4 * TM + c0 + n], True, False)
                    mm(o, ident[0:8, hd:hd + 1].to_broadcast([8, P]), SM["negc"][:, 0:n], False, False)
                    ins = mm(bank[:, at_ + n - P:at_ + n], ident, causal, False, True)
                    at_ += n
                aux.full(ins, ("fs", hd))

            def fox_turn(hd):
                p = Pf[:, hd % 2 * 416:hd % 2 * 416 + 416]
                wait_read(pe, aux, ("fs", hd))
                bank = aux.open(pe, ("fT", hd))
                for n, c0 in enumerate((M, P + 2 * M, 2 * P + 2 * M)):
                    ins = pe.transpose(bank[:, n * P:(n + 1) * P], p[:, c0:c0 + P], ident)
                aux.full(ins, ("fT", hd))
                bank = aux.open(pe, ("fm", hd))
                for n, c0 in enumerate((0, P + M)):
                    ins = pe.transpose(bank[0:M, n * P:(n + 1) * P], p[:, c0:c0 + M], ident)
                aux.full(ins, ("fm", hd))

            def fox_values(hd):
                wait_read(pe, aux, ("fT", hd))
                wait_read(pe, aux, ("fm", hd))
                slot = hd % 2 * 640
                bank = aux.open(pe, ("fo", hd))

                def v(c, m):
                    v0 = R3 + 8 * TM + c * 512 + hd * FD
                    return R[0:m, v0:v0 + FD]

                for b in range(TT):
                    o = bank[:, b * FD:(b + 1) * FD]
                    mm(o, PfT[0:M, slot + 384 + b * P:slot + 384 + (b + 1) * P], v(0, M), True, False)
                    for k in range(b + 1):
                        ins = mm(o, PfT[:, slot + (b + k) * P:slot + (b + k + 1) * P], v(1 + k, P), False, k == b)
                aux.full(ins, ("fo", hd))

            state, v_new = R1 + 3072, R1 + 3584
            pe.wait_ge(sem("fox_c"), 1)
            wait_read(pe, main, ("fv", 2))
            pe.wait_ge(sem("xy_init"), 6)
            for kind, *key in gdn_fox_order():
                if kind == "Fs":
                    fox_scores(key[0])
                elif kind == "Ft":
                    fox_turn(key[0])
                elif kind == "Fo":
                    fox_values(key[0])
                elif kind == "Lz":
                    lv, c = key
                    pe.wait_ge(sem("level_part"), LEVEL_LIST.index((lv, c)) + 1)
                    if lv:
                        wait_read(pe, aux, ("y", lv - 1, c))
                    n = CHUNKS[c][1]
                    bank = aux.open(pe, ("z", lv, c))
                    for hd in range(GH):
                        ins = mm(bank[0:n, hd * n:(hd + 1) * n], mat(xT2, 0, c, hd), mat(PTb, C_ALL, c, hd), True, True)
                    aux.full(ins, ("z", lv, c))
                elif kind == "Lx":
                    lv, c = key
                    wait_read(pe, aux, ("z", lv, c))
                    n = CHUNKS[c][1]
                    if not last_level(lv, c):
                        bank = aux.open(pe, ("x", lv, c))
                        for hd in range(GH):
                            ins = mm(bank[0:n, hd * n:(hd + 1) * n], mat(xT2, C_ALL, c, hd), mat(PTb, 0, c, hd),
                                     True, True)
                        aux.full(ins, ("x", lv, c))
                    bank = aux.open(pe, ("y", lv, c))
                    for hd in range(GH):
                        ins = mm(bank[0:n, hd * n:(hd + 1) * n], mat(PTb, 0, c, hd), mat(xT2, C_ALL, c, hd), True, True)
                    aux.full(ins, ("y", lv, c))
                elif kind == "W":
                    c = key[0]
                    wait_read(pe, aux, ("y", len(LEVELS) - 1, c))
                    bank = aux.open(pe, ("gw", c))
                    for hd in range(GH):
                        ins = mm(bank[:, hd * P:(hd + 1) * P], chunk_rows(RK, c, hd), mat(PTb, C_ALL, c, hd), True, True)
                    aux.full(ins, ("gw", c))
                else:
                    c = key[0]
                    t0, n = CHUNKS[c]
                    if c:
                        wait_read(pe, aux, ("st", c - 1))
                        wait_read(pe, aux, ("gw", c))
                    else:
                        wait_read(pe, aux, ("y", 3, 0))
                    bank = aux.open(pe, ("vn", c))
                    for hd in range(GH):
                        o = bank[0:n, hd * P:(hd + 1) * P]
                        ins = mm(o, mat(PTb, C_ALL, c, hd), chunk_rows(RV, c, hd), True, c == 0)
                        if c:
                            w0 = (c - 1) * 512 + hd * P
                            ins = mm(o, nw[:, w0:w0 + P], R[:, state + hd * P:state + (hd + 1) * P], False, True)
                    aux.full(ins, ("vn", c))
                    wait_read(pe, aux, ("vn", c))
                    if c:
                        bank = aux.open(pe, ("go", c))
                        for hd in range(GH):
                            o = bank[:, hd * P:(hd + 1) * P]
                            mm(o, ch(hd, t0, n), R[:, state + hd * P:state + (hd + 1) * P], True, False)
                            k0 = R4 + 3072 + (c - 1) * 512 + hd * P
                            ins = mm(o, R[:, k0:k0 + P], R[:, v_new + hd * P:v_new + (hd + 1) * P], False, True)
                        aux.full(ins, ("go", c))
                    if c < 2:
                        bank = aux.open(pe, ("st", c))
                        for hd in range(GH):
                            ins = mm(bank[:, hd * P:(hd + 1) * P], chunk_rows(KDEC, c, hd),
                                     R[0:n, v_new + hd * P:v_new + (hd + 1) * P], True, True)
                        aux.full(ins, ("st", c))

            pe.wait_ge(sem("mix_ready"), 2)
            wait_read(pe, aux, ("fo", FH - 1))
            for f in range(4):
                turn("mT", f, lambda kt, t: R[:, R4 + 1024 + t * D + kt * P:R4 + 1024 + t * D + (kt + 1) * P])
            wait_turned("mT", range(4))
            for c in range(2):
                project_b([("mo", c, t) for t in range(TT)], x_src, rows, KD)
            turn_norm("xT_ffn", 5)
            wait_turned("xT_ffn", range(4))
            for n in range(11):
                project_a([("fg", n)], x_src, M, T)
                project_a([("fu", n)], x_src, M, T)

            def hidden(k, t):
                return R[:, k * T + t * P:k * T + (t + 1) * P]

            wait_read(pe, main, ("fu", 10))
            banks = {(c, t): main.open(pe, ("dn", c, t)) for c in range(2) for t in range(TT)}
            for c in range(2):
                for k0 in range(0, 20, 4):
                    w, product = next_unit()
                    w = w.rearrange("p (k c) -> p k c", k=4)
                    for t in range(TT):
                        for k in range(4):
                            product(banks[c, t], hidden(k0 + k, t), w[:, k, :], k0 + k == 0, False)
            w, product = next_unit()
            w = w.rearrange("p (k c) -> p k c", k=2)
            for c in range(2):
                for t in range(TT):
                    for k in range(2):
                        ins = product(banks[c, t], hidden(20 + k, t), w[:, k, c * 512:(c + 1) * 512], False, k == 1)
                    main.full(ins, ("dn", c, t))
            assert begun[0] == NU

        @block.scalar
        def _(act):
            own = Marks(act, "act_step")

            def read_by(key):
                wait_read(act, main, key)

            def norm_stats(n, wait_rows):
                for t in range(TT):
                    wait_rows(t)
                    ins = act.activation(xnrow(t), hrow(t), ACT.Square, accum_out=sumsq[:, 2 * n + t:2 * n + t + 1])
                own.then_wait(ins)
                act.activation(std[:, 2 * n:2 * n + 2], sumsq[:, 2 * n:2 * n + 2], ACT.Sqrt, scale=1.0 / D,
                               bias=eps).then_inc(sem("std_ready"), 1)

            def odd(name, n, dst, gain, imm=None):
                for f in range(1, n, 2):
                    evacuate(act, True, name, f, dst, gain, imm)

            gates = [0]

            def gate_tanh(key, before):
                i = gates[0]
                gates[0] += 1
                bank = main.wait(act, key)
                if before:
                    wait_read(act, main, before)
                act.activation(tmp[:, i % 2 * 512:i % 2 * 512 + 512], bank, ACT.Tanh, scale=0.5).then_inc(
                    sem("gate_tanh"), 1)

            act.wait_ge(sem("eps_ready"), 1)
            act.wait_ge(sem("meta_in"), 16)
            own.then_wait(act.activation(tmp[0:M, 0:D], R[0:M, R3:R3 + D], ACT.Square, accum_out=msum[0:M, 0:1]))
            act.activation(msum[0:M, 1:2], msum[0:M, 0:1], ACT.Sqrt, scale=1.0 / D, bias=eps[0:M, :]).then_inc(
                sem("meta_std"), 1)
            norm_stats(0, lambda t: act.wait_ge(sem(f"x_in{t}"), 16))
            act.wait_ge(sem("par_in"), 16)
            odd("xT_ret", 4, into_xT, gain_of("ret_norm"))
            for c in range(4):
                for t in range(TT):
                    key = ("rv", c, t)
                    bank = main.wait(act, key)
                    main.free(act.copy(R[:, R2 + t * 2048 + c * 512:R2 + t * 2048 + (c + 1) * 512], bank), key)
            act.wait_ge(sem("rotated"), 8)
            seq = [("rg", c, t) for c in range(4) for t in range(TT)]
            for half in range(2):
                for i in range(4 * half, 4 * half + 4):
                    gate_tanh(seq[i], seq[i - 2] if i >= 2 else None)
                act.wait_ge(sem("ret_var"), 4 * (half + 1))
                act.activation(rsd[:, 4 * half:4 * half + 4],
                               mv.rearrange("p (i c) -> p i c", c=2)[:, 4 * half:4 * half + 4, 1], ACT.Sqrt,
                               bias=eps).then_inc(sem("ret_std"), 1)
                act.wait_ge(sem("ret_norm"), half + 1)
                for i in range(4 * half, 4 * half + 4):
                    key = ("rpv", i // 2, i % 2)
                    bank = aux.wait(act, key)
                    if i >= 4:
                        act.wait_ge(sem("ret_y"), i - 3)
                    aux.free(act.activation(xn[:, i % 4 * 512:(i % 4 + 1) * 512], bank, ACT.Identity,
                                            scale=rrs[:, i:i + 1], bias=nmr[:, i:i + 1]), key)
            act.wait_ge(sem("half_gn"), 1)
            odd("yT", 8, into_R1, lambda kt: half_gn[:, kt:kt + 1])

            def ple(n, norm, wait_rows):
                norm_stats(norm, wait_rows)
                for c in range(2):
                    for t in range(TT):
                        key = ("emb", n, c, t)
                        bank = main.wait(act, key)
                        c0 = R2 + t * D + c * 512
                        main.free(act.activation(R[:, c0:c0 + 512], bank, ACT.Copy, scale=0.5), key)
                odd(f"xT_ple{n}", 4, into_xT, gain_of(f"ple_norm{n}"))
                for i in range(4):
                    key = ("pg", n, i // 2, i % 2)
                    bank = main.wait(act, key)
                    if i >= 2:
                        act.wait_ge(sem("h_ready"), 4 * n + i - 1)
                    main.free(act.activation(tmp[:, i % 2 * 512:i % 2 * 512 + 512], bank, ACT.Tanh, scale=0.5), key)

            ple(0, 1, lambda t: read_by(("ro", 1, t)))

            norm_stats(2, lambda t: act.wait_ge(sem("h_ready"), 3 + t))
            for f in (1, 3):
                two_gains(act, True, f)
            for n in range(8):
                key = ("kvA", n)
                bank = main.wait(act, key)
                main.free(act.copy(R[:, R1 + n * 512:R1 + (n + 1) * 512], bank), key)
            for n in range(2):
                for t in range(TT):
                    key = ("kvB", n, t)
                    bank = main.wait(act, key)
                    c0 = R2 + n * D + t * 512
                    main.free(act.copy(R[:, c0:c0 + 512], bank), key)
            for n in range(2):
                bank = main.wait(act, ("cmp", n))[0:CMP_ROWS, 0:256]
                g = tmp[0:CMP_ROWS, n * 512:n * 512 + 256]
                act.activation(g, bank, ACT.Square).then_inc(sem("gelu_square"), 1)
                act.wait_ge(sem("gelu_in"), n + 1)
                act.activation(g, g, ACT.Tanh, scale=float(np.sqrt(2.0 / np.pi))).then_inc(sem("gelu_tanh"), 1)
            for n in range(8):
                key = ("nq", n)
                bank = main.wait(act, key)
                main.free(act.activation(R[:, R3 + n * 512:R3 + (n + 1) * 512], bank, ACT.Copy, scale=float(P) ** -0.5), key)
            for t in range(TT):
                key = ("bg", t)
                bank = main.wait(act, key)
                main.free(act.activation(bgt[:, t * 48:(t + 1) * 48], bank[:, 0:48], ACT.Tanh, scale=0.5), key)
            for b in range(TT):
                act.wait_ge(sem("cmp_shifted"), b + 1)
                cx = xn[:, b * 240:(b + 1) * 240]
                act.activation(cx, cx, ACT.Exp).then_inc(sem("cmp_exp"), 1)
            seq = [("ng", c, t) for c in range(4) for t in range(TT)]
            for kind, i in nsa_order():
                if kind == "S":
                    b, h0, nh = STEPS[i]
                    n_keys = (b + 1) * P
                    for br, name in enumerate(("s", "w")):
                        bank = aux.at((name, i))
                        act.wait_ge(sem("nsa_max"), 2 * i + br + 1)
                        for n in range(nh):
                            c0 = R2 + 2048 + i % 2 * 1024 + br * 512 + n * n_keys
                            col = i * 8 + br * nh + n
                            ins = act.activation(R[:, c0:c0 + n_keys], bank[:, n * n_keys:(n + 1) * n_keys], ACT.Exp,
                                                 bias=nmx[:, col:col + 1], accum_out=esum[:, col:col + 1])
                        aux.free(ins, (name, i))
                elif kind == "G":
                    for t in range(TT):
                        k = 2 * i + t
                        gate_tanh(seq[k], seq[k - 2] if k >= 2 else None)
                else:
                    bank = aux.wait(act, ("wT", i))
                    c0 = i % 2 * 1024 + 512
                    aux.free(act.copy(PTb[:, c0:c0 + 512], bank), ("wT", i))
            odd("oT", 8, into_R1, None, 0.5)
            ple(1, 3, lambda t: read_by(("no", 1, t)))

            norm_stats(4, lambda t: act.wait_ge(sem("h_ready"), 7 + t))
            norm_stats(5, lambda t: act.wait_ge(sem("x2_ready"), t + 1))
            odd("xT_attn", 4, into_xT, gain_of("attn_norm_w_2"))
            bank = main.wait(act, "gb")
            main.free(act.activation(SM["beta"], bank[0:4, 0:TM], ACT.Tanh, scale=0.5), "gb")
            act.activation(cst[0:4, 0:1], param("a_log_2", 0, 4), ACT.Exp).then_inc(sem("a_exp"), 1)

            def conv_tanh(jj):
                act.wait_ge(sem("conv_done"), jj + 1)
                if jj >= 2:
                    act.wait_ge(sem("conv_silu"), jj - 1)
                c0 = R2 + GIN_TILES[jj] * TM
                act.activation(tmp[:, jj % 2 * 512:jj % 2 * 512 + TM], R[:, c0:c0 + TM], ACT.Tanh, scale=0.5).then_inc(
                    sem("conv_tanh"), 1)

            for jj in range(12):
                bank = main.wait(act, ("gin", jj))
                c0 = R1 + GIN_TILES[jj] * RAW_W + 3
                main.free(act.copy(R[:, c0:c0 + TM], bank[:, 0:TM]), ("gin", jj))
                if jj:
                    conv_tanh(jj - 1)
            conv_tanh(11)

            def fox_in(j):
                bank = main.wait(act, ("fin", j))
                main.free(act.activation(R[:, R3 + j * TM:R3 + (j + 1) * TM], bank[:, 0:TM], ACT.Copy,
                                         scale=float(FD) ** -0.5 if j < 4 else 1.0), ("fin", j))

            for j in range(4):
                fox_in(j)
            act.wait_ge(sem("conv_silu"), 8)
            act.activation(xT2[:, :], R[:, R2:R2 + 8 * TM], ACT.Square).then_inc(sem("squares"), 1)
            for j in range(4, 8):
                fox_in(j)
            read_by("ff")
            act.activation(SM["la"], SM["ga"], ACT.Abs)
            own.then_wait(act.activation(SM["lf"], SM["ff"], ACT.Abs))
            act.activation(SM["la"], SM["la"], ACT.Exp, scale=-1.0)
            own.then_wait(act.activation(SM["lf"], SM["lf"], ACT.Exp, scale=-1.0))
            act.activation(SM["la"], SM["la"], ACT.Ln, bias=1.0)
            act.activation(SM["lf"], SM["lf"], ACT.Ln, bias=1.0).then_inc(sem("soft_logs"), 1)
            bank = aux.wait(act, "ss")
            aux.free(act.activation(SM["r8"], bank[0:8, 0:TM], ACT.Sqrt, scale=0.25, bias=eps[0:8, :]), "ss")
            for c in range(3):
                m = CHUNKS[c][1]
                bank = main.wait(act, ("fv", c))
                c0 = R3 + 8 * TM + c * 512
                main.free(act.copy(R[0:m, c0:c0 + 512], bank[0:m, :]), ("fv", c))
            for t in range(TT):
                if t == 0:
                    act.wait_ge(sem("conv_silu"), 12)
                gate_tanh(("gz", t), None)

            for c, (t0, n) in enumerate(CHUNKS):
                act.wait_ge(sem("log_decays"), c + 1)
                act.activation(e3[0:n, c * 12:(c + 1) * 12], g3[0:n, c * 12:(c + 1) * 12], ACT.Exp).then_inc(
                    sem("decays_small"), 1)
                if c:
                    act.wait_ge(sem("bc_read"), c)
                    if c == 2:
                        act.wait_ge(sem("q_scaled"), 1)
                    aux.free(act.activation(xn[:, 1536:2048], aux.at(("bc", c)), ACT.Exp), ("bc", c))
                act.wait_ge(sem("clamped"), c + 1)
                if c:
                    act.activation(xn[0:n, 1024:1024 + 4 * n], xn[0:n, 1024:1024 + 4 * n], ACT.Exp)
                act.activation(xn[0:n, 512:512 + 4 * n], xn[0:n, 512:512 + 4 * n], ACT.Exp, scale=-1.0).then_inc(
                    sem("decay_ready"), 1)

            for kind, *key in gdn_fox_order():
                if kind == "Lz":
                    lv, c = key
                    n = CHUNKS[c][1]
                    bank = aux.wait(act, ("z", lv, c))
                    c0 = C_ALL + C_OFF[c]
                    aux.free(act.copy(xT2[0:n, c0:c0 + 4 * n], bank[0:n, 0:4 * n]), ("z", lv, c))
                elif kind == "Fs":
                    hd = key[0]
                    bank = aux.at(("fs", hd))
                    act.wait_ge(sem("fox_max"), hd + 1)
                    at_ = 0
                    for b in range(TT):
                        n = M + (b + 1) * P
                        c0 = hd % 2 * 416 + at_
                        ins = act.activation(Pf[:, c0:c0 + n], bank[:, at_:at_ + n], ACT.Exp,
                                             bias=fnm[:, 2 * hd + b:2 * hd + b + 1],
                                             accum_out=fsum[:, 2 * hd + b:2 * hd + b + 1])
                        at_ += n
                    aux.free(ins, ("fs", hd))
                elif kind == "Ft":
                    hd = key[0]
                    bank = aux.wait(act, ("fT", hd))
                    aux.free(act.copy(PfT[:, hd % 2 * 640:hd % 2 * 640 + 384], bank[:, 0:384]), ("fT", hd))
                elif kind == "Fo":
                    hd = key[0]
                    bank = aux.wait(act, ("fo", hd))
                    act.wait_ge(sem("fox_recip"), hd + 1)
                    for b in range(TT):
                        c0 = R4 + 1024 + b * D + 512 + hd * FD
                        ins = act.activation(R[:, c0:c0 + FD], bank[:, b * FD:(b + 1) * FD], ACT.Copy,
                                             scale=frs[:, 2 * hd + b:2 * hd + b + 1])
                    aux.free(ins, ("fo", hd))
                elif kind == "W":
                    c = key[0]
                    bank = aux.wait(act, ("gw", c))
                    aux.free(act.activation(nw[:, (c - 1) * 512:c * 512], bank, ACT.Copy, scale=-1.0), ("gw", c))
                elif kind == "V":
                    c = key[0]
                    n = CHUNKS[c][1]
                    bank = aux.wait(act, ("vn", c))
                    aux.free(act.copy(R[0:n, R1 + 3584:R1 + 4096], bank[0:n, :]), ("vn", c))
                    if c:
                        bank = aux.wait(act, ("go", c))
                        if c == 2:
                            act.wait_ge(sem("mix_ready"), 1)
                        act.activation(tmp[:, 0:512], bank, ACT.Square).then_inc(sem("go_square"), 1)
                        act.wait_ge(sem("go_sum"), c)
                        act.activation(gsd[:, 4 * c - 4:4 * c], gss[:, 4 * c - 4:4 * c], ACT.Sqrt, scale=1.0 / P,
                                       bias=eps).then_inc(sem("go_std"), 1)
            odd("mT", 4, into_xT, mix_gain)
            norm_stats(6, lambda t: read_by(("mo", 1, t)))
            odd("xT_ffn", 4, into_xT, gain_of("ffn_norm_w_2"))
            for n in range(11):
                gate_tanh(("fg", n), ("fg", n - 2) if n >= 2 else None)
            norm_stats(7, lambda t: read_by(("dn", 1, t)))

        @block.vector
        def _(dve):
            own = Marks(dve, "dve_step")

            def even(name, n, dst, gain, imm=None):
                for f in range(0, n, 2):
                    evacuate(dve, False, name, f, dst, gain, imm)

            def roots(n):
                dve.wait_ge(sem("std_ready"), n + 1)
                own.then_wait(dve.reciprocal(rstd[:, 2 * n:2 * n + 2], std[:, 2 * n:2 * n + 2]))

            def norm(n):
                roots(n)
                for t in range(TT):
                    dve.tensor_scalar(xnrow(t), hrow(t), rstd[:, 2 * n + t:2 * n + t + 1], None, ALU.mult).then_inc(
                        sem("xn_ready"), 1)

            def add_to_h(keys):
                for key in keys:
                    _, c, t = key
                    bank = main.wait(dve, key)
                    main.free(dve.tensor_tensor(hrow(t, c * 512, 512), hrow(t, c * 512, 512), bank, ALU.add), key)

            gates = [0]

            def gate(key, dst):
                i = gates[0]
                gates[0] += 1
                dve.wait_ge(sem("gate_tanh"), i + 1)
                bank = main.at(key)
                main.free(dve.scalar_tensor_tensor(dst, tmp[:, i % 2 * 512:i % 2 * 512 + 512], 1.0, bank, ALU.add,
                                                   ALU.mult), key)

            dve.memset(eps, EPS).then_inc(sem("eps_ready"), 1)
            dve.wait_ge(sem("par_in"), 16)
            dve.tensor_scalar(half_gn, par[:, PARAM["ret_gn"]:PARAM["ret_gn"] + 17], 0.5, None, ALU.mult).then_inc(
                sem("half_gn"), 1)
            dve.wait_ge(sem("meta_std"), 1)
            own.then_wait(dve.reciprocal(msum[0:M, 2:3], msum[0:M, 1:2]))
            dve.tensor_scalar(R[0:M, R3:R3 + D], R[0:M, R3:R3 + D], msum[0:M, 2:3], None, ALU.mult).then_inc(
                sem("meta_rows"), 1)
            norm(0)
            bank = aux.wait(dve, "meta")
            for kt in range(KD):
                ins = dve.tensor_scalar(kt_cols(xT, kt, 0, M), bank[:, kt * M:(kt + 1) * M],
                                        param("attn_norm_w_2", kt), None, ALU.mult)
            aux.free(ins, "meta")
            even("xT_ret", 4, into_xT, gain_of("ret_norm"))

            dve.wait_ge(sem("ret_in"), 16)
            cos, sin = R[:, R4 + RT_COS:R4 + RT_COS + T], R[:, R4 + RT_SIN:R4 + RT_SIN + T]
            for n in range(8):
                key = ("rqk", n)
                bank = main.wait(dve, key).rearrange("p (f t) -> p f t", f=2)
                ta, tb = tmp[:, 0:512], tmp[:, 512:1024]
                if n:
                    dve.wait_ge(sem("rotated"), n)
                dve.tensor_tensor(ta.rearrange("p (f t) -> p f t", f=2), bank, over(cos, 2), ALU.mult)
                main.free(dve.tensor_tensor(tb.rearrange("p (f t) -> p f t", f=2), bank, over(sin, 2), ALU.mult), key)
                wait_read(dve, main, key)
                c0 = R1 + n * 512
                dve.tensor_tensor(R[:, c0:c0 + T], ta[:, 0:T], tb[:, T:2 * T], ALU.subtract)
                dve.tensor_tensor(R[:, c0 + T:c0 + 2 * T], tb[:, 0:T], ta[:, T:2 * T], ALU.add).then_inc(
                    sem("rotated"), 1)
            for hd in range(RH):
                key = ("rs", hd)
                bank = aux.wait(dve, key)
                decay = R[:, R4 + RT_DECAY + hd * T:R4 + RT_DECAY + (hd + 1) * T]
                dve.tensor_tensor(PTb[:, hd * 384:hd * 384 + T], bank[:, 0:T], decay, ALU.mult)
                aux.free(dve.tensor_tensor(PTb[:, hd * 384 + T:(hd + 1) * 384], bank[:, T:T + P], decay[:, 0:P],
                                           ALU.mult), key)
            for half in range(2):
                for c in (2 * half, 2 * half + 1):
                    for t in range(TT):
                        gate(("rg", c, t), R[:, R3 + t * 2048 + c * 512:R3 + t * 2048 + (c + 1) * 512])
                for i in range(4 * half, 4 * half + 4):
                    bank = aux.wait(dve, ("rpv", i // 2, i % 2))
                    ins = dve.bn_stats(bn[:, i % 4 * 6:(i % 4 + 1) * 6], bank)
                own.then_wait(ins)
                for i in range(4 * half, 4 * half + 4):
                    dve.bn_aggr(mv[:, 2 * i:2 * i + 2], bn[:, i % 4 * 6:(i % 4 + 1) * 6]).then_inc(sem("ret_var"), 1)
                dve.wait_ge(sem("ret_std"), half + 1)
                four = slice(4 * half, 4 * half + 4)
                own.then_wait(dve.reciprocal(rrs[:, four], rsd[:, four]))
                dve.scalar_tensor_tensor(nmr[:, four], mv.rearrange("p (i c) -> p i c", c=2)[:, four, 0], -1.0,
                                         rrs[:, four], ALU.mult, ALU.mult).then_inc(sem("ret_norm"), 1)
            even("yT", 8, into_R1, lambda kt: half_gn[:, kt:kt + 1])
            add_to_h([("ro", c, t) for c in range(2) for t in range(TT)])

            def ple(n, norm_n):
                norm(norm_n)
                even(f"xT_ple{n}", 4, into_xT, gain_of(f"ple_norm{n}"))
                wait_read(dve, main, ("emb", n, 1, 1))
                for i in range(4):
                    c, t = i // 2, i % 2
                    wait_read(dve, main, ("pg", n, c, t))
                    g = tmp[:, i % 2 * 512:i % 2 * 512 + 512]
                    c0 = R2 + t * D + c * 512
                    own.then_wait(dve.scalar_tensor_tensor(g, g, 1.0, R[:, c0:c0 + 512], ALU.add, ALU.mult))
                    dve.tensor_tensor(hrow(t, c * 512, 512), hrow(t, c * 512, 512), g, ALU.add).then_inc(
                        sem("h_ready"), 1)

            ple(0, 1)

            norm(2)
            for f in (0, 2):
                two_gains(dve, False, f)
            for n, name in enumerate(("cmp_pe_k", "cmp_pe_v")):
                wait_read(dve, main, ("kvA", 2 * n + 1))
                src = R[:, R1 + n * D:R1 + (n + 1) * D].rearrange("p (g m l) -> p l g m", g=NSA_G, l=CMP_STRIDE)
                for o in range(2):
                    c0 = R3 + n * CMP_L * CMP_ROWS + o * CMP_STRIDE * CMP_ROWS
                    dst = R[:, c0:c0 + CMP_STRIDE * CMP_ROWS].rearrange("p (l g m) -> p l g m", g=NSA_G, m=CMP_N)
                    p0 = PARAM[name] + o * CMP_STRIDE
                    pe_cols = par[:, p0:p0 + CMP_STRIDE].unsqueeze(2).unsqueeze(3).to_broadcast(
                        [P, CMP_STRIDE, NSA_G, CMP_N])
                    ins = dve.tensor_tensor(dst, src[:, :, :, o:o + CMP_N], pe_cols, ALU.add)
                ins.then_inc(sem("blocks_ready"), 1)
            for n in range(2):
                dve.wait_ge(sem("gelu_square"), n + 1)
                bank = main.at(("cmp", n))[0:CMP_ROWS, 0:256]
                g = tmp[0:CMP_ROWS, n * 512:n * 512 + 256]
                own.then_wait(dve.tensor_scalar(g, g, 0.044715, 1.0, ALU.mult, ALU.add))
                dve.tensor_tensor(g, g, bank, ALU.mult).then_inc(sem("gelu_in"), 1)
                dve.wait_ge(sem("gelu_tanh"), n + 1)
                main.free(dve.scalar_tensor_tensor(tmp[0:CMP_ROWS, n * 512 + 256:n * 512 + 512], g, 1.0, bank, ALU.add,
                                                   ALU.mult), ("cmp", n))
            for n in range(2):
                bank = aux.wait(dve, ("hT", n))
                aux.free(dve.tensor_copy(Pf[:, n * 120:(n + 1) * 120], bank[:, 0:120]), ("hT", n))
            bank = aux.wait(dve, ("c2", 0))
            aux.free(dve.tensor_scalar(Pf[:, CMP_K:CMP_K + CMP_ROWS], bank[:, 0:CMP_ROWS], 0.5, None, ALU.mult), ("c2", 0))
            bank = aux.wait(dve, ("c2", 1))
            aux.free(dve.tensor_scalar(Pf[0:CMP_N, CMP_V:CMP_V + 512], bank[0:CMP_N, :], 0.5, None, ALU.mult), ("c2", 1))
            wait_read(dve, main, ("bg", 1))
            own.then_wait(dve.tensor_scalar(bgt, bgt, 1.0, 0.5, ALU.add, ALU.mult))

            def heads(ap):
                return ap.rearrange("p (h n) -> p h n", h=NSA_H)

            for b in range(TT):
                cx = xn[:, b * 240:(b + 1) * 240]
                bank = aux.wait(dve, ("cs", b))
                mask = tab[:, TB_CMP + b * CMP_N:TB_CMP + (b + 1) * CMP_N]
                aux.free(dve.tensor_tensor(heads(cx), heads(bank[:, 0:240]), over(mask, NSA_H), ALU.add), ("cs", b))
                wait_read(dve, aux, ("cs", b))
                own.then_wait(dve.tensor_reduce(cst[:, b * 16:(b + 1) * 16], heads(cx), AX, ALU.max))
                dve.tensor_tensor(heads(cx), heads(cx), spread(cst[:, b * 16:(b + 1) * 16], CMP_N),
                                  ALU.subtract).then_inc(sem("cmp_shifted"), 1)
            for b in range(TT):
                cx = xn[:, b * 240:(b + 1) * 240]
                cs = cst[:, b * 16:(b + 1) * 16]
                dve.wait_ge(sem("cmp_exp"), b + 1)
                own.then_wait(dve.tensor_reduce(cs, heads(cx), AX, ALU.add))
                own.then_wait(dve.reciprocal(cs, cs))
                own.then_wait(dve.scalar_tensor_tensor(
                    cs, cs, tab[:, TB_ROW + b:TB_ROW + b + 1],
                    bgt[:, b * 48:(b + 1) * 48].rearrange("p (h c) -> p h c", c=3)[:, :, 0], ALU.mult, ALU.mult))
                dve.tensor_tensor(heads(cx), heads(cx), spread(cs, CMP_N), ALU.mult).then_inc(sem("cmp_p"), 1)

            for kind, i in nsa_order():
                if kind == "S":
                    b, h0, nh = STEPS[i]
                    for br, name in enumerate(("s", "w")):
                        bank = aux.wait(dve, (name, i))
                        c0 = i * 8 + br * nh
                        dve.tensor_reduce(nmx[:, c0:c0 + nh], bank.rearrange("p (h n) -> p h n", h=nh), AX, ALU.max,
                                          negate=True).then_inc(sem("nsa_max"), 1)
                    wait_read(dve, aux, ("w", i))
                    sc = esc[:, i * 8:i * 8 + 2 * nh]
                    own.then_wait(dve.reciprocal(sc, esum[:, i * 8:i * 8 + 2 * nh]))
                    g = bgt[:, b * 48 + h0 * 3:b * 48 + (h0 + nh) * 3].rearrange("p (n c) -> p c n", c=3)[:, 1:3, :]
                    sc = sc.rearrange("p (c n) -> p c n", c=2)
                    dve.tensor_tensor(sc, sc, g, ALU.mult).then_inc(sem("nsa_scale"), 1)
                elif kind == "G":
                    for t in range(TT):
                        gate(("ng", i, t), R[:, R4 + t * 2048 + i * 512:R4 + t * 2048 + (i + 1) * 512])
                else:
                    b, h0, nh = STEPS[i]
                    slot = i % 2
                    bank = aux.wait(dve, ("sT", i))
                    aux.free(dve.tensor_copy(PTb[:, slot * 1024:slot * 1024 + 512], bank), ("sT", i))
                    bank = aux.wait(dve, ("cT", i))
                    aux.free(dve.tensor_copy(nw[0:CMP_N, slot * 512:slot * 512 + nh * P], bank[0:CMP_N, 0:nh * P]),
                             ("cT", i))
                    bank = aux.wait(dve, ("o", i))
                    wait_read(dve, main, ("ng", h0 // NSA_HPG, b))
                    y = R[:, R4 + b * 2048 + h0 * P:R4 + b * 2048 + (h0 + nh) * P]
                    aux.free(dve.tensor_tensor(y, y, bank[:, 0:nh * P], ALU.mult), ("o", i))
            even("oT", 8, into_R1, None, 0.5)
            add_to_h([("no", c, t) for c in range(2) for t in range(TT)])
            ple(1, 3)

            roots(4)
            dve.wait_ge(sem("gain1_in"), 16)
            for t in range(TT):
                dve.scalar_tensor_tensor(hrow(t), hrow(t), rstd[:, 8 + t:9 + t], G1[:, 0:D], ALU.mult,
                                         ALU.mult).then_inc(sem("x2_ready"), 1)
            norm(5)
            even("xT_attn", 4, into_xT, gain_of("attn_norm_w_2"))
            raw = R[:, R1:R1 + 12 * RAW_W].rearrange("p (j t) -> p j t", j=12)
            dve.memset(raw[:, :, 0:3], 0.0)
            own.then_wait(dve.memset(SM["ones"], 1.0))
            for key, rows_, name, bias in (("ga", 4, "ga", "dt_bias_2"), ("ff", 8, "ff", "fgate_b_2")):
                bank = main.wait(dve, key)
                main.free(dve.tensor_scalar(SM[name], bank[0:rows_, 0:TM], param(bias, 0, rows_), None, ALU.add), key)
            wait_read(dve, main, "gb")
            dve.tensor_scalar(SM["beta"], SM["beta"], 1.0, 0.5, ALU.add, ALU.mult).then_inc(sem("scans"), 1)

            def conv(jj):
                j = GIN_TILES[jj]
                wait_read(dve, main, ("gin", jj))
                y = R[:, R2 + j * TM:R2 + (j + 1) * TM]
                own.then_wait(dve.tensor_scalar(y, raw[:, j, 0:TM], param("conv_w_2", j), None, ALU.mult))
                for k in range(1, 4):
                    ins = dve.scalar_tensor_tensor(y, raw[:, j, k:k + TM], param("conv_w_2", 12 * k + j), y, ALU.mult,
                                                   ALU.add)
                    if k < 3:
                        own.then_wait(ins)
                ins.then_inc(sem("conv_done"), 1)

            def silu(jj):
                j = GIN_TILES[jj]
                y = R[:, R2 + j * TM:R2 + (j + 1) * TM]
                dve.wait_ge(sem("conv_tanh"), jj + 1)
                dve.scalar_tensor_tensor(y, tmp[:, jj % 2 * 512:jj % 2 * 512 + TM], 1.0, y, ALU.add,
                                         ALU.mult).then_inc(sem("conv_silu"), 1)

            for jj in range(12):
                conv(jj)
                if jj:
                    silu(jj - 1)
            silu(11)
            dve.wait_ge(sem("a_exp"), 1)
            own.then_wait(dve.tensor_scalar(cst[0:4, 1:2], cst[0:4, 0:1], -1.0, None, ALU.mult))
            dve.wait_ge(sem("soft_logs"), 1)
            dve.scalar_tensor_tensor(SM["la"], SM["ga"], 0.0, SM["la"], ALU.max, ALU.add)
            own.then_wait(dve.scalar_tensor_tensor(SM["lf"], SM["ff"], 0.0, SM["lf"], ALU.min, ALU.subtract))
            own.then_wait(dve.tensor_scalar(SM["la"], SM["la"], cst[0:4, 1:2], None, ALU.mult))
            for t0, n in CHUNKS:
                dve.tensor_tensor_scan(SM["gc"][:, t0:t0 + n], SM["ones"][0:4, 0:n], SM["la"][:, t0:t0 + n], 0.0,
                                       ALU.mult, ALU.add).then_inc(sem("scans"), 1)
            own.then_wait(dve.tensor_tensor_scan(SM["ff"], SM["ones"], SM["lf"], 0.0, ALU.mult, ALU.add))
            dve.tensor_scalar(SM["negc"], SM["ff"], -1.0, None, ALU.mult).then_inc(sem("fox_c"), 1)
            wait_read(dve, aux, "ss")
            dve.reciprocal(SM["r8"], SM["r8"]).then_inc(sem("qk_factor"), 1)
            dve.wait_ge(sem("conv_silu"), 12)
            for j in range(8):
                bank = aux.wait(dve, ("rb", j))
                y = R[:, R2 + j * TM:R2 + (j + 1) * TM]
                aux.free(dve.scalar_tensor_tensor(y, y, 0.5 * float(P) ** -0.5 if j < 4 else 0.5, bank[:, 0:TM],
                                                  ALU.mult, ALU.mult), ("rb", j))
            bank = aux.wait(dve, "tok")
            dve.tensor_copy(tk[0:M, 0:8], bank[0:M, 0:8])
            aux.free(dve.tensor_copy(tk[:, 8:24], bank[:, 8:24]), "tok")
            for t in range(TT):
                gate(("gz", t), R[:, R4 + t * 512:R4 + (t + 1) * 512])

            wait_read(dve, aux, "tok")
            for c, (t0, n) in enumerate(CHUNKS):
                def four(ap, w=None):
                    return ap.rearrange("p (h n) -> p h n", h=GH)

                gc, beta = tk[0:n, c * 8:c * 8 + 4], tk[0:n, c * 8 + 4:c * 8 + 8]
                d, d1, d2 = (xn[0:n, s * 512:s * 512 + 4 * n] for s in range(3))
                bank = aux.wait(dve, ("bc", c))
                own.then_wait(dve.tensor_copy(g3[:, c * 12 + 8:c * 12 + 12], four(bank[:, 0:4 * n])[:, :, n - 1]))
                ins = dve.tensor_tensor(four(d), four(bank[0:n, 0:4 * n]), spread(gc, n), ALU.subtract)
                if c:
                    ins.then_inc(sem("bc_read"), 1)
                    dve.wait_ge(sem("bc_read"), c)
                else:
                    aux.free(ins, ("bc", c))
                    wait_read(dve, aux, ("bc", c))
                dve.tensor_copy(g3[0:n, c * 12:c * 12 + 4], gc)
                dve.tensor_tensor(g3[0:n, c * 12 + 4:c * 12 + 8], g3[0:n, c * 12 + 8:c * 12 + 12], gc,
                                  ALU.subtract).then_inc(sem("log_decays"), 1)
                if c:
                    dve.tensor_tensor(four(d2), four(d), over(tab[0:n, TB_INCL:TB_INCL + n], GH), ALU.min)
                dve.tensor_tensor(four(d1), four(d), over(tab[0:n, TB_STRICT:TB_STRICT + n], GH), ALU.max).then_inc(
                    sem("clamped"), 1)
                dve.wait_ge(sem("decays_small"), c + 1)
                dve.tensor_tensor(be[0:n, c * 4:c * 4 + 4], beta, e3[0:n, c * 12:c * 12 + 4], ALU.mult)
                own.then_wait(dve.tensor_scalar(hb[0:n, c * 4:c * 4 + 4], beta, 0.5, None, ALU.mult))
                dve.wait_ge(sem("decay_ready"), c + 1)
                own.then_wait(dve.tensor_tensor(four(d1), four(d1), spread(beta, n), ALU.mult))
                bank = aux.wait(dve, ("kk", c))
                a0 = 2 * C_ALL + C_OFF[c]
                aux.free(dve.tensor_tensor(PTb[0:n, a0:a0 + 4 * n], d1, bank[0:n, 0:4 * n], ALU.mult), ("kk", c))
                if c:
                    bank = aux.wait(dve, ("qk", c))
                    k0 = R4 + 3072 + (c - 1) * 512
                    aux.free(dve.tensor_tensor(R[:, k0:k0 + 512], d2, bank, ALU.mult), ("qk", c))
                    wait_read(dve, aux, ("bc", c))
                    q = R[:, R2:R2 + 12 * TM].rearrange("p (j t) -> p j t", j=12)[:, 0:4, t0:t0 + n]
                    dve.tensor_tensor(q, q, four(xn[:, 1536:2048]), ALU.mult).then_inc(sem("q_scaled"), 1)

                def rows_of(base):
                    buf, b0 = base
                    return four(buf[0:n, b0 + c * 512:b0 + (c + 1) * 512])

                bank = four(aux.wait(dve, ("kt", c))[0:n, :])
                if c < 2:
                    dve.tensor_tensor(rows_of(KDEC), bank, spread(e3[0:n, c * 12 + 4:c * 12 + 8], P), ALU.mult)
                aux.free(dve.tensor_tensor(rows_of(RK), bank, spread(be[0:n, c * 4:c * 4 + 4], P), ALU.mult), ("kt", c))
                bank = four(aux.wait(dve, ("vt", c))[0:n, :])
                aux.free(dve.tensor_tensor(rows_of(RV), bank, spread(hb[0:n, c * 4:c * 4 + 4], P), ALU.mult), ("vt", c))

            state = R[:, R1 + 3072:R1 + 3584]
            for kind, *key in gdn_fox_order():
                if kind == "Lx":
                    lv, c = key
                    n = CHUNKS[c][1]
                    by = aux.wait(dve, ("y", lv, c))
                    if not last_level(lv, c):
                        bx = aux.at(("x", lv, c))
                        X = PTb[0:n, C_OFF[c]:C_OFF[c] + 4 * n]
                        aux.free(dve.tensor_tensor(X, X, bx[0:n, 0:4 * n], ALU.subtract), ("x", lv, c))
                    Y = PTb[0:n, C_ALL + C_OFF[c]:C_ALL + C_OFF[c] + 4 * n]
                    aux.free(dve.tensor_tensor(Y, Y, by[0:n, 0:4 * n], ALU.subtract), ("y", lv, c))
                elif kind == "Fs":
                    hd = key[0]
                    bank = aux.wait(dve, ("fs", hd))
                    dve.tensor_reduce(fnm[:, 2 * hd:2 * hd + 1], bank[:, 0:P + M], AX, ALU.max, negate=True)
                    dve.tensor_reduce(fnm[:, 2 * hd + 1:2 * hd + 2], bank[:, P + M:3 * P + 2 * M], AX, ALU.max,
                                      negate=True).then_inc(sem("fox_max"), 1)
                elif kind == "Ft":
                    hd = key[0]
                    wait_read(dve, aux, ("fs", hd))
                    dve.reciprocal(frs[:, 2 * hd:2 * hd + 2], fsum[:, 2 * hd:2 * hd + 2]).then_inc(sem("fox_recip"), 1)
                    bank = aux.wait(dve, ("fm", hd))
                    c0 = hd % 2 * 640 + 384
                    aux.free(dve.tensor_copy(PfT[0:M, c0:c0 + 256], bank[0:M, 0:256]), ("fm", hd))
                elif kind == "V":
                    c = key[0]
                    if c:
                        dve.wait_ge(sem("go_square"), c)
                        s4 = slice(4 * c - 4, 4 * c)
                        dve.tensor_reduce(gss[:, s4], tmp[:, 0:512].rearrange("p (h n) -> p h n", h=GH), AX,
                                          ALU.add).then_inc(sem("go_sum"), 1)
                        dve.wait_ge(sem("go_std"), c)
                        own.then_wait(dve.reciprocal(grs[:, s4], gsd[:, s4]))
                        bank = aux.at(("go", c)).rearrange("p (h n) -> p h n", h=GH)
                        on = tmp[:, 512:1024]
                        aux.free(dve.tensor_tensor(on.rearrange("p (h n) -> p h n", h=GH), bank,
                                                   spread(grs[:, s4], P), ALU.mult), ("go", c))
                        wait_read(dve, aux, ("go", c))
                        m0 = R4 + 1024 + (c - 1) * D
                        dve.tensor_tensor(R[:, m0:m0 + 512], on, R[:, R4 + (c - 1) * 512:R4 + c * 512],
                                          ALU.mult).then_inc(sem("mix_ready"), 1)
                    if c < 2:
                        bank = aux.wait(dve, ("st", c))
                        if c == 0:
                            aux.free(dve.tensor_copy(state, bank), ("st", c))
                        else:
                            s3 = state.rearrange("p (h n) -> p h n", h=GH)
                            own.then_wait(dve.tensor_tensor(s3, s3, spread(e3[:, c * 12 + 8:c * 12 + 12], P), ALU.mult))
                            aux.free(dve.tensor_tensor(state, state, bank, ALU.add), ("st", c))
            even("mT", 4, into_xT, mix_gain)
            add_to_h([("mo", c, t) for c in range(2) for t in range(TT)])
            norm(6)
            even("xT_ffn", 4, into_xT, gain_of("ffn_norm_w_2"))
            for n in range(11):
                a = xn[:, n % 2 * 512:n % 2 * 512 + 512]
                gate(("fg", n), a)
                wait_read(dve, main, ("fg", n))
                bank = main.wait(dve, ("fu", n))
                main.free(dve.scalar_tensor_tensor(R[:, n * 512:(n + 1) * 512], a, 0.5, bank, ALU.mult, ALU.mult),
                          ("fu", n))
            add_to_h([("dn", c, t) for c in range(2) for t in range(TT)])
            roots(7)
            dve.wait_ge(sem("gain2_in"), 16)
            for t in range(TT):
                dve.scalar_tensor_tensor(xnrow(t), hrow(t), rstd[:, 14 + t:15 + t], gfin2[:, :], ALU.mult,
                                         ALU.mult).then_inc(sem("out_rows"), 1)

        @block.gpsimd
        def _(pool):
            for i in range(8):
                hd, t = i // 2, i % 2
                wait_read(pool, aux, ("rpv", hd, t))
                wait_read(pool, main, ("rg", hd, t))
                y = R[:, R3 + t * 2048 + hd * 512:R3 + t * 2048 + (hd + 1) * 512]
                pool.tensor_tensor(y, y, xn[:, i % 4 * 512:(i % 4 + 1) * 512], ALU.mult).then_inc(sem("ret_y"), 1)
            for i, (b, h0, nh) in enumerate(STEPS):
                pool.wait_ge(sem("nsa_scale"), i + 1)
                c0 = R2 + 2048 + i % 2 * 1024
                p = R[:, c0:c0 + 1024].rearrange("p (h n) -> p h n", h=2 * nh)
                pool.tensor_tensor(p, p, spread(esc[:, i * 8:i * 8 + 2 * nh], 1024 // (2 * nh)), ALU.mult).then_inc(
                    sem("nsa_p"), 1)
            wait_read(pool, aux, ("o", len(STEPS) - 1))
            for c, (t0, n) in enumerate(CHUNKS):
                for base in (0, C_ALL):
                    c0 = base + C_OFF[c]
                    pool.tensor_copy(PTb[0:n, c0:c0 + 4 * n].rearrange("p (h n) -> p h n", h=GH),
                                     over(ident[0:n, 0:n], GH)).then_inc(sem("xy_init"), 1)
            for lv, c in LEVEL_LIST:
                n = CHUNKS[c][1]
                wait_read(pool, aux, ("kk", c))
                if lv:
                    aux.wait(pool, ("z", lv - 1, c))
                a0, m0 = 2 * C_ALL + C_OFF[c], TB_LEVEL + lv * P
                pool.tensor_tensor(xT2[0:n, C_OFF[c]:C_OFF[c] + 4 * n].rearrange("p (h n) -> p h n", h=GH),
                                   PTb[0:n, a0:a0 + 4 * n].rearrange("p (h n) -> p h n", h=GH),
                                   over(tab[0:n, m0:m0 + n], GH), ALU.mult).then_inc(sem("level_part"), 1)


_INS = ["x", "meta", "weights", "side", "params", "tabs", "ret_tabs", "p_t", "gains"]


def kernel(**inputs):
    import numpy as _np
    import concourse.bacc as _bacc
    from concourse import mybir as _mybir
    from concourse.bass_utils import run_bass_kernel_spmd as _run

    a = {k: _np.asarray(v) for k, v in inputs.items()}
    w = {}
    for name in ("ret_w_in", "ret_w_out", "nsa_w_in", "nsa_w_out", "w_in_2", "w_out_2", "w_gate_2", "w_up_2", "w_down_2"):
        w[name] = a[name][0]
    for name in ("kv_w", "cmp_w1_k", "cmp_w1_v"):
        w[name] = a[name]
    for i in range(2):
        w[f"ple_w_gate{i}"], w[f"ple_w_emb{i}"] = a["ple_w_gate"][i], a["ple_w_emb"][i]

    def tiles(m, k0, kt, c0, n):
        return m[k0 * P:(k0 + kt) * P, c0:c0 + n].reshape(kt, P, n).transpose(1, 0, 2).reshape(P, kt * n)

    shape_of = {"A": (8, 256), "B": (4, 512), "E": (2, 1024), "C": (8, 256)}
    weights = _np.empty((NU, P, UNIT), _np.float32)
    for u, (name, kind, k0, c0) in enumerate(UNITS):
        kt, n = shape_of[kind]
        weights[u] = tiles(w[name], k0, kt, c0, n)
    side = _np.concatenate([
        tiles(w["nsa_w_in"], 0, KD, 4096, 48),
        tiles(_np.concatenate([w["w_in_2"][:, 2048:2056], w["w_in_2"][:, 3592:3600]], 1), 0, KD, 0, 16),
        tiles(a["cmp_w2_k"], 0, 2, 0, P), tiles(a["cmp_w2_v"], 0, 2, 0, P)], 1)

    def columns(v):
        return v.reshape(-1, P).T

    def column(v):
        out = _np.zeros((P, 1), _np.float32)
        out[:v.size, 0] = v.reshape(-1)
        return out

    params = _np.concatenate([
        columns(a["ret_norm"][0]), columns(a["kv_norm"]), columns(a["nsa_norm"][0]), columns(a["ple_norm"][0]),
        columns(a["ple_norm"][1]), columns(a["attn_norm_w_2"][0]), columns(a["ffn_norm_w_2"][0]),
        columns(a["ret_gn"][0]), columns(a["gdn_norm_w_2"][0]), a["cmp_pe_k"].T, a["cmp_pe_v"].T,
        columns(a["conv_w_2"][0].reshape(-1)), column(a["a_log_2"]), column(a["dt_bias_2"]), column(a["fgate_b_2"])], 1)
    p_t = _np.concatenate([tiles(_np.ascontiguousarray(a["p"][i, 0].T), 0, 2, 0, T) for i in range(2)], 1)
    tabs, ret_tabs = tables()
    arrays = {
        "x": a["x"][0], "meta": a["meta_tokens_2"], "weights": weights, "side": side, "params": params,
        "tabs": tabs, "ret_tabs": ret_tabs, "p_t": p_t,
        "gains": _np.stack([a["final_norm"], a["final_norm_w_2"]]),
    }
    nc = _bacc.Bacc("TRN2", target_bir_lowering=False, num_devices=1)
    args, feed = [], {}
    for name in _INS:
        feed[f"in_{name}"] = _np.ascontiguousarray(arrays[name])
        args.append(nc.dram_tensor(f"in_{name}", feed[f"in_{name}"].shape, _mybir.dt.from_np(feed[f"in_{name}"].dtype),
                                   kind="ExternalInput").ap())
    args.append(nc.dram_tensor("out_0", (T, D), F32, kind="ExternalOutput").ap())
    two_models_kernel(nc, *args)
    r = _run(nc, [feed], core_ids=[0])
    return r.results[0]["out_0"].reshape(1, T, D)
```

```python
from contextlib import ExitStack

import numpy as np

import concourse.bass as bass
from concourse import mybir

F32 = mybir.dt.float32
F32R = mybir.dt.float32r
ALU = mybir.AluOpType
ACT = mybir.ActivationFunctionType
AX = mybir.AxisListType.X

P = 128
D = 1024
KD = D // P
T = 256
TT = T // P
M = 16
TM = T + M
EPS = 1e-6
NEG = -1e30

RH = 4
NSA_H, NSA_G, NSA_HPG = 16, 4, 4
CMP_L, CMP_STRIDE = 32, 16
CMP_N = (T - CMP_L) // CMP_STRIDE + 1
CMP_ROWS = NSA_G * CMP_N
GH = 4
FH, FD = 8, 64
FF = 2816
CHUNKS = [(0, M), (M, P), (M + P, P)]
LEVELS = [1, 2, 4, 8, 16, 32, 64]

UNIT = 2048
RING = 4
HIGH = 3



def weight_units():
    units = []

    def a(name, c0, n):
        units.extend((name, "A", 0, c0 + 256 * i) for i in range(n // 256))

    def b(name, c0, n, kt=KD):
        for c in range(n // 512):
            units.extend((name, "B", k0, c0 + 512 * c) for k0 in range(0, kt, 4))

    a("ret_w_in", 0, 2048)
    b("ret_w_in", 2048, 4096)
    b("ret_w_out", 0, D, 16)
    units.append(("ple_w_emb0", "E", 0, 0))
    b("ple_w_gate0", 0, D)
    a("kv_w", 0, 1024)
    a("kv_w", 1024, 512)
    a("kv_w", 2048, 512)
    b("kv_w", 1536, 512)
    b("kv_w", 2560, 512)
    units.extend(("cmp_w1_k", "C", k0, 0) for k0 in range(0, CMP_L, 8))
    units.extend(("cmp_w1_v", "C", k0, 0) for k0 in range(0, CMP_L, 8))
    a("nsa_w_in", 0, 2048)
    b("nsa_w_in", 2048, 2048)
    b("nsa_w_out", 0, D, 16)
    units.append(("ple_w_emb1", "E", 0, 0))
    b("ple_w_gate1", 0, D)
    a("w_in_2", 512, 512)
    a("w_in_2", 0, 512)
    a("w_in_2", 1024, 512)
    a("w_in_2", 2056, 1024)
    b("w_in_2", 3080, 512)
    b("w_in_2", 1536, 512)
    b("w_out_2", 0, D)
    for c in range(0, FF, 256):
        units.append(("w_gate_2", "A", 0, c))
        units.append(("w_up_2", "A", 0, c))
    for c in range(2):
        units.extend(("w_down_2", "B", k0, 512 * c) for k0 in range(0, 20, 4))
    units.append(("w_down_2", "E", 20, 0))
    return units


UNITS = weight_units()
NU = len(UNITS)
IS_SPLIT = [not name.startswith("ple_w_emb") for name, *_ in UNITS]
SPLITS = [sum(IS_SPLIT[:u + 1]) for u in range(NU)]

PARAM = {}
_at = 0
for _name, _n in [("ret_norm", 8), ("kv_norm", 8), ("nsa_norm", 8), ("ple_norm0", 8), ("ple_norm1", 8),
                  ("attn_norm_w_2", 8), ("ffn_norm_w_2", 8), ("ret_gn", 16), ("gdn_norm_w_2", 1),
                  ("cmp_pe_k", CMP_L), ("cmp_pe_v", CMP_L), ("conv_w_2", 48), ("a_log_2", 1),
                  ("dt_bias_2", 1), ("fgate_b_2", 1)]:
    PARAM[_name] = _at
    _at += _n
NPARAM = _at
SIDE_BG, SIDE_G2, SIDE_W2K, SIDE_W2V = 0, KD * 48, KD * 64, KD * 64 + 256
NSIDE = KD * 64 + 512
TB_ID, TB_CAUSAL, TB_CMP, TB_ROW, TB_STRICT, TB_INCL, TB_LEVEL = 0, 128, 256, 286, 288, 416, 544
TB_ONE = TB_LEVEL + 128 * len(LEVELS)
NTAB = TB_ONE + 15
RT_COS, RT_SIN, RT_DECAY = 0, 256, 512
NRT = 512 + RH * 256


def tables():
    i = np.arange(P)
    t = np.zeros((P, NTAB), np.float32)
    t[:, TB_ID:TB_ID + P] = np.eye(P)
    t[:, TB_CAUSAL:TB_CAUSAL + P] = np.where(i[None] <= i[:, None], 0.0, NEG)
    end = np.arange(CMP_N) * CMP_STRIDE + CMP_L - 1
    for b in range(TT):
        t[:, TB_CMP + b * CMP_N:TB_CMP + (b + 1) * CMP_N] = np.where(end[None] <= (b * P + i)[:, None], 0.0, NEG)
        t[:, TB_ROW + b] = (b * P + i >= CMP_L - 1)
    t[:, TB_STRICT:TB_STRICT + P] = np.where(i[None] < i[:, None], 0.0, -NEG)
    t[:, TB_INCL:TB_INCL + P] = np.where(i[None] >= i[:, None], 0.0, NEG)
    for n, m in enumerate(LEVELS):
        same = (i[:, None] // (2 * m)) == (i[None] // (2 * m))
        t[:, TB_LEVEL + n * P:TB_LEVEL + (n + 1) * P] = same & (i[:, None] // m % 2 == 1) & (i[None] // m % 2 == 0)
    t[:, TB_ONE + 7] = 1.0
    r = np.zeros((P, NRT), np.float32)
    inv = (np.float32(10000.0) ** (-np.arange(P, dtype=np.float32) / np.float32(P))).astype(np.float32)
    ang = (np.arange(T, dtype=np.float32)[None] * inv[:, None]).astype(np.float32)
    r[:, RT_COS:RT_COS + T] = np.cos(ang)
    r[:, RT_SIN:RT_SIN + T] = np.sin(ang)
    lg = np.log1p(-(2.0 ** (-5.0 - np.arange(RH))))
    diff = (np.arange(T)[None] - i[:, None]).astype(np.float64)
    for h in range(RH):
        r[:, RT_DECAY + h * T:RT_DECAY + (h + 1) * T] = np.where(
            diff >= 0, np.exp(np.maximum(diff, 0) * lg[h]), 0.0) * 256.0 ** -0.5
    return t, r


class Banks:

    def __init__(self, tensor, first, uses, full, freed, begun):
        self.tensor, self.first, self.uses, self.full_sem, self.freed = tensor, first, uses, full, freed
        self.index = {key: n for n, (key, _) in enumerate(uses)}
        assert len(self.index) == len(uses)
        self.rank, counts = [], {}
        for _, engine in uses:
            counts[engine] = counts.get(engine, 0) + 1
            self.rank.append(counts[engine])
        self.filled, self.released = 0, {}
        self.begun = begun
        self.unit = {}

    def at(self, key):
        return self.tensor[:, self.first + self.index[key] % 4, :]

    def open(self, pe, key):
        n = self.index[key] - 4
        if n >= 0:
            pe.wait_ge(self.freed[self.uses[n][1]], self.rank[n])
        return self.at(key)

    def full(self, ins, key):
        self.unit[key] = self.begun[0] - 1
        assert self.index[key] == self.filled, (key, self.uses[self.filled])
        self.filled += 1
        ins.then_inc(self.full_sem, 1)

    def wait(self, engine, key):
        engine.wait_ge(self.full_sem, self.index[key] + 1)
        return self.at(key)

    def free(self, ins, key):
        n = self.index[key]
        engine = self.uses[n][1]
        self.released[engine] = self.released.get(engine, 0) + 1
        assert self.released[engine] == self.rank[n], (key, engine)
        ins.then_inc(self.freed[engine], 1)


STEPS = [(0, 4 * g, 4) for g in range(4)] + [(1, 2 * n, 2) for n in range(8)]
NORMS = ["ret", "ple0", "kv", "ple1", "final", "attn", "ffn", "last"]


def main_uses():
    u = [(("rqk", n), "dve") for n in range(8)]
    u += [(("rv", c, t), "act") for c in range(4) for t in range(TT)]
    u += [(("rg", c, t), "dve") for c in range(4) for t in range(TT)]
    u += [(("ro", c, t), "dve") for c in range(2) for t in range(TT)]

    def ple(n):
        return [(("emb", n, c, t), "act") for c in range(2) for t in range(TT)] + \
               [(("pg", n, c, t), "act") for c in range(2) for t in range(TT)]

    u += ple(0)
    u += [(("kvA", n), "act") for n in range(8)]
    u += [(("kvB", n, t), "act") for n in range(2) for t in range(TT)]
    u += [(("cmp", n), "dve") for n in range(2)]
    u += [(("nq", n), "act") for n in range(8)]
    u += [(("bg", t), "act") for t in range(TT)]
    u += [(("ng", c, t), "dve") for c in range(4) for t in range(TT)]
    u += [(("no", c, t), "dve") for c in range(2) for t in range(TT)]
    u += ple(1)
    u += [("gb", "act"), ("ga", "dve"), ("ff", "dve")]
    u += [(("gin", j), "act") for j in range(12)]
    u += [(("fin", j), "act") for j in range(8)]
    u += [(("fv", c), "act") for c in range(3)]
    u += [(("gz", t), "dve") for t in range(TT)]
    u += [(("mo", c, t), "dve") for c in range(2) for t in range(TT)]
    for n in range(11):
        u += [(("fg", n), "dve"), (("fu", n), "dve")]
    u += [(("dn", c, t), "dve") for c in range(2) for t in range(TT)]
    return u


def tr_uses(name, n):
    return [((name, f), "dve") for f in range(n)]


def nsa_order():
    order = [("S", 0), ("S", 1)]
    for i in range(len(STEPS)):
        order += [("G", i)] * (i < 4) + [("O", i)]
        if i + 2 < len(STEPS):
            order.append(("S", i + 2))
    return order


def aux_uses():
    u = [("meta", "dve")] + tr_uses("xT_ret", 4)
    u += [(("rs", h), "dve") for h in range(RH)]
    for h in range(RH):
        u += [(("rpv", h, t), "act") for t in range(TT)]
    u += tr_uses("yT", 8)
    u += tr_uses("xT_ple0", 4)
    u += tr_uses("xT_kv", 4)
    u += [(("hT", n), "dve") for n in range(2)] + [(("c2", n), "dve") for n in range(2)]
    u += [(("cs", b), "dve") for b in range(TT)]
    for kind, i in nsa_order():
        if kind == "S":
            u += [(("s", i), "act"), (("w", i), "act")]
        if kind == "O":
            u += [(("sT", i), "dve"), (("wT", i), "act"), (("cT", i), "dve"), (("o", i), "dve")]
    u += tr_uses("oT", 8)
    u += tr_uses("xT_ple1", 4)
    u += tr_uses("xT_attn", 4)
    u += [("ss", "act")] + [(("rb", j), "dve") for j in range(8)]
    u += [("tok", "dve")]
    for c in range(3):
        u += [(("bc", c), "act" if c else "dve"), (("kk", c), "dve")]
        if c:
            u += [(("qk", c), "dve")]
        u += [(("kt", c), "dve"), (("vt", c), "dve")]
    u += gdn_fox_uses()
    u += tr_uses("mT", 4)
    u += tr_uses("xT_ffn", 4)
    return u


def level_chunks(n):
    return [c for c in (1, 2, 0) if 2 * LEVELS[n] <= CHUNKS[c][1]]


def last_level(n, c):
    return 2 * LEVELS[n] == CHUNKS[c][1]


def gdn_fox_order():
    order = [("Fs", 0)]
    for n in range(len(LEVELS)):
        order += [("Lz", n, c) for c in level_chunks(n)] + [("Ft", n)]
        order += [("Lx", n, c) for c in level_chunks(n)] + [("Fo", n), ("Fs", n + 1)]
    order += [("W", 1), ("W", 2), ("V", 0), ("Ft", 7), ("V", 1), ("Fo", 7), ("V", 2)]
    return order


def gdn_fox_uses():
    u = []
    for kind, *at in gdn_fox_order():
        n = at[0]
        if kind == "Lz":
            u += [(("z", *at), "act")]
        elif kind == "Lx":
            u += ([] if last_level(*at) else [(("x", *at), "dve")]) + [(("y", *at), "dve")]
        elif kind == "Fs":
            u += [(("fs", n), "act")]
        elif kind == "Ft":
            u += [(("fT", n), "act"), (("fm", n), "dve")]
        elif kind == "Fo":
            u += [(("fo", n), "act")]
        elif kind == "W":
            u += [(("gw", n), "act")]
        else:
            u += [(("vn", n), "act")] + [(("go", n), "dve")] * (n > 0) + [(("st", n), "dve")] * (n < 2)
    return u


R1, R2, R3, R4 = 0, 4096, 8192, 12288
GIN_TILES = [4, 5, 6, 7, 0, 1, 2, 3, 8, 9, 10, 11]
RAW_W = TM + 3
C_OFF = [0, 4 * M, 4 * M + 4 * P]
C_ALL = 4 * M + 8 * P
CMP_K, CMP_V = 4 * CMP_ROWS, 5 * CMP_ROWS
LEVEL_LIST = [(n, c) for n in range(len(LEVELS)) for c in level_chunks(n)]


def two_models_kernel(nc, x, meta, weights, side, params, tabs, ret_tabs, p_t, gains, out):
    ctx = ExitStack()
    with ctx:
        one_pass = {}

        def sb(name, cols, parts=False):
            buf = ctx.enter_context(nc.sbuf_tensor(name, [P, cols], F32))
            if parts:
                one_pass[buf.name] = nc.alloc_sbuf_tensor_at(f"{name}_parts", [P, cols], F32R,
                                                             offset=nc.sbuf_base - 4 * cols)
            return buf

        def as_r(ap):
            return bass.AP(tensor=one_pass[ap.tensor.name], offset=ap.offset, ap=ap.ap)

        def value_of(ap):
            return as_r(ap).bitcast(F32)

        sems = {}

        def sem(name):
            if name not in sems:
                sems[name] = ctx.enter_context(nc.semaphore(name))
            return sems[name]

        ring = sb("ring", RING * UNIT, True)
        high = sb("high", HIGH * UNIT, True)
        gates_high = sb("gates_high", KD * 16, True)
        side_sb = sb("side_sb", NSIDE, True)
        tab = sb("tab", NTAB)
        par = sb("par", NPARAM)
        h = sb("h", TT * D)
        xn = sb("xn", TT * D, True)
        xT = sb("xT", KD * TM, True)
        xT2 = sb("xT2", KD * TM, True)
        R = sb("R", 4 * 4096, True)
        PTb = sb("PTb", 4096, True)
        G1 = sb("G1", 2 * D)
        tmp = sb("tmp", 1024)
        nw = sb("nw", 1088)
        Pf = sb("Pf", 1088)
        PfT = sb("PfT", 1280)
        small = sb("small", 560)
        psum = ctx.enter_context(nc.psum_tensor("psum", [P, 8, 512], F32))

        freed = {e: sem(f"main_read_by_{e}") for e in ("act", "dve")}
        begun = [0]
        main = Banks(psum, 0, main_uses(), sem("main_filled"), freed, begun)
        freed = {e: sem(f"aux_read_by_{e}") for e in ("act", "dve")}
        aux = Banks(psum, 4, aux_uses(), sem("aux_filled"), freed, begun)

        at = [0]

        def cols(n):
            at[0] += n
            assert at[0] <= 560
            return small[:, at[0] - n:at[0]]

        sumsq, std, rstd = cols(16), cols(16), cols(16)
        msum = cols(3)
        eps = cols(1)
        bn, mv, rsd, rrs, nmr = cols(24), cols(16), cols(8), cols(8), cols(8)
        half_gn = cols(17)
        bgt = cols(96)
        nmx, esum, esc = cols(96), cols(96), cols(96)
        tk, g3, e3, be = nmx[:, 0:24], nmx[:, 24:60], esum[:, 0:36], esum[:, 36:48]
        hb, fnm, fsum, frs = esum[:, 48:60], esc[:, 0:16], esc[:, 16:32], esc[:, 32:48]
        gss, gsd, grs = esc[:, 48:56], esc[:, 56:64], esc[:, 64:72]
        cst = cols(32)

        ident = tab[:, TB_ID:TB_ID + P]
        causal = tab[:, TB_CAUSAL:TB_CAUSAL + P]

        def param(name, n=0, rows=P):
            return par[0:rows, PARAM[name] + n:PARAM[name] + n + 1]

        def hrow(t, c=0, n=D):
            return h[:, t * D + c:t * D + c + n]

        def xnrow(t):
            return xn[:, t * D:(t + 1) * D]

        def spread(ap, inner):
            return ap.unsqueeze(2).to_broadcast([ap.shape[0], ap.shape[1], inner])

        def over(ap, outer):
            return ap.unsqueeze(1).to_broadcast([ap.shape[0], outer, ap.shape[1]])

        def kt_cols(buf, kt, c0, n, width=TM, base=0):
            return buf[:, base + kt * width + c0:base + kt * width + c0 + n]

        def into_x(kt):
            return kt_cols(xT, kt, M, T), kt_cols(xT2, kt, M, T)

        def into_kv(kt):
            return kt_cols(xT, kt, M, T), R[:, R4 + kt * T:R4 + (kt + 1) * T]

        def into_nsa(kt):
            return kt_cols(xT2, kt, M, T), PTb[:, 2048 + kt * T:2048 + (kt + 1) * T]

        def into_out(kt):
            return R[:, R1 + kt * T:R1 + (kt + 1) * T], R[:, R2 + kt * T:R2 + (kt + 1) * T]

        class Marks:

            def __init__(self, engine, name):
                self.engine, self.sem, self.n = engine, sem(name), 0

            def then_wait(self, ins):
                self.n += 1
                ins.then_inc(self.sem, 1)
                self.engine.wait_ge(self.sem, self.n)

        def wait_read(engine, banks, key):
            n = banks.index[key]
            engine.wait_ge(banks.freed[banks.uses[n][1]], banks.rank[n])

        turns = []

        def turned(name, n, *readers):
            for place, gain in readers:
                for f in range(n):
                    turns.append(((name, f), [(kt, place(kt), gain(kt)) for kt in (2 * f, 2 * f + 1)],
                                  place is readers[-1][0]))

        def gain_of(name):
            return lambda kt: param(name, kt)

        turned("xT_ret", 4, (into_x, gain_of("ret_norm")))
        turned("yT", 8, (into_out, lambda kt: half_gn[:, kt:kt + 1]))
        turned("xT_ple0", 4, (into_x, gain_of("ple_norm0")))
        turned("xT_kv", 4, (into_kv, gain_of("kv_norm")), (into_nsa, gain_of("nsa_norm")))
        turned("oT", 8, (into_out, lambda kt: 0.5))
        turned("xT_ple1", 4, (into_x, gain_of("ple_norm1")))
        turned("xT_attn", 4, (into_x, gain_of("attn_norm_w_2")))
        turned("mT", 4, (into_x, lambda kt: half_gn[:, 16:17] if kt < 4 else 1.0))
        turned("xT_ffn", 4, (into_x, gain_of("ffn_norm_w_2")))

        def turned_high(act, name, wait):
            for key, parts, frees in turns:
                if key[0] == name:
                    bank = wait(aux, key)
                    if name == "xT_kv" and frees:
                        act.wait_ge(sem("kv_low"), key[1] + 1)
                    for n, (kt, (hi, _), g) in enumerate(parts):
                        ins = act.activation(as_r(hi), bank[:, n * T:(n + 1) * T], ACT.Copy, scale=g)
                    ins.then_inc(sem("turned_high"), 1)

        def turned_low(dve, name, wait):
            for n_turn, (key, parts, frees) in enumerate(turns):
                if key[0] == name:
                    bank = wait(aux, key)
                    dve.wait_ge(sem("turned_high"), n_turn + 1)
                    for n, (kt, (hi, lo), g) in enumerate(parts):
                        ins = dve.scalar_tensor_tensor(as_r(lo), bank[:, n * T:(n + 1) * T], g, value_of(hi),
                                                       ALU.mult,
                                                       ALU.subtract)
                    if frees:
                        aux.free(ins, key)
                    else:
                        ins.then_inc(sem("kv_low"), 1)

        def split_units(engine, split, ahead):
            done = [0]

            def up_to(u):
                while done[0] <= min(u, NU - 1):
                    if IS_SPLIT[done[0]]:
                        split(done[0])
                    done[0] += 1

            def wait(banks, key):
                up_to(banks.unit[key] + ahead)
                return banks.wait(engine, key)

            def after_read(banks, key):
                up_to(banks.unit[key] + ahead)
                wait_read(engine, banks, key)

            return wait, after_read, up_to

        def blocks(n):
            size = CMP_L * CMP_ROWS
            hi = R[:, R3 + n * size:R3 + (n + 1) * size]
            return hi, (R[:, R4 + 2048:R4 + 2048 + size] if n == 0 else xn[:, 0:size])

        def hidden(k, part):
            return R[:, (part * 22 + k) * T:(part * 22 + k + 1) * T]

        RV, RK, KDEC = (R, R1), (R, R1 + 1536), (G1, 0)
        SM = {}
        for n, (name, rows) in enumerate([("ga", 4), ("la", 4), ("gc", 4), ("beta", 4), ("ff", 8), ("lf", 8), ("ones", 8)]):
            SM[name] = R[0:rows, R4 + 1024 + n * TM:R4 + 1024 + (n + 1) * TM]
        SM["negc"] = R[0:8, R3 + 8 * TM + 1536:R3 + 9 * TM + 1536]
        SM["r8"] = xn[0:8, 0:TM]

        block = ctx.enter_context(nc.Block())

        @block.sync
        def _(sp):
            def load(name, dst, src):
                sp.dma_start(dst, src).then_inc(sem(name), 16)

            for t in range(TT):
                load(f"x_in{t}", hrow(t), x[t * P:(t + 1) * P, :])
            load("par_in", par[:, :], params)
            load("tab_in", tab[:, :], tabs)
            load("meta_in", R[0:M, R3:R3 + D], meta)

            def unit(u):
                if u >= RING:
                    sp.wait_ge(sem("units_used"), u - RING + 1)
                sp.dma_start(ring[:, u % RING * UNIT:(u % RING + 1) * UNIT], weights[u]).then_inc(
                    sem(f"unit_in{u % RING}"), 16)

            for u in range(2):
                unit(u)
            load("ret_in", R[:, R4:R4 + NRT], ret_tabs)
            for u in range(2, RING):
                unit(u)
            load("pT_in", G1[:, D:2 * D], p_t)
            load("side_in", side_sb[:, :], side)
            load("gain1_in", G1[:, 0:D], gains[0:1, :].to_broadcast([P, D]))
            for u in range(RING, NU):
                if u == UNITS.index(("w_gate_2", "A", 0, 0)):
                    main.wait(sp, ("emb", 1, 1, 1))
                    load("gain2_in", G1[:, D:2 * D], gains[1:2, :].to_broadcast([P, D]))
                unit(u)
            for t in range(TT):
                sp.wait_ge(sem("out_rows"), t + 1)
                sp.dma_start(out[t * P:(t + 1) * P, :], xnrow(t)).then_inc(sem("stored"), 16)
            sp.wait_ge(sem("stored"), 16 * TT)

        @block.tensor
        def _(pe):
            def mm(out, lhsT, rhs, first, last):
                return pe.matmul(out, lhsT, rhs, start=first, stop=last, skip_group_check=True)

            def parts3(product, out, lhsT, rhs, first, last):
                product(out, as_r(lhsT[0]), as_r(rhs[0]), first, False)
                product(out, as_r(lhsT[1]), as_r(rhs[0]), False, False)
                return product(out, as_r(lhsT[0]), as_r(rhs[1]), False, last)

            def next_unit(k):
                u = begun[0]
                begun[0] += 1
                if IS_SPLIT[u]:
                    pe.wait_ge(sem("units_low"), SPLITS[u])
                else:
                    pe.wait_ge(sem(f"unit_in{u % RING}"), 16 * (u // RING + 1))
                first = [u > 0]

                def product(*args):
                    ins = mm(*args)
                    if first[0]:
                        ins.then_inc(sem("units_used"), 1)
                    first[0] = False
                    return ins

                low = ring[:, u % RING * UNIT:(u % RING + 1) * UNIT].rearrange("p (k c) -> p k c", k=k)
                hi = high[:, u % HIGH * UNIT:(u % HIGH + 1) * UNIT].rearrange("p (k c) -> p k c", k=k)
                return lambda i, c: (hi[:, i, c], low[:, i, c]), product

            def project_a(keys, src, c0, n):
                w, product = next_unit(KD)
                for f in range(2):
                    key = keys[f * (len(keys) - 1)]
                    base = f * n if len(keys) == 1 else 0
                    if f == 0 or len(keys) == 2:
                        bank = main.open(pe, key)
                    for k in range(KD):
                        x_k = src(k, c0, n)
                        ins = parts3(product, bank[:, base:base + n], w(k, slice(f * P, (f + 1) * P)), x_k,
                                     k == 0, k == KD - 1)
                    if f == 1 or len(keys) == 2:
                        main.full(ins, key)

            def project_b(keys, src, rows, kt, ready=None):
                banks = [main.open(pe, key) for key in keys]
                for k0 in range(0, kt, 4):
                    if ready:
                        ready(k0)
                    w, product = next_unit(4)
                    for n, bank in enumerate(banks):
                        c0, m = rows[n]
                        for k in range(4):
                            x_k = src(k0 + k, c0, m)
                            ins = parts3(product, bank[0:m, :], x_k, w(k, slice(0, 512)), k0 + k == 0,
                                         k0 + k == kt - 1)
                        if k0 + 4 == kt:
                            main.full(ins, keys[n])

            def turn(name, f, src):
                bank = aux.open(pe, (name, f))
                for k in range(2):
                    for t in range(TT):
                        ins = pe.transpose(bank[:, k * T + t * P:k * T + (t + 1) * P], src(2 * f + k, t), ident)
                aux.full(ins, (name, f))

            def from_xn(kt, t):
                return xn[:, t * D + kt * P:t * D + (kt + 1) * P]

            def turn_norm(name, n):
                pe.wait_ge(sem("xn_ready"), 2 * (n + 1))
                for f in range(4):
                    turn(name, f, from_xn)

            pending = {}

            def need(place, name, n):
                for f in range(n):
                    pending[place, f] = name

            def tile_ready(place, k):
                name = pending.pop((place, k // 2), None)
                if name and place == "kv":
                    pe.wait_ge(sem("kv_low"), k // 2 + 1)
                elif name:
                    wait_read(pe, aux, (name, k // 2))

            def source(place, into):
                def tile_of(k, c0, n):
                    tile_ready(place, k)
                    return tuple(part[:, c0:c0 + n] for part in into(k))
                return tile_of

            def x_src(k, c0, n):
                tile_ready("x", k)
                return kt_cols(xT, k, c0, n), kt_cols(xT2, k, c0, n)

            kv_src = source("kv", into_kv)
            nsa_src = source("nsa", into_nsa)
            out_src = source("out", into_out)

            rows = [(M, P), (M + P, P)]
            rows0 = [(0, P), (P, P)]

            pe.wait_ge(sem("tab_in"), 16)
            pe.wait_ge(sem("meta_rows"), 1)
            bank = aux.open(pe, "meta")
            for kt in range(KD):
                ins = pe.transpose(bank[:, kt * M:(kt + 1) * M], R[0:M, R3 + kt * P:R3 + (kt + 1) * P], ident[0:M, 0:M])
            aux.full(ins, "meta")
            turn_norm("xT_ret", 0)
            need("x", "xT_ret", 4)
            for n in range(8):
                project_a([("rqk", n)], x_src, M, T)
            project_b([("rv", 0, t) for t in range(TT)], x_src, rows, KD)

            def qk_tile(which, hd, half, c0, n):
                return kt_cols(R, which * 8 + hd * 2 + half, c0, n, T, R1)

            pe.wait_ge(sem("rotated"), 8)
            for hd in range(RH):
                bank = aux.open(pe, ("rs", hd))
                for half in range(2):
                    mm(bank[:, 0:T], qk_tile(1, hd, half, 0, P), qk_tile(0, hd, half, 0, T), half == 0, half == 1)
                for half in range(2):
                    ins = mm(bank[:, T:T + P], qk_tile(1, hd, half, P, P), qk_tile(0, hd, half, P, P),
                             half == 0, half == 1)
                aux.full(ins, ("rs", hd))
            for c in range(1, 4):
                project_b([("rv", c, t) for t in range(TT)], x_src, rows, KD)

            def retention_values(hd):
                wait_read(pe, aux, ("rs", hd))
                for t in range(TT):
                    wait_read(pe, main, ("rv", hd, t))
                st = PTb[:, hd * 384:(hd + 1) * 384]
                v0 = R[:, R2 + hd * 512:R2 + (hd + 1) * 512]
                v1 = R[:, R2 + 2048 + hd * 512:R2 + 2048 + (hd + 1) * 512]
                bank = aux.open(pe, ("rpv", hd, 0))
                aux.full(mm(bank, st[:, 0:P], v0, True, True), ("rpv", hd, 0))
                bank = aux.open(pe, ("rpv", hd, 1))
                mm(bank, st[:, P:T], v0, True, False)
                aux.full(mm(bank, st[:, T:T + P], v1, False, True), ("rpv", hd, 1))

            for half in range(2):
                for c in (2 * half, 2 * half + 1):
                    project_b([("rg", c, t) for t in range(TT)], x_src, rows, KD)
                for hd in (2 * half, 2 * half + 1):
                    retention_values(hd)

            def y_src(base):
                return lambda kt, t: R[:, base + t * 2048 + kt * P:base + t * 2048 + (kt + 1) * P]

            def turn_before(name, src, need):
                def ready(k0):
                    if k0 % 8 == 0:
                        need(k0 // 8)
                        for f in range(k0 // 2, k0 // 2 + 4):
                            turn(name, f, src)
                        for f in range(k0 // 2, k0 // 2 + 4):
                            pending["out", f] = name
                return ready

            project_b([("ro", 0, t) for t in range(TT)], out_src, rows0, 16,
                      turn_before("yT", y_src(R3), lambda half: pe.wait_ge(sem("ret_y"), 4 * (half + 1))))
            project_b([("ro", 1, t) for t in range(TT)], out_src, rows0, 16)

            def ple(n, norm):
                pe.wait_ge(sem("pT_in"), 16)
                w, product = next_unit(2)
                for c in range(2):
                    for t in range(TT):
                        bank = main.open(pe, ("emb", n, c, t))
                        for k in range(2):
                            c0 = D + (n * 2 + k) * T + t * P
                            _, w_k = w(k, slice(c * 512, (c + 1) * 512))
                            ins = product(bank, G1[:, c0:c0 + P], w_k, k == 0, k == 1)
                        main.full(ins, ("emb", n, c, t))
                turn_norm(f"xT_ple{n}", norm)
                need("x", f"xT_ple{n}", 4)
                for c in range(2):
                    project_b([("pg", n, c, t) for t in range(TT)], x_src, rows, KD)

            ple(0, 1)

            turn_norm("xT_kv", 2)
            need("kv", "xT_kv", 4)
            need("nsa", "xT_kv", 4)
            for n in range(8):
                project_a([("kvA", n)], kv_src, 0, T)
            for n in range(2):
                project_b([("kvB", n, t) for t in range(TT)], kv_src, rows0, KD)
            for n in range(2):
                pe.wait_ge(sem("blocks_low"), n + 1)
                bank = main.open(pe, ("cmp", n))
                for k0 in range(0, CMP_L, 8):
                    w, product = next_unit(8)
                    hi, lo = blocks(n)
                    for k in range(8):
                        at_ = slice((k0 + k) * CMP_ROWS, (k0 + k + 1) * CMP_ROWS)
                        ins = parts3(product, bank[0:CMP_ROWS, 0:256], (hi[:, at_], lo[:, at_]), w(k, slice(0, 256)),
                                     k0 + k == 0, k0 + k == CMP_L - 1)
                main.full(ins, ("cmp", n))
            for n in range(4):
                project_a([("nq", n)], nsa_src, 0, T)
            pe.wait_ge(sem("side_in"), 16)
            for n in range(2):
                wait_read(pe, main, ("cmp", n))
                bank = aux.open(pe, ("hT", n))
                for k in range(2):
                    c0 = n * 512 + 256 + k * P
                    ins = pe.transpose(bank[:, k * CMP_ROWS:(k + 1) * CMP_ROWS], tmp[0:CMP_ROWS, c0:c0 + P],
                                       ident[0:CMP_ROWS, 0:CMP_ROWS])
                aux.full(ins, ("hT", n))
            wait_read(pe, aux, ("hT", 0))
            bank = aux.open(pe, ("c2", 0))
            for k in range(2):
                ins = mm(bank[:, 0:CMP_ROWS], side_sb[:, SIDE_W2K + k * P:SIDE_W2K + (k + 1) * P],
                         Pf[:, k * CMP_ROWS:(k + 1) * CMP_ROWS], k == 0, k == 1)
            aux.full(ins, ("c2", 0))
            wait_read(pe, aux, ("hT", 1))
            bank = aux.open(pe, ("c2", 1))
            for g in range(NSA_G):
                for k in range(2):
                    c0 = 2 * CMP_ROWS + k * CMP_ROWS + g * CMP_N
                    ins = mm(bank[0:CMP_N, g * P:(g + 1) * P], Pf[:, c0:c0 + CMP_N],
                             side_sb[:, SIDE_W2V + k * P:SIDE_W2V + (k + 1) * P], k == 0, k == 1)
            aux.full(ins, ("c2", 1))
            for n in range(4, 8):
                project_a([("nq", n)], nsa_src, 0, T)
            for t in range(TT):
                bank = main.open(pe, ("bg", t))
                for k in range(KD):
                    for part, x_k in enumerate(nsa_src(k, *rows0[t])):
                        ins = mm(bank[:, 0:48], value_of(x_k), side_sb[:, SIDE_BG + k * 48:SIDE_BG + (k + 1) * 48],
                                 k + part == 0, part == 1 and k == KD - 1)
                main.full(ins, ("bg", t))

            def q_tile(hd, b):
                return kt_cols(R, hd, b * P, P, T, R3)

            wait_read(pe, aux, ("c2", 1))
            wait_read(pe, main, ("nq", 7))
            for b in range(TT):
                bank = aux.open(pe, ("cs", b))
                for hd in range(NSA_H):
                    c0 = CMP_K + hd // NSA_HPG * CMP_N
                    ins = mm(bank[:, hd * CMP_N:(hd + 1) * CMP_N], q_tile(hd, b), Pf[:, c0:c0 + CMP_N], True, True)
                aux.full(ins, ("cs", b))
            wait_read(pe, main, ("kvB", 1, 1))

            def nsa_scores(i):
                b, h0, nh = STEPS[i]
                kt = b + 1
                for key, base in ((("s", i), R1 + 2048), (("w", i), R1 + 3072)):
                    bank = aux.open(pe, key)
                    for n in range(nh):
                        k0 = base + (h0 + n) // NSA_HPG * T
                        c0 = n * kt * P
                        mm(bank[:, c0:c0 + kt * P], q_tile(h0 + n, b), R[:, k0:k0 + kt * P], True, False)
                        ins = mm(bank[:, c0 + b * P:c0 + kt * P], ident, causal, False, True)
                    aux.full(ins, key)

            def nsa_values(i):
                b, h0, nh = STEPS[i]
                kt = b + 1
                slot = i % 2
                pe.wait_ge(sem("nsa_p"), i + 1)
                for key, base in ((("sT", i), 0), (("wT", i), 512)):
                    bank = aux.open(pe, key)
                    for n in range(4):
                        c0 = R2 + 2048 + slot * 1024 + base + n * P
                        ins = pe.transpose(bank[:, n * P:(n + 1) * P], R[:, c0:c0 + P], ident)
                    aux.full(ins, key)
                pe.wait_ge(sem("cmp_p"), b + 1)
                bank = aux.open(pe, ("cT", i))
                for n in range(nh):
                    c0 = b * 240 + (h0 + n) * CMP_N
                    ins = pe.transpose(bank[0:CMP_N, n * P:(n + 1) * P], xn[:, c0:c0 + CMP_N], ident)
                aux.full(ins, ("cT", i))
                bank = aux.open(pe, ("o", i))
                for key in ("sT", "wT", "cT"):
                    wait_read(pe, aux, (key, i))
                for n in range(nh):
                    g = (h0 + n) // NSA_HPG
                    o = bank[:, n * P:(n + 1) * P]
                    mm(o, nw[0:CMP_N, slot * 512 + n * P:slot * 512 + (n + 1) * P],
                       Pf[0:CMP_N, CMP_V + g * P:CMP_V + (g + 1) * P], True, False)
                    for br in range(2):
                        for k in range(kt):
                            c0 = slot * 1024 + br * 512 + (n * kt + k) * P
                            v0 = R2 + br * 1024 + k * 512 + g * P
                            ins = mm(o, PTb[:, c0:c0 + P], R[:, v0:v0 + P], False, br == 1 and k == kt - 1)
                aux.full(ins, ("o", i))

            for kind, i in nsa_order():
                if kind == "S":
                    nsa_scores(i)
                elif kind == "G":
                    project_b([("ng", i, t) for t in range(TT)], nsa_src, rows0, KD)
                else:
                    nsa_values(i)
            project_b([("no", 0, t) for t in range(TT)], out_src, rows0, 16,
                      turn_before("oT", y_src(R4), lambda half: wait_read(pe, aux, ("o", len(STEPS) - 1))))
            project_b([("no", 1, t) for t in range(TT)], out_src, rows0, 16)
            ple(1, 3)

            turn_norm("xT_attn", 4)
            need("x", "xT_attn", 4)
            wait_read(pe, aux, "meta")
            pe.wait_ge(sem("gates_low"), 1)
            for key, c0, n in (("gb", 0, 4), ("ga", 4, 4), ("ff", 8, 8)):
                bank = main.open(pe, key)
                for k in range(KD):
                    w0 = k * 16 + c0
                    w_k = gates_high[:, w0:w0 + n], side_sb[:, SIDE_G2 + w0:SIDE_G2 + w0 + n]
                    ins = parts3(mm, bank[0:n, 0:TM], w_k, x_src(k, 0, TM), k == 0, k == KD - 1)
                main.full(ins, key)
            for u in range(6):
                project_a([("gin", 2 * u), ("gin", 2 * u + 1)], x_src, 0, TM)
            for u in range(4):
                project_a([("fin", 2 * u), ("fin", 2 * u + 1)], x_src, 0, TM)

            def ch(j, c0, n):
                return kt_cols(R, j, c0, n, TM, R2)

            pe.wait_ge(sem("squares"), 1)
            bank = aux.open(pe, "ss")
            for j in range(8):
                ins = mm(bank[0:8, 0:TM], tab[:, TB_ONE + 7 - j:TB_ONE + 15 - j], PTb[:, j * TM:(j + 1) * TM],
                         j == 0, j == 7)
            aux.full(ins, "ss")
            project_b([("fv", c) for c in range(3)], x_src, [(0, M)] + rows, KD)
            pe.wait_ge(sem("qk_factor"), 1)
            for j in range(8):
                bank = aux.open(pe, ("rb", j))
                aux.full(mm(bank[:, 0:TM], ident[0:8, j:j + 1].to_broadcast([8, P]), SM["r8"], True, True), ("rb", j))
            pe.wait_ge(sem("scans"), 4)
            bank = aux.open(pe, "tok")
            for c, (t0, n) in enumerate(CHUNKS):
                for i, src in enumerate(("gc", "beta")):
                    ins = pe.transpose(bank[0:n, c * 8 + i * 4:c * 8 + i * 4 + 4], SM[src][:, t0:t0 + n],
                                       ident[0:4, 0:4])
            aux.full(ins, "tok")
            project_b([("gz", t) for t in range(TT)], x_src, rows, KD)

            wait_read(pe, aux, ("rb", 7))
            pe.wait_ge(sem("conv_silu"), 12)
            for c, (t0, n) in enumerate(CHUNKS):
                bank = aux.open(pe, ("bc", c))
                for hd in range(GH):
                    ins = mm(bank[:, hd * n:(hd + 1) * n], ident[0:4, hd:hd + 1].to_broadcast([4, P]),
                             SM["gc"][:, t0:t0 + n], True, True)
                aux.full(ins, ("bc", c))
                bank = aux.open(pe, ("kk", c))
                for hd in range(GH):
                    ins = mm(bank[0:n, hd * n:(hd + 1) * n], ch(4 + hd, t0, n), ch(4 + hd, t0, n), True, True)
                aux.full(ins, ("kk", c))
                if c:
                    bank = aux.open(pe, ("qk", c))
                    for hd in range(GH):
                        ins = mm(bank[0:n, hd * n:(hd + 1) * n], ch(4 + hd, t0, n), ch(hd, t0, n), True, True)
                    aux.full(ins, ("qk", c))
                for key, j0 in (("kt", 4), ("vt", 8)):
                    bank = aux.open(pe, (key, c))
                    for hd in range(GH):
                        ins = pe.transpose(bank[0:n, hd * P:(hd + 1) * P], ch(j0 + hd, t0, n), ident)
                    aux.full(ins, (key, c))

            def mat(buf, base, c, hd):
                n = CHUNKS[c][1]
                return buf[0:n, base + C_OFF[c] + hd * n:base + C_OFF[c] + (hd + 1) * n]

            def chunk_rows(base, c, hd):
                buf, b0 = base
                return buf[0:CHUNKS[c][1], b0 + c * 512 + hd * P:b0 + c * 512 + (hd + 1) * P]

            def fox_scores(hd):
                bank = aux.open(pe, ("fs", hd))
                p0, c0 = hd % 2 * FD, hd // 2 * TM
                at_ = 0
                for b in range(TT):
                    n = M + (b + 1) * P
                    o = bank[:, at_:at_ + n]
                    q0 = R3 + c0 + M + b * P
                    mm(o, R[p0:p0 + FD, q0:q0 + P], R[p0:p0 + FD, R3 + 4 * TM + c0:R3 + 4 * TM + c0 + n], True, False)
                    mm(o, ident[0:8, hd:hd + 1].to_broadcast([8, P]), SM["negc"][:, 0:n], False, False)
                    ins = mm(bank[:, at_ + n - P:at_ + n], ident, causal, False, True)
                    at_ += n
                aux.full(ins, ("fs", hd))

            def fox_turn(hd):
                p = Pf[:, hd % 2 * 416:hd % 2 * 416 + 416]
                wait_read(pe, aux, ("fs", hd))
                bank = aux.open(pe, ("fT", hd))
                for n, c0 in enumerate((M, P + 2 * M, 2 * P + 2 * M)):
                    ins = pe.transpose(bank[:, n * P:(n + 1) * P], p[:, c0:c0 + P], ident)
                aux.full(ins, ("fT", hd))
                bank = aux.open(pe, ("fm", hd))
                for n, c0 in enumerate((0, P + M)):
                    ins = pe.transpose(bank[0:M, n * P:(n + 1) * P], p[:, c0:c0 + M], ident)
                aux.full(ins, ("fm", hd))

            def fox_values(hd):
                wait_read(pe, aux, ("fT", hd))
                wait_read(pe, aux, ("fm", hd))
                slot = hd % 2 * 640
                bank = aux.open(pe, ("fo", hd))

                def v(c, m):
                    v0 = R3 + 8 * TM + c * 512 + hd * FD
                    return R[0:m, v0:v0 + FD]

                for b in range(TT):
                    o = bank[:, b * FD:(b + 1) * FD]
                    mm(o, PfT[0:M, slot + 384 + b * P:slot + 384 + (b + 1) * P], v(0, M), True, False)
                    for k in range(b + 1):
                        ins = mm(o, PfT[:, slot + (b + k) * P:slot + (b + k + 1) * P], v(1 + k, P), False, k == b)
                aux.full(ins, ("fo", hd))

            state, v_new = R1 + 3072, R1 + 3584
            pe.wait_ge(sem("fox_c"), 1)
            wait_read(pe, main, ("fv", 2))
            pe.wait_ge(sem("xy_init"), 6)
            for kind, *key in gdn_fox_order():
                if kind == "Fs":
                    fox_scores(key[0])
                elif kind == "Ft":
                    fox_turn(key[0])
                elif kind == "Fo":
                    fox_values(key[0])
                elif kind == "Lz":
                    lv, c = key
                    pe.wait_ge(sem("level_part"), LEVEL_LIST.index((lv, c)) + 1)
                    if lv:
                        wait_read(pe, aux, ("y", lv - 1, c))
                    n = CHUNKS[c][1]
                    bank = aux.open(pe, ("z", lv, c))
                    for hd in range(GH):
                        ins = mm(bank[0:n, hd * n:(hd + 1) * n], mat(xT2, 0, c, hd), mat(PTb, C_ALL, c, hd), True, True)
                    aux.full(ins, ("z", lv, c))
                elif kind == "Lx":
                    lv, c = key
                    wait_read(pe, aux, ("z", lv, c))
                    n = CHUNKS[c][1]
                    if not last_level(lv, c):
                        bank = aux.open(pe, ("x", lv, c))
                        for hd in range(GH):
                            ins = mm(bank[0:n, hd * n:(hd + 1) * n], mat(xT2, C_ALL, c, hd), mat(PTb, 0, c, hd),
                                     True, True)
                        aux.full(ins, ("x", lv, c))
                    bank = aux.open(pe, ("y", lv, c))
                    for hd in range(GH):
                        ins = mm(bank[0:n, hd * n:(hd + 1) * n], mat(PTb, 0, c, hd), mat(xT2, C_ALL, c, hd), True, True)
                    aux.full(ins, ("y", lv, c))
                elif kind == "W":
                    c = key[0]
                    wait_read(pe, aux, ("y", len(LEVELS) - 1, c))
                    bank = aux.open(pe, ("gw", c))
                    for hd in range(GH):
                        ins = mm(bank[:, hd * P:(hd + 1) * P], chunk_rows(RK, c, hd), mat(PTb, C_ALL, c, hd), True, True)
                    aux.full(ins, ("gw", c))
                else:
                    c = key[0]
                    t0, n = CHUNKS[c]
                    if c:
                        wait_read(pe, aux, ("st", c - 1))
                        wait_read(pe, aux, ("gw", c))
                    else:
                        wait_read(pe, aux, ("y", 3, 0))
                    bank = aux.open(pe, ("vn", c))
                    for hd in range(GH):
                        o = bank[0:n, hd * P:(hd + 1) * P]
                        ins = mm(o, mat(PTb, C_ALL, c, hd), chunk_rows(RV, c, hd), True, c == 0)
                        if c:
                            w0 = (c - 1) * 512 + hd * P
                            ins = mm(o, nw[:, w0:w0 + P], R[:, state + hd * P:state + (hd + 1) * P], False, True)
                    aux.full(ins, ("vn", c))
                    wait_read(pe, aux, ("vn", c))
                    if c:
                        bank = aux.open(pe, ("go", c))
                        for hd in range(GH):
                            o = bank[:, hd * P:(hd + 1) * P]
                            mm(o, ch(hd, t0, n), R[:, state + hd * P:state + (hd + 1) * P], True, False)
                            k0 = R4 + 3072 + (c - 1) * 512 + hd * P
                            ins = mm(o, R[:, k0:k0 + P], R[:, v_new + hd * P:v_new + (hd + 1) * P], False, True)
                        aux.full(ins, ("go", c))
                    if c < 2:
                        bank = aux.open(pe, ("st", c))
                        for hd in range(GH):
                            ins = mm(bank[:, hd * P:(hd + 1) * P], chunk_rows(KDEC, c, hd),
                                     R[0:n, v_new + hd * P:v_new + (hd + 1) * P], True, True)
                        aux.full(ins, ("st", c))

            pe.wait_ge(sem("mix_ready"), 2)
            wait_read(pe, aux, ("fo", FH - 1))
            for f in range(4):
                turn("mT", f, lambda kt, t: R[:, R4 + 1024 + t * D + kt * P:R4 + 1024 + t * D + (kt + 1) * P])
            need("x", "mT", 4)
            for c in range(2):
                project_b([("mo", c, t) for t in range(TT)], x_src, rows, KD)
            turn_norm("xT_ffn", 5)
            need("x", "xT_ffn", 4)
            for n in range(11):
                project_a([("fg", n)], x_src, M, T)
                project_a([("fu", n)], x_src, M, T)

            def hidden_src(k, t):
                return tuple(hidden(k, part)[:, t * P:(t + 1) * P] for part in range(2))

            banks = {(c, t): main.open(pe, ("dn", c, t)) for c in range(2) for t in range(TT)}
            for c in range(2):
                for k0 in range(0, 20, 4):
                    if c == 0:
                        pe.wait_ge(sem("hidden_low"), k0 // 2 + 2)
                    w, product = next_unit(4)
                    for t in range(TT):
                        for k in range(4):
                            parts3(product, banks[c, t], hidden_src(k0 + k, t), w(k, slice(0, 512)), k0 + k == 0, False)
            pe.wait_ge(sem("hidden_low"), 11)
            w, product = next_unit(2)
            for c in range(2):
                for t in range(TT):
                    for k in range(2):
                        ins = parts3(product, banks[c, t], hidden_src(20 + k, t), w(k, slice(c * 512, (c + 1) * 512)),
                                     False, k == 1)
                    main.full(ins, ("dn", c, t))
            assert begun[0] == NU

        @block.scalar
        def _(act):
            own = Marks(act, "act_step")

            def split_high(u):
                act.wait_ge(sem(f"unit_in{u % RING}"), 16 * (u // RING + 1))
                if u >= HIGH:
                    act.wait_ge(sem("units_used"), u - HIGH + 1)
                act.copy(as_r(high[:, u % HIGH * UNIT:(u % HIGH + 1) * UNIT]),
                         ring[:, u % RING * UNIT:(u % RING + 1) * UNIT]).then_inc(sem("units_high"), 1)

            wait, after_read, split_up_to = split_units(act, split_high, HIGH - 1)

            def norm_stats(n, wait_rows):
                for t in range(TT):
                    wait_rows(t)
                    ins = act.activation(xnrow(t), hrow(t), ACT.Square, accum_out=sumsq[:, 2 * n + t:2 * n + t + 1])
                own.then_wait(ins)
                act.activation(std[:, 2 * n:2 * n + 2], sumsq[:, 2 * n:2 * n + 2], ACT.Sqrt, scale=1.0 / D,
                               bias=eps).then_inc(sem("std_ready"), 1)

            def high_parts(name):
                turned_high(act, name, wait)

            gates = [0]

            def gate_tanh(key, before):
                i = gates[0]
                gates[0] += 1
                bank = wait(main, key)
                if before:
                    after_read(main, before)
                act.activation(tmp[:, i % 2 * 512:i % 2 * 512 + 512], bank, ACT.Tanh, scale=0.5).then_inc(
                    sem("gate_tanh"), 1)

            act.wait_ge(sem("eps_ready"), 1)
            act.wait_ge(sem("meta_in"), 16)
            own.then_wait(act.activation(tmp[0:M, 0:D], R[0:M, R3:R3 + D], ACT.Square, accum_out=msum[0:M, 0:1]))
            act.activation(msum[0:M, 1:2], msum[0:M, 0:1], ACT.Sqrt, scale=1.0 / D, bias=eps[0:M, :]).then_inc(
                sem("meta_std"), 1)
            norm_stats(0, lambda t: act.wait_ge(sem(f"x_in{t}"), 16))
            act.wait_ge(sem("par_in"), 16)
            split_up_to(1)
            high_parts("xT_ret")
            for c in range(4):
                for t in range(TT):
                    key = ("rv", c, t)
                    bank = wait(main, key)
                    main.free(act.copy(R[:, R2 + t * 2048 + c * 512:R2 + t * 2048 + (c + 1) * 512], bank), key)
            act.wait_ge(sem("rotated"), 8)
            seq = [("rg", c, t) for c in range(4) for t in range(TT)]
            for half in range(2):
                for i in range(4 * half, 4 * half + 4):
                    gate_tanh(seq[i], seq[i - 2] if i >= 2 else None)
                act.wait_ge(sem("ret_var"), 4 * (half + 1))
                act.activation(rsd[:, 4 * half:4 * half + 4],
                               mv.rearrange("p (i c) -> p i c", c=2)[:, 4 * half:4 * half + 4, 1], ACT.Sqrt,
                               bias=eps).then_inc(sem("ret_std"), 1)
                act.wait_ge(sem("ret_norm"), half + 1)
                for i in range(4 * half, 4 * half + 4):
                    key = ("rpv", i // 2, i % 2)
                    bank = wait(aux, key)
                    if i >= 4:
                        act.wait_ge(sem("ret_y"), i - 3)
                    aux.free(act.activation(xn[:, i % 4 * 512:(i % 4 + 1) * 512], bank, ACT.Identity,
                                            scale=rrs[:, i:i + 1], bias=nmr[:, i:i + 1]), key)
            act.wait_ge(sem("half_gn"), 1)
            high_parts("yT")

            def ple(n, norm, wait_rows):
                norm_stats(norm, wait_rows)
                for c in range(2):
                    for t in range(TT):
                        key = ("emb", n, c, t)
                        bank = wait(main, key)
                        c0 = R2 + t * D + c * 512
                        main.free(act.activation(R[:, c0:c0 + 512], bank, ACT.Copy, scale=0.5), key)
                high_parts(f"xT_ple{n}")
                for i in range(4):
                    key = ("pg", n, i // 2, i % 2)
                    bank = wait(main, key)
                    if i >= 2:
                        act.wait_ge(sem("h_ready"), 4 * n + i - 1)
                    main.free(act.activation(tmp[:, i % 2 * 512:i % 2 * 512 + 512], bank, ACT.Tanh, scale=0.5), key)

            ple(0, 1, lambda t: after_read(main, ("ro", 1, t)))

            act.wait_ge(sem("side_in"), 16)
            act.copy(as_r(gates_high[:, :]), side_sb[:, SIDE_G2:SIDE_G2 + KD * 16]).then_inc(sem("gates_high"), 1)

            norm_stats(2, lambda t: act.wait_ge(sem("h_ready"), 3 + t))
            high_parts("xT_kv")

            def blocks_high(n):
                act.wait_ge(sem("blocks_ready"), n + 1)
                hi, lo = blocks(n)
                act.copy(as_r(hi), lo).then_inc(sem("blocks_high"), 1)

            for n in range(8):
                key = ("kvA", n)
                bank = wait(main, key)
                main.free(act.copy(R[:, R1 + n * 512:R1 + (n + 1) * 512], bank), key)
                if n in (3, 5):
                    blocks_high(n // 2 - 1)
            for n in range(2):
                for t in range(TT):
                    key = ("kvB", n, t)
                    bank = wait(main, key)
                    c0 = R2 + n * D + t * 512
                    main.free(act.copy(R[:, c0:c0 + 512], bank), key)
            for n in range(2):
                bank = wait(main, ("cmp", n))[0:CMP_ROWS, 0:256]
                g = tmp[0:CMP_ROWS, n * 512:n * 512 + 256]
                act.activation(g, bank, ACT.Square).then_inc(sem("gelu_square"), 1)
                act.wait_ge(sem("gelu_in"), n + 1)
                act.activation(g, g, ACT.Tanh, scale=float(np.sqrt(2.0 / np.pi))).then_inc(sem("gelu_tanh"), 1)
            for n in range(8):
                key = ("nq", n)
                bank = wait(main, key)
                main.free(act.activation(R[:, R3 + n * 512:R3 + (n + 1) * 512], bank, ACT.Copy, scale=float(P) ** -0.5), key)
            for t in range(TT):
                key = ("bg", t)
                bank = wait(main, key)
                main.free(act.activation(bgt[:, t * 48:(t + 1) * 48], bank[:, 0:48], ACT.Tanh, scale=0.5), key)
            for b in range(TT):
                act.wait_ge(sem("cmp_shifted"), b + 1)
                cx = xn[:, b * 240:(b + 1) * 240]
                act.activation(cx, cx, ACT.Exp).then_inc(sem("cmp_exp"), 1)
            seq = [("ng", c, t) for c in range(4) for t in range(TT)]
            for kind, i in nsa_order():
                if kind == "S":
                    b, h0, nh = STEPS[i]
                    n_keys = (b + 1) * P
                    for br, name in enumerate(("s", "w")):
                        bank = wait(aux, (name, i))
                        act.wait_ge(sem("nsa_max"), 2 * i + br + 1)
                        for n in range(nh):
                            c0 = R2 + 2048 + i % 2 * 1024 + br * 512 + n * n_keys
                            col = i * 8 + br * nh + n
                            ins = act.activation(R[:, c0:c0 + n_keys], bank[:, n * n_keys:(n + 1) * n_keys], ACT.Exp,
                                                 bias=nmx[:, col:col + 1], accum_out=esum[:, col:col + 1])
                        aux.free(ins, (name, i))
                elif kind == "G":
                    for t in range(TT):
                        k = 2 * i + t
                        gate_tanh(seq[k], seq[k - 2] if k >= 2 else None)
                else:
                    bank = wait(aux, ("wT", i))
                    c0 = i % 2 * 1024 + 512
                    aux.free(act.copy(PTb[:, c0:c0 + 512], bank), ("wT", i))
            high_parts("oT")
            ple(1, 3, lambda t: after_read(main, ("no", 1, t)))

            norm_stats(4, lambda t: act.wait_ge(sem("h_ready"), 7 + t))
            norm_stats(5, lambda t: act.wait_ge(sem("x2_ready"), t + 1))
            high_parts("xT_attn")
            bank = wait(main, "gb")
            main.free(act.activation(SM["beta"], bank[0:4, 0:TM], ACT.Tanh, scale=0.5), "gb")
            act.activation(cst[0:4, 0:1], param("a_log_2", 0, 4), ACT.Exp).then_inc(sem("a_exp"), 1)

            def conv_tanh(jj):
                act.wait_ge(sem("conv_done"), jj + 1)
                if jj >= 2:
                    act.wait_ge(sem("conv_silu"), jj - 1)
                c0 = R2 + GIN_TILES[jj] * TM
                act.activation(tmp[:, jj % 2 * 512:jj % 2 * 512 + TM], R[:, c0:c0 + TM], ACT.Tanh, scale=0.5).then_inc(
                    sem("conv_tanh"), 1)

            for jj in range(12):
                bank = wait(main, ("gin", jj))
                c0 = R1 + GIN_TILES[jj] * RAW_W + 3
                main.free(act.copy(R[:, c0:c0 + TM], bank[:, 0:TM]), ("gin", jj))
                if jj:
                    conv_tanh(jj - 1)
            conv_tanh(11)

            def fox_in(j):
                bank = wait(main, ("fin", j))
                main.free(act.activation(R[:, R3 + j * TM:R3 + (j + 1) * TM], bank[:, 0:TM], ACT.Copy,
                                         scale=float(FD) ** -0.5 if j < 4 else 1.0), ("fin", j))

            for j in range(4):
                fox_in(j)
            act.wait_ge(sem("conv_silu"), 8)
            act.activation(PTb[:, 0:8 * TM], R[:, R2:R2 + 8 * TM], ACT.Square).then_inc(sem("squares"), 1)
            for j in range(4, 8):
                fox_in(j)
            after_read(main, "ff")
            act.activation(SM["la"], SM["ga"], ACT.Abs)
            own.then_wait(act.activation(SM["lf"], SM["ff"], ACT.Abs))
            act.activation(SM["la"], SM["la"], ACT.Exp, scale=-1.0)
            own.then_wait(act.activation(SM["lf"], SM["lf"], ACT.Exp, scale=-1.0))
            act.activation(SM["la"], SM["la"], ACT.Ln, bias=1.0)
            act.activation(SM["lf"], SM["lf"], ACT.Ln, bias=1.0).then_inc(sem("soft_logs"), 1)
            bank = wait(aux, "ss")
            aux.free(act.activation(SM["r8"], bank[0:8, 0:TM], ACT.Sqrt, scale=0.25, bias=eps[0:8, :]), "ss")
            for c in range(3):
                m = CHUNKS[c][1]
                bank = wait(main, ("fv", c))
                c0 = R3 + 8 * TM + c * 512
                main.free(act.copy(R[0:m, c0:c0 + 512], bank[0:m, :]), ("fv", c))
            for t in range(TT):
                if t == 0:
                    act.wait_ge(sem("conv_silu"), 12)
                gate_tanh(("gz", t), None)

            for c, (t0, n) in enumerate(CHUNKS):
                act.wait_ge(sem("log_decays"), c + 1)
                act.activation(e3[0:n, c * 12:(c + 1) * 12], g3[0:n, c * 12:(c + 1) * 12], ACT.Exp).then_inc(
                    sem("decays_small"), 1)
                if c:
                    act.wait_ge(sem("bc_read"), c)
                    if c == 2:
                        act.wait_ge(sem("q_scaled"), 1)
                    aux.free(act.activation(xn[:, 1536:2048], aux.at(("bc", c)), ACT.Exp), ("bc", c))
                act.wait_ge(sem("clamped"), c + 1)
                if c:
                    act.activation(xn[0:n, 1024:1024 + 4 * n], xn[0:n, 1024:1024 + 4 * n], ACT.Exp)
                act.activation(xn[0:n, 512:512 + 4 * n], xn[0:n, 512:512 + 4 * n], ACT.Exp, scale=-1.0).then_inc(
                    sem("decay_ready"), 1)

            for kind, *key in gdn_fox_order():
                if kind == "Lz":
                    lv, c = key
                    n = CHUNKS[c][1]
                    bank = wait(aux, ("z", lv, c))
                    c0 = C_ALL + C_OFF[c]
                    aux.free(act.copy(xT2[0:n, c0:c0 + 4 * n], bank[0:n, 0:4 * n]), ("z", lv, c))
                elif kind == "Fs":
                    hd = key[0]
                    bank = wait(aux, ("fs", hd))
                    act.wait_ge(sem("fox_max"), hd + 1)
                    at_ = 0
                    for b in range(TT):
                        n = M + (b + 1) * P
                        c0 = hd % 2 * 416 + at_
                        ins = act.activation(Pf[:, c0:c0 + n], bank[:, at_:at_ + n], ACT.Exp,
                                             bias=fnm[:, 2 * hd + b:2 * hd + b + 1],
                                             accum_out=fsum[:, 2 * hd + b:2 * hd + b + 1])
                        at_ += n
                    aux.free(ins, ("fs", hd))
                elif kind == "Ft":
                    hd = key[0]
                    bank = wait(aux, ("fT", hd))
                    aux.free(act.copy(PfT[:, hd % 2 * 640:hd % 2 * 640 + 384], bank[:, 0:384]), ("fT", hd))
                elif kind == "Fo":
                    hd = key[0]
                    bank = wait(aux, ("fo", hd))
                    act.wait_ge(sem("fox_recip"), hd + 1)
                    for b in range(TT):
                        c0 = R4 + 1024 + b * D + 512 + hd * FD
                        ins = act.activation(R[:, c0:c0 + FD], bank[:, b * FD:(b + 1) * FD], ACT.Copy,
                                             scale=frs[:, 2 * hd + b:2 * hd + b + 1])
                    aux.free(ins, ("fo", hd))
                elif kind == "W":
                    c = key[0]
                    bank = wait(aux, ("gw", c))
                    aux.free(act.activation(nw[:, (c - 1) * 512:c * 512], bank, ACT.Copy, scale=-1.0), ("gw", c))
                elif kind == "V":
                    c = key[0]
                    n = CHUNKS[c][1]
                    bank = wait(aux, ("vn", c))
                    aux.free(act.copy(R[0:n, R1 + 3584:R1 + 4096], bank[0:n, :]), ("vn", c))
                    if c:
                        bank = wait(aux, ("go", c))
                        if c == 2:
                            act.wait_ge(sem("mix_ready"), 1)
                        act.activation(tmp[:, 0:512], bank, ACT.Square).then_inc(sem("go_square"), 1)
                        act.wait_ge(sem("go_sum"), c)
                        act.activation(gsd[:, 4 * c - 4:4 * c], gss[:, 4 * c - 4:4 * c], ACT.Sqrt, scale=1.0 / P,
                                       bias=eps).then_inc(sem("go_std"), 1)
            high_parts("mT")
            norm_stats(6, lambda t: after_read(main, ("mo", 1, t)))
            high_parts("xT_ffn")

            def hidden_high(n):
                after_read(main, ("fu", n))
                act.copy(as_r(R[:, n * 512:(n + 1) * 512]), R[:, 22 * T + n * 512:22 * T + (n + 1) * 512]).then_inc(
                    sem("hidden_high"), 1)

            for n in range(11):
                gate_tanh(("fg", n), ("fg", n - 2) if n >= 2 else None)
                if n:
                    hidden_high(n - 1)
            hidden_high(10)
            norm_stats(7, lambda t: after_read(main, ("dn", 1, t)))

        @block.vector
        def _(dve):
            own = Marks(dve, "dve_step")

            def low_part(hi, value):
                return dve.tensor_tensor(as_r(value), value, value_of(hi), ALU.subtract)

            def split_low(u):
                dve.wait_ge(sem("units_high"), SPLITS[u])
                low_part(high[:, u % HIGH * UNIT:(u % HIGH + 1) * UNIT],
                         ring[:, u % RING * UNIT:(u % RING + 1) * UNIT]).then_inc(sem("units_low"), 1)

            wait, after_read, split_up_to = split_units(dve, split_low, HIGH - 2)

            def low_parts(name):
                turned_low(dve, name, wait)

            def roots(n):
                dve.wait_ge(sem("std_ready"), n + 1)
                own.then_wait(dve.reciprocal(rstd[:, 2 * n:2 * n + 2], std[:, 2 * n:2 * n + 2]))

            def norm(n):
                roots(n)
                for t in range(TT):
                    dve.tensor_scalar(xnrow(t), hrow(t), rstd[:, 2 * n + t:2 * n + t + 1], None, ALU.mult).then_inc(
                        sem("xn_ready"), 1)

            def add_to_h(keys):
                for key in keys:
                    _, c, t = key
                    bank = wait(main, key)
                    main.free(dve.tensor_tensor(hrow(t, c * 512, 512), hrow(t, c * 512, 512), bank, ALU.add), key)

            gates = [0]

            def gate(key, dst):
                i = gates[0]
                gates[0] += 1
                bank = wait(main, key)
                dve.wait_ge(sem("gate_tanh"), i + 1)
                main.free(dve.scalar_tensor_tensor(dst, tmp[:, i % 2 * 512:i % 2 * 512 + 512], 1.0, bank, ALU.add,
                                                   ALU.mult), key)

            dve.memset(eps, EPS).then_inc(sem("eps_ready"), 1)
            dve.wait_ge(sem("par_in"), 16)
            dve.tensor_scalar(half_gn, par[:, PARAM["ret_gn"]:PARAM["ret_gn"] + 17], 0.5, None, ALU.mult).then_inc(
                sem("half_gn"), 1)
            dve.wait_ge(sem("meta_std"), 1)
            own.then_wait(dve.reciprocal(msum[0:M, 2:3], msum[0:M, 1:2]))
            dve.tensor_scalar(R[0:M, R3:R3 + D], R[0:M, R3:R3 + D], msum[0:M, 2:3], None, ALU.mult).then_inc(
                sem("meta_rows"), 1)
            norm(0)
            bank = wait(aux, "meta")
            for kt in range(KD):
                ins = dve.tensor_scalar(as_r(kt_cols(xT, kt, 0, M)), bank[:, kt * M:(kt + 1) * M],
                                        param("attn_norm_w_2", kt), None, ALU.mult)
            own.then_wait(ins)
            for kt in range(KD):
                ins = dve.scalar_tensor_tensor(as_r(kt_cols(xT2, kt, 0, M)), bank[:, kt * M:(kt + 1) * M],
                                               param("attn_norm_w_2", kt), value_of(kt_cols(xT, kt, 0, M)), ALU.mult,
                                               ALU.subtract)
            aux.free(ins, "meta")
            low_parts("xT_ret")
            split_up_to(1)

            dve.wait_ge(sem("ret_in"), 16)
            cos, sin = R[:, R4 + RT_COS:R4 + RT_COS + T], R[:, R4 + RT_SIN:R4 + RT_SIN + T]
            for n in range(8):
                key = ("rqk", n)
                bank = wait(main, key).rearrange("p (f t) -> p f t", f=2)
                ta, tb = tmp[:, 0:512], tmp[:, 512:1024]
                if n:
                    dve.wait_ge(sem("rotated"), n)
                dve.tensor_tensor(ta.rearrange("p (f t) -> p f t", f=2), bank, over(cos, 2), ALU.mult)
                main.free(dve.tensor_tensor(tb.rearrange("p (f t) -> p f t", f=2), bank, over(sin, 2), ALU.mult), key)
                after_read(main, key)
                c0 = R1 + n * 512
                dve.tensor_tensor(R[:, c0:c0 + T], ta[:, 0:T], tb[:, T:2 * T], ALU.subtract)
                dve.tensor_tensor(R[:, c0 + T:c0 + 2 * T], tb[:, 0:T], ta[:, T:2 * T], ALU.add).then_inc(
                    sem("rotated"), 1)
            for hd in range(RH):
                key = ("rs", hd)
                bank = wait(aux, key)
                decay = R[:, R4 + RT_DECAY + hd * T:R4 + RT_DECAY + (hd + 1) * T]
                dve.tensor_tensor(PTb[:, hd * 384:hd * 384 + T], bank[:, 0:T], decay, ALU.mult)
                aux.free(dve.tensor_tensor(PTb[:, hd * 384 + T:(hd + 1) * 384], bank[:, T:T + P], decay[:, 0:P],
                                           ALU.mult), key)
            for half in range(2):
                for c in (2 * half, 2 * half + 1):
                    for t in range(TT):
                        gate(("rg", c, t), R[:, R3 + t * 2048 + c * 512:R3 + t * 2048 + (c + 1) * 512])
                for i in range(4 * half, 4 * half + 4):
                    bank = wait(aux, ("rpv", i // 2, i % 2))
                    ins = dve.bn_stats(bn[:, i % 4 * 6:(i % 4 + 1) * 6], bank)
                own.then_wait(ins)
                for i in range(4 * half, 4 * half + 4):
                    dve.bn_aggr(mv[:, 2 * i:2 * i + 2], bn[:, i % 4 * 6:(i % 4 + 1) * 6]).then_inc(sem("ret_var"), 1)
                dve.wait_ge(sem("ret_std"), half + 1)
                four = slice(4 * half, 4 * half + 4)
                own.then_wait(dve.reciprocal(rrs[:, four], rsd[:, four]))
                dve.scalar_tensor_tensor(nmr[:, four], mv.rearrange("p (i c) -> p i c", c=2)[:, four, 0], -1.0,
                                         rrs[:, four], ALU.mult, ALU.mult).then_inc(sem("ret_norm"), 1)
            low_parts("yT")
            add_to_h([("ro", c, t) for c in range(2) for t in range(TT)])

            def ple(n, norm_n):
                norm(norm_n)
                low_parts(f"xT_ple{n}")
                after_read(main, ("emb", n, 1, 1))
                for i in range(4):
                    c, t = i // 2, i % 2
                    after_read(main, ("pg", n, c, t))
                    g = tmp[:, i % 2 * 512:i % 2 * 512 + 512]
                    c0 = R2 + t * D + c * 512
                    own.then_wait(dve.scalar_tensor_tensor(g, g, 1.0, R[:, c0:c0 + 512], ALU.add, ALU.mult))
                    dve.tensor_tensor(hrow(t, c * 512, 512), hrow(t, c * 512, 512), g, ALU.add).then_inc(
                        sem("h_ready"), 1)

            ple(0, 1)

            norm(2)
            low_parts("xT_kv")
            for n, name in enumerate(("cmp_pe_k", "cmp_pe_v")):
                after_read(main, ("kvA", 2 * n + 1))
                src = R[:, R1 + n * D:R1 + (n + 1) * D].rearrange("p (g m l) -> p l g m", g=NSA_G, l=CMP_STRIDE)
                for o in range(2):
                    _, lo = blocks(n)
                    dst = lo[:, o * CMP_STRIDE * CMP_ROWS:(o + 1) * CMP_STRIDE * CMP_ROWS].rearrange("p (l g m) -> p l g m", g=NSA_G, m=CMP_N)
                    p0 = PARAM[name] + o * CMP_STRIDE
                    pe_cols = par[:, p0:p0 + CMP_STRIDE].unsqueeze(2).unsqueeze(3).to_broadcast(
                        [P, CMP_STRIDE, NSA_G, CMP_N])
                    ins = dve.tensor_tensor(dst, src[:, :, :, o:o + CMP_N], pe_cols, ALU.add)
                ins.then_inc(sem("blocks_ready"), 1)
            for n in range(2):
                split_up_to(main.unit["kvA", 3 + 2 * n] + 1)
                dve.wait_ge(sem("blocks_high"), n + 1)
                low_part(*blocks(n)).then_inc(sem("blocks_low"), 1)
            dve.wait_ge(sem("gates_high"), 1)
            low_part(gates_high[:, :], side_sb[:, SIDE_G2:SIDE_G2 + KD * 16]).then_inc(sem("gates_low"), 1)
            for n in range(2):
                bank = wait(main, ("cmp", n))[0:CMP_ROWS, 0:256]
                g = tmp[0:CMP_ROWS, n * 512:n * 512 + 256]
                dve.wait_ge(sem("gelu_square"), n + 1)
                own.then_wait(dve.tensor_scalar(g, g, 0.044715, 1.0, ALU.mult, ALU.add))
                dve.tensor_tensor(g, g, bank, ALU.mult).then_inc(sem("gelu_in"), 1)
                dve.wait_ge(sem("gelu_tanh"), n + 1)
                main.free(dve.scalar_tensor_tensor(tmp[0:CMP_ROWS, n * 512 + 256:n * 512 + 512], g, 1.0, bank, ALU.add,
                                                   ALU.mult), ("cmp", n))
            for n in range(2):
                bank = wait(aux, ("hT", n))
                aux.free(dve.tensor_copy(Pf[:, n * 120:(n + 1) * 120], bank[:, 0:120]), ("hT", n))
            bank = wait(aux, ("c2", 0))
            aux.free(dve.tensor_scalar(Pf[:, CMP_K:CMP_K + CMP_ROWS], bank[:, 0:CMP_ROWS], 0.5, None, ALU.mult), ("c2", 0))
            bank = wait(aux, ("c2", 1))
            aux.free(dve.tensor_scalar(Pf[0:CMP_N, CMP_V:CMP_V + 512], bank[0:CMP_N, :], 0.5, None, ALU.mult), ("c2", 1))
            after_read(main, ("bg", 1))
            own.then_wait(dve.tensor_scalar(bgt, bgt, 1.0, 0.5, ALU.add, ALU.mult))

            def heads(ap):
                return ap.rearrange("p (h n) -> p h n", h=NSA_H)

            for b in range(TT):
                cx = xn[:, b * 240:(b + 1) * 240]
                bank = wait(aux, ("cs", b))
                mask = tab[:, TB_CMP + b * CMP_N:TB_CMP + (b + 1) * CMP_N]
                aux.free(dve.tensor_tensor(heads(cx), heads(bank[:, 0:240]), over(mask, NSA_H), ALU.add), ("cs", b))
                after_read(aux, ("cs", b))
                own.then_wait(dve.tensor_reduce(cst[:, b * 16:(b + 1) * 16], heads(cx), AX, ALU.max))
                dve.tensor_tensor(heads(cx), heads(cx), spread(cst[:, b * 16:(b + 1) * 16], CMP_N),
                                  ALU.subtract).then_inc(sem("cmp_shifted"), 1)
            for b in range(TT):
                cx = xn[:, b * 240:(b + 1) * 240]
                cs = cst[:, b * 16:(b + 1) * 16]
                dve.wait_ge(sem("cmp_exp"), b + 1)
                own.then_wait(dve.tensor_reduce(cs, heads(cx), AX, ALU.add))
                own.then_wait(dve.reciprocal(cs, cs))
                own.then_wait(dve.scalar_tensor_tensor(
                    cs, cs, tab[:, TB_ROW + b:TB_ROW + b + 1],
                    bgt[:, b * 48:(b + 1) * 48].rearrange("p (h c) -> p h c", c=3)[:, :, 0], ALU.mult, ALU.mult))
                dve.tensor_tensor(heads(cx), heads(cx), spread(cs, CMP_N), ALU.mult).then_inc(sem("cmp_p"), 1)

            for kind, i in nsa_order():
                if kind == "S":
                    b, h0, nh = STEPS[i]
                    for br, name in enumerate(("s", "w")):
                        bank = wait(aux, (name, i))
                        c0 = i * 8 + br * nh
                        dve.tensor_reduce(nmx[:, c0:c0 + nh], bank.rearrange("p (h n) -> p h n", h=nh), AX, ALU.max,
                                          negate=True).then_inc(sem("nsa_max"), 1)
                    after_read(aux, ("w", i))
                    sc = esc[:, i * 8:i * 8 + 2 * nh]
                    own.then_wait(dve.reciprocal(sc, esum[:, i * 8:i * 8 + 2 * nh]))
                    g = bgt[:, b * 48 + h0 * 3:b * 48 + (h0 + nh) * 3].rearrange("p (n c) -> p c n", c=3)[:, 1:3, :]
                    sc = sc.rearrange("p (c n) -> p c n", c=2)
                    dve.tensor_tensor(sc, sc, g, ALU.mult).then_inc(sem("nsa_scale"), 1)
                elif kind == "G":
                    for t in range(TT):
                        gate(("ng", i, t), R[:, R4 + t * 2048 + i * 512:R4 + t * 2048 + (i + 1) * 512])
                else:
                    b, h0, nh = STEPS[i]
                    slot = i % 2
                    bank = wait(aux, ("sT", i))
                    aux.free(dve.tensor_copy(PTb[:, slot * 1024:slot * 1024 + 512], bank), ("sT", i))
                    bank = wait(aux, ("cT", i))
                    aux.free(dve.tensor_copy(nw[0:CMP_N, slot * 512:slot * 512 + nh * P], bank[0:CMP_N, 0:nh * P]),
                             ("cT", i))
                    bank = wait(aux, ("o", i))
                    after_read(main, ("ng", h0 // NSA_HPG, b))
                    y = R[:, R4 + b * 2048 + h0 * P:R4 + b * 2048 + (h0 + nh) * P]
                    aux.free(dve.tensor_tensor(y, y, bank[:, 0:nh * P], ALU.mult), ("o", i))
            low_parts("oT")
            add_to_h([("no", c, t) for c in range(2) for t in range(TT)])
            ple(1, 3)

            roots(4)
            dve.wait_ge(sem("gain1_in"), 16)
            for t in range(TT):
                dve.scalar_tensor_tensor(hrow(t), hrow(t), rstd[:, 8 + t:9 + t], G1[:, 0:D], ALU.mult,
                                         ALU.mult).then_inc(sem("x2_ready"), 1)
            norm(5)
            low_parts("xT_attn")
            raw = R[:, R1:R1 + 12 * RAW_W].rearrange("p (j t) -> p j t", j=12)
            dve.memset(raw[:, :, 0:3], 0.0)
            own.then_wait(dve.memset(SM["ones"], 1.0))
            for key, rows_, name, bias in (("ga", 4, "ga", "dt_bias_2"), ("ff", 8, "ff", "fgate_b_2")):
                bank = wait(main, key)
                main.free(dve.tensor_scalar(SM[name], bank[0:rows_, 0:TM], param(bias, 0, rows_), None, ALU.add), key)
            after_read(main, "gb")
            dve.tensor_scalar(SM["beta"], SM["beta"], 1.0, 0.5, ALU.add, ALU.mult).then_inc(sem("scans"), 1)

            def conv(jj):
                j = GIN_TILES[jj]
                after_read(main, ("gin", jj))
                y = R[:, R2 + j * TM:R2 + (j + 1) * TM]
                own.then_wait(dve.tensor_scalar(y, raw[:, j, 0:TM], param("conv_w_2", j), None, ALU.mult))
                for k in range(1, 4):
                    ins = dve.scalar_tensor_tensor(y, raw[:, j, k:k + TM], param("conv_w_2", 12 * k + j), y, ALU.mult,
                                                   ALU.add)
                    if k < 3:
                        own.then_wait(ins)
                ins.then_inc(sem("conv_done"), 1)

            def silu(jj):
                j = GIN_TILES[jj]
                y = R[:, R2 + j * TM:R2 + (j + 1) * TM]
                dve.wait_ge(sem("conv_tanh"), jj + 1)
                dve.scalar_tensor_tensor(y, tmp[:, jj % 2 * 512:jj % 2 * 512 + TM], 1.0, y, ALU.add,
                                         ALU.mult).then_inc(sem("conv_silu"), 1)

            for jj in range(12):
                conv(jj)
                if jj:
                    silu(jj - 1)
            silu(11)
            dve.wait_ge(sem("a_exp"), 1)
            own.then_wait(dve.tensor_scalar(cst[0:4, 1:2], cst[0:4, 0:1], -1.0, None, ALU.mult))
            split_up_to(main.unit["fin", 7] + 1)
            dve.wait_ge(sem("soft_logs"), 1)
            dve.scalar_tensor_tensor(SM["la"], SM["ga"], 0.0, SM["la"], ALU.max, ALU.add)
            own.then_wait(dve.scalar_tensor_tensor(SM["lf"], SM["ff"], 0.0, SM["lf"], ALU.min, ALU.subtract))
            own.then_wait(dve.tensor_scalar(SM["la"], SM["la"], cst[0:4, 1:2], None, ALU.mult))
            for t0, n in CHUNKS:
                dve.tensor_tensor_scan(SM["gc"][:, t0:t0 + n], SM["ones"][0:4, 0:n], SM["la"][:, t0:t0 + n], 0.0,
                                       ALU.mult, ALU.add).then_inc(sem("scans"), 1)
            own.then_wait(dve.tensor_tensor_scan(SM["ff"], SM["ones"], SM["lf"], 0.0, ALU.mult, ALU.add))
            dve.tensor_scalar(SM["negc"], SM["ff"], -1.0, None, ALU.mult).then_inc(sem("fox_c"), 1)
            after_read(aux, "ss")
            dve.reciprocal(SM["r8"], SM["r8"]).then_inc(sem("qk_factor"), 1)
            dve.wait_ge(sem("conv_silu"), 12)
            for j in range(8):
                bank = wait(aux, ("rb", j))
                y = R[:, R2 + j * TM:R2 + (j + 1) * TM]
                aux.free(dve.scalar_tensor_tensor(y, y, 0.5 * float(P) ** -0.5 if j < 4 else 0.5, bank[:, 0:TM],
                                                  ALU.mult, ALU.mult), ("rb", j))
            bank = wait(aux, "tok")
            dve.tensor_copy(tk[0:M, 0:8], bank[0:M, 0:8])
            aux.free(dve.tensor_copy(tk[:, 8:24], bank[:, 8:24]), "tok")
            for t in range(TT):
                gate(("gz", t), R[:, R4 + t * 512:R4 + (t + 1) * 512])

            after_read(aux, "tok")
            for c, (t0, n) in enumerate(CHUNKS):
                def four(ap, w=None):
                    return ap.rearrange("p (h n) -> p h n", h=GH)

                gc, beta = tk[0:n, c * 8:c * 8 + 4], tk[0:n, c * 8 + 4:c * 8 + 8]
                d, d1, d2 = (xn[0:n, s * 512:s * 512 + 4 * n] for s in range(3))
                bank = wait(aux, ("bc", c))
                own.then_wait(dve.tensor_copy(g3[:, c * 12 + 8:c * 12 + 12], four(bank[:, 0:4 * n])[:, :, n - 1]))
                ins = dve.tensor_tensor(four(d), four(bank[0:n, 0:4 * n]), spread(gc, n), ALU.subtract)
                if c:
                    ins.then_inc(sem("bc_read"), 1)
                    dve.wait_ge(sem("bc_read"), c)
                else:
                    aux.free(ins, ("bc", c))
                    after_read(aux, ("bc", c))
                dve.tensor_copy(g3[0:n, c * 12:c * 12 + 4], gc)
                dve.tensor_tensor(g3[0:n, c * 12 + 4:c * 12 + 8], g3[0:n, c * 12 + 8:c * 12 + 12], gc,
                                  ALU.subtract).then_inc(sem("log_decays"), 1)
                if c:
                    dve.tensor_tensor(four(d2), four(d), over(tab[0:n, TB_INCL:TB_INCL + n], GH), ALU.min)
                dve.tensor_tensor(four(d1), four(d), over(tab[0:n, TB_STRICT:TB_STRICT + n], GH), ALU.max).then_inc(
                    sem("clamped"), 1)
                dve.wait_ge(sem("decays_small"), c + 1)
                dve.tensor_tensor(be[0:n, c * 4:c * 4 + 4], beta, e3[0:n, c * 12:c * 12 + 4], ALU.mult)
                own.then_wait(dve.tensor_scalar(hb[0:n, c * 4:c * 4 + 4], beta, 0.5, None, ALU.mult))
                dve.wait_ge(sem("decay_ready"), c + 1)
                own.then_wait(dve.tensor_tensor(four(d1), four(d1), spread(beta, n), ALU.mult))
                bank = wait(aux, ("kk", c))
                a0 = 2 * C_ALL + C_OFF[c]
                aux.free(dve.tensor_tensor(PTb[0:n, a0:a0 + 4 * n], d1, bank[0:n, 0:4 * n], ALU.mult), ("kk", c))
                if c:
                    bank = wait(aux, ("qk", c))
                    k0 = R4 + 3072 + (c - 1) * 512
                    aux.free(dve.tensor_tensor(R[:, k0:k0 + 512], d2, bank, ALU.mult), ("qk", c))
                    after_read(aux, ("bc", c))
                    q = R[:, R2:R2 + 12 * TM].rearrange("p (j t) -> p j t", j=12)[:, 0:4, t0:t0 + n]
                    dve.tensor_tensor(q, q, four(xn[:, 1536:2048]), ALU.mult).then_inc(sem("q_scaled"), 1)

                def rows_of(base):
                    buf, b0 = base
                    return four(buf[0:n, b0 + c * 512:b0 + (c + 1) * 512])

                bank = four(wait(aux, ("kt", c))[0:n, :])
                if c < 2:
                    dve.tensor_tensor(rows_of(KDEC), bank, spread(e3[0:n, c * 12 + 4:c * 12 + 8], P), ALU.mult)
                aux.free(dve.tensor_tensor(rows_of(RK), bank, spread(be[0:n, c * 4:c * 4 + 4], P), ALU.mult), ("kt", c))
                bank = four(wait(aux, ("vt", c))[0:n, :])
                aux.free(dve.tensor_tensor(rows_of(RV), bank, spread(hb[0:n, c * 4:c * 4 + 4], P), ALU.mult), ("vt", c))

            state = R[:, R1 + 3072:R1 + 3584]
            for kind, *key in gdn_fox_order():
                if kind == "Lx":
                    lv, c = key
                    n = CHUNKS[c][1]
                    by = wait(aux, ("y", lv, c))
                    if not last_level(lv, c):
                        bx = aux.at(("x", lv, c))
                        X = PTb[0:n, C_OFF[c]:C_OFF[c] + 4 * n]
                        aux.free(dve.tensor_tensor(X, X, bx[0:n, 0:4 * n], ALU.subtract), ("x", lv, c))
                    Y = PTb[0:n, C_ALL + C_OFF[c]:C_ALL + C_OFF[c] + 4 * n]
                    aux.free(dve.tensor_tensor(Y, Y, by[0:n, 0:4 * n], ALU.subtract), ("y", lv, c))
                elif kind == "Fs":
                    hd = key[0]
                    bank = wait(aux, ("fs", hd))
                    dve.tensor_reduce(fnm[:, 2 * hd:2 * hd + 1], bank[:, 0:P + M], AX, ALU.max, negate=True)
                    dve.tensor_reduce(fnm[:, 2 * hd + 1:2 * hd + 2], bank[:, P + M:3 * P + 2 * M], AX, ALU.max,
                                      negate=True).then_inc(sem("fox_max"), 1)
                elif kind == "Ft":
                    hd = key[0]
                    after_read(aux, ("fs", hd))
                    dve.reciprocal(frs[:, 2 * hd:2 * hd + 2], fsum[:, 2 * hd:2 * hd + 2]).then_inc(sem("fox_recip"), 1)
                    bank = wait(aux, ("fm", hd))
                    c0 = hd % 2 * 640 + 384
                    aux.free(dve.tensor_copy(PfT[0:M, c0:c0 + 256], bank[0:M, 0:256]), ("fm", hd))
                elif kind == "V":
                    c = key[0]
                    if c:
                        dve.wait_ge(sem("go_square"), c)
                        s4 = slice(4 * c - 4, 4 * c)
                        dve.tensor_reduce(gss[:, s4], tmp[:, 0:512].rearrange("p (h n) -> p h n", h=GH), AX,
                                          ALU.add).then_inc(sem("go_sum"), 1)
                        dve.wait_ge(sem("go_std"), c)
                        own.then_wait(dve.reciprocal(grs[:, s4], gsd[:, s4]))
                        bank = aux.at(("go", c)).rearrange("p (h n) -> p h n", h=GH)
                        on = tmp[:, 512:1024]
                        aux.free(dve.tensor_tensor(on.rearrange("p (h n) -> p h n", h=GH), bank,
                                                   spread(grs[:, s4], P), ALU.mult), ("go", c))
                        after_read(aux, ("go", c))
                        m0 = R4 + 1024 + (c - 1) * D
                        dve.tensor_tensor(R[:, m0:m0 + 512], on, R[:, R4 + (c - 1) * 512:R4 + c * 512],
                                          ALU.mult).then_inc(sem("mix_ready"), 1)
                    if c < 2:
                        bank = wait(aux, ("st", c))
                        if c == 0:
                            aux.free(dve.tensor_copy(state, bank), ("st", c))
                        else:
                            s3 = state.rearrange("p (h n) -> p h n", h=GH)
                            own.then_wait(dve.tensor_tensor(s3, s3, spread(e3[:, c * 12 + 8:c * 12 + 12], P), ALU.mult))
                            aux.free(dve.tensor_tensor(state, state, bank, ALU.add), ("st", c))
            low_parts("mT")
            add_to_h([("mo", c, t) for c in range(2) for t in range(TT)])
            norm(6)
            low_parts("xT_ffn")

            def hidden_low(n):
                dve.wait_ge(sem("hidden_high"), n + 1)
                low_part(R[:, n * 512:(n + 1) * 512], R[:, 22 * T + n * 512:22 * T + (n + 1) * 512]).then_inc(
                    sem("hidden_low"), 1)

            for n in range(11):
                a = xn[:, n % 2 * 512:n % 2 * 512 + 512]
                gate(("fg", n), a)
                after_read(main, ("fg", n))
                bank = wait(main, ("fu", n))
                product = R[:, 22 * T + n * 512:22 * T + (n + 1) * 512]
                main.free(dve.scalar_tensor_tensor(product, a, 0.5, bank, ALU.mult, ALU.mult), ("fu", n))
                if n:
                    hidden_low(n - 1)
            hidden_low(10)
            add_to_h([("dn", c, t) for c in range(2) for t in range(TT)])
            roots(7)
            dve.wait_ge(sem("gain2_in"), 16)
            for t in range(TT):
                dve.scalar_tensor_tensor(xnrow(t), hrow(t), rstd[:, 14 + t:15 + t], G1[:, D:2 * D], ALU.mult,
                                         ALU.mult).then_inc(sem("out_rows"), 1)

        @block.gpsimd
        def _(pool):
            for i in range(8):
                hd, t = i // 2, i % 2
                wait_read(pool, aux, ("rpv", hd, t))
                wait_read(pool, main, ("rg", hd, t))
                y = R[:, R3 + t * 2048 + hd * 512:R3 + t * 2048 + (hd + 1) * 512]
                pool.tensor_tensor(y, y, xn[:, i % 4 * 512:(i % 4 + 1) * 512], ALU.mult).then_inc(sem("ret_y"), 1)
            for i, (b, h0, nh) in enumerate(STEPS):
                pool.wait_ge(sem("nsa_scale"), i + 1)
                c0 = R2 + 2048 + i % 2 * 1024
                p = R[:, c0:c0 + 1024].rearrange("p (h n) -> p h n", h=2 * nh)
                pool.tensor_tensor(p, p, spread(esc[:, i * 8:i * 8 + 2 * nh], 1024 // (2 * nh)), ALU.mult).then_inc(
                    sem("nsa_p"), 1)
            aux.wait(pool, "ss")
            for c, (t0, n) in enumerate(CHUNKS):
                for base in (0, C_ALL):
                    c0 = base + C_OFF[c]
                    pool.tensor_copy(PTb[0:n, c0:c0 + 4 * n].rearrange("p (h n) -> p h n", h=GH),
                                     over(ident[0:n, 0:n], GH)).then_inc(sem("xy_init"), 1)
            for lv, c in LEVEL_LIST:
                n = CHUNKS[c][1]
                wait_read(pool, aux, ("kk", c))
                main.wait(pool, ("gz", 1))
                if lv:
                    aux.wait(pool, ("z", lv - 1, c))
                a0, m0 = 2 * C_ALL + C_OFF[c], TB_LEVEL + lv * P
                pool.tensor_tensor(xT2[0:n, C_OFF[c]:C_OFF[c] + 4 * n].rearrange("p (h n) -> p h n", h=GH),
                                   PTb[0:n, a0:a0 + 4 * n].rearrange("p (h n) -> p h n", h=GH),
                                   over(tab[0:n, m0:m0 + n], GH), ALU.mult).then_inc(sem("level_part"), 1)


_INS = ["x", "meta", "weights", "side", "params", "tabs", "ret_tabs", "p_t", "gains"]


def kernel(**inputs):
    import numpy as _np
    import concourse.bacc as _bacc
    from concourse import mybir as _mybir
    from concourse.bass_utils import run_bass_kernel_spmd as _run

    a = {k: _np.asarray(v) for k, v in inputs.items()}
    w = {}
    for name in ("ret_w_in", "ret_w_out", "nsa_w_in", "nsa_w_out", "w_in_2", "w_out_2", "w_gate_2", "w_up_2", "w_down_2"):
        w[name] = a[name][0]
    for name in ("kv_w", "cmp_w1_k", "cmp_w1_v"):
        w[name] = a[name]
    for i in range(2):
        w[f"ple_w_gate{i}"], w[f"ple_w_emb{i}"] = a["ple_w_gate"][i], a["ple_w_emb"][i]

    def tiles(m, k0, kt, c0, n):
        return m[k0 * P:(k0 + kt) * P, c0:c0 + n].reshape(kt, P, n).transpose(1, 0, 2).reshape(P, kt * n)

    shape_of = {"A": (8, 256), "B": (4, 512), "E": (2, 1024), "C": (8, 256)}
    weights = _np.empty((NU, P, UNIT), _np.float32)
    for u, (name, kind, k0, c0) in enumerate(UNITS):
        kt, n = shape_of[kind]
        weights[u] = tiles(w[name], k0, kt, c0, n)
    side = _np.concatenate([
        tiles(w["nsa_w_in"], 0, KD, 4096, 48),
        tiles(_np.concatenate([w["w_in_2"][:, 2048:2056], w["w_in_2"][:, 3592:3600]], 1), 0, KD, 0, 16),
        tiles(a["cmp_w2_k"], 0, 2, 0, P), tiles(a["cmp_w2_v"], 0, 2, 0, P)], 1)

    def columns(v):
        return v.reshape(-1, P).T

    def column(v):
        out = _np.zeros((P, 1), _np.float32)
        out[:v.size, 0] = v.reshape(-1)
        return out

    params = _np.concatenate([
        columns(a["ret_norm"][0]), columns(a["kv_norm"]), columns(a["nsa_norm"][0]), columns(a["ple_norm"][0]),
        columns(a["ple_norm"][1]), columns(a["attn_norm_w_2"][0]), columns(a["ffn_norm_w_2"][0]),
        columns(a["ret_gn"][0]), columns(a["gdn_norm_w_2"][0]), a["cmp_pe_k"].T, a["cmp_pe_v"].T,
        columns(a["conv_w_2"][0].reshape(-1)), column(a["a_log_2"]), column(a["dt_bias_2"]), column(a["fgate_b_2"])], 1)
    p_t = _np.concatenate([tiles(_np.ascontiguousarray(a["p"][i, 0].T), 0, 2, 0, T) for i in range(2)], 1)
    tabs, ret_tabs = tables()
    arrays = {
        "x": a["x"][0], "meta": a["meta_tokens_2"], "weights": weights, "side": side, "params": params,
        "tabs": tabs, "ret_tabs": ret_tabs, "p_t": p_t,
        "gains": _np.stack([a["final_norm"], a["final_norm_w_2"]]),
    }
    nc = _bacc.Bacc("TRN2", target_bir_lowering=False, num_devices=1)
    args, feed = [], {}
    for name in _INS:
        feed[f"in_{name}"] = _np.ascontiguousarray(arrays[name])
        args.append(nc.dram_tensor(f"in_{name}", feed[f"in_{name}"].shape, _mybir.dt.from_np(feed[f"in_{name}"].dtype),
                                   kind="ExternalInput").ap())
    args.append(nc.dram_tensor("out_0", (T, D), F32, kind="ExternalOutput").ap())
    two_models_kernel(nc, *args)
    r = _run(nc, [feed], core_ids=[0])
    return r.results[0]["out_0"].reshape(1, T, D)
```

```python
from contextlib import ExitStack

import numpy as np

import concourse.bass as bass
from concourse import mybir

F32 = mybir.dt.float32
F32R = mybir.dt.float32r
BF16 = mybir.dt.bfloat16
ALU = mybir.AluOpType
ACT = mybir.ActivationFunctionType
AX = mybir.AxisListType.X

P = 128
D = 1024
KD = D // P
T = 256
TT = T // P
M = 16
TM = T + M
EPS = 1e-6
NEG = -1e30

RH = 4
NSA_H, NSA_G, NSA_HPG = 16, 4, 4
CMP_L, CMP_STRIDE = 32, 16
CMP_N = (T - CMP_L) // CMP_STRIDE + 1
CMP_ROWS = NSA_G * CMP_N
GH = 4
FH, FD = 8, 64
FF = 2816
CHUNKS = [(0, M), (M, P), (M + P, P)]
LEVELS = [1, 2, 4, 8, 16, 32, 64]

UNIT = 2048
RING = 4
HIGH = 3



def query_order():
    order = []
    for n in range(8):
        order += [("c", n), ("q", n - n // 4)] if n % 4 < 3 else [("c", n)]
    return order + [("q", 6), ("g", 0), ("q", 7)]


def weight_units():
    units = []

    def a(name, c0, n):
        units.extend((name, "A", 0, c0 + 256 * i) for i in range(n // 256))

    def b(name, c0, n, kt=KD):
        for c in range(n // 512):
            units.extend((name, "B", k0, c0 + 512 * c) for k0 in range(0, kt, 4))

    a("ret_w_in", 0, 2048)
    b("ret_w_in", 2048, 4096)
    b("ret_w_out", 0, D, 16)
    units.append(("ple_w_emb0", "E", 0, 0))
    b("ple_w_gate0", 0, D)
    a("kv_w", 0, 1024)
    a("kv_w", 1024, 512)
    a("kv_w", 2048, 512)
    b("kv_w", 1536, 512)
    b("kv_w", 2560, 512)
    for kind, n in query_order():
        if kind == "c":
            units.append(("cmp_w1_v" if n >= 4 else "cmp_w1_k", "C", n % 4 * 8, 0))
        elif kind == "q":
            a("nsa_w_in", 256 * n, 256)
    b("nsa_w_in", 2048, 2048)
    b("nsa_w_out", 0, D, 16)
    units.append(("ple_w_emb1", "E", 0, 0))
    b("ple_w_gate1", 0, D)
    a("w_in_2", 512, 512)
    a("w_in_2", 0, 512)
    a("w_in_2", 1024, 512)
    a("w_in_2", 2056, 1024)
    b("w_in_2", 3080, 512)
    b("w_in_2", 1536, 512)
    units.extend(("w_out_2", "B", k0, c0) for k0 in (4, 0) for c0 in (0, 512))
    for c in range(0, FF, 256):
        units.append(("w_gate_2", "A", 0, c))
        units.append(("w_up_2", "A", 0, c))
    for c in range(2):
        units.extend(("w_down_2", "B", k0, 512 * c) for k0 in range(0, 20, 4))
    units.append(("w_down_2", "E", 20, 0))
    return units


UNITS = weight_units()
NU = len(UNITS)
IS_SPLIT = [not name.startswith("ple_w_emb") for name, *_ in UNITS]
SPLITS = [sum(IS_SPLIT[:u + 1]) for u in range(NU)]

PARAM = {}
_at = 0
for _name, _n in [("ret_norm", 8), ("kv_norm", 8), ("nsa_norm", 8), ("ple_norm0", 8), ("ple_norm1", 8),
                  ("attn_norm_w_2", 8), ("ffn_norm_w_2", 8), ("ret_gn", 16), ("gdn_norm_w_2", 1),
                  ("cmp_pe_k", CMP_L), ("cmp_pe_v", CMP_L), ("conv_w_2", 48), ("a_log_2", 1),
                  ("dt_bias_2", 1), ("fgate_b_2", 1)]:
    PARAM[_name] = _at
    _at += _n
NPARAM = _at
SIDE_BG, SIDE_G2, SIDE_W2K, SIDE_W2V = 0, KD * 48, KD * 64, KD * 64 + 256
NSIDE = KD * 64 + 512
TB_ID, TB_CAUSAL, TB_CMP, TB_ROW, TB_STRICT, TB_INCL, TB_LEVEL = 0, 128, 256, 286, 288, 416, 544
TB_ONE = TB_LEVEL + 128 * len(LEVELS)
NTAB = TB_ONE + 15
RT_COS, RT_SIN, RT_DECAY = 0, 256, 512
NRT = 512 + RH * 256


def tables():
    i = np.arange(P)
    t = np.zeros((P, NTAB), np.float32)
    t[:, TB_ID:TB_ID + P] = np.eye(P)
    t[:, TB_CAUSAL:TB_CAUSAL + P] = np.where(i[None] <= i[:, None], 0.0, NEG)
    end = np.arange(CMP_N) * CMP_STRIDE + CMP_L - 1
    for b in range(TT):
        t[:, TB_CMP + b * CMP_N:TB_CMP + (b + 1) * CMP_N] = np.where(end[None] <= (b * P + i)[:, None], 0.0, NEG)
        t[:, TB_ROW + b] = (b * P + i >= CMP_L - 1)
    t[:, TB_STRICT:TB_STRICT + P] = np.where(i[None] < i[:, None], 0.0, -NEG)
    t[:, TB_INCL:TB_INCL + P] = np.where(i[None] >= i[:, None], 0.0, NEG)
    for n, m in enumerate(LEVELS):
        same = (i[:, None] // (2 * m)) == (i[None] // (2 * m))
        t[:, TB_LEVEL + n * P:TB_LEVEL + (n + 1) * P] = same & (i[:, None] // m % 2 == 1) & (i[None] // m % 2 == 0)
    t[:, TB_ONE + 7] = 1.0
    r = np.zeros((P, NRT), np.float32)
    inv = (np.float32(10000.0) ** (-np.arange(P, dtype=np.float32) / np.float32(P))).astype(np.float32)
    ang = (np.arange(T, dtype=np.float32)[None] * inv[:, None]).astype(np.float32)
    r[:, RT_COS:RT_COS + T] = np.cos(ang)
    r[:, RT_SIN:RT_SIN + T] = np.sin(ang)
    lg = np.log1p(-(2.0 ** (-5.0 - np.arange(RH))))
    diff = (np.arange(T)[None] - i[:, None]).astype(np.float64)
    for h in range(RH):
        r[:, RT_DECAY + h * T:RT_DECAY + (h + 1) * T] = np.where(
            diff >= 0, np.exp(np.maximum(diff, 0) * lg[h]), 0.0) * 256.0 ** -0.5
    return t, r


class Banks:

    def __init__(self, tensor, first, uses, full, freed, begun):
        self.tensor, self.first, self.uses, self.full_sem, self.freed = tensor, first, uses, full, freed
        self.index = {key: n for n, (key, _) in enumerate(uses)}
        assert len(self.index) == len(uses)
        self.rank, counts = [], {}
        for _, engine in uses:
            counts[engine] = counts.get(engine, 0) + 1
            self.rank.append(counts[engine])
        self.filled, self.released = 0, {}
        self.begun = begun
        self.unit = {}

    def at(self, key):
        return self.tensor[:, self.first + self.index[key] % 4, :]

    def open(self, pe, key):
        n = self.index[key] - 4
        if n >= 0:
            pe.wait_ge(self.freed[self.uses[n][1]], self.rank[n])
        return self.at(key)

    def full(self, ins, key):
        self.unit[key] = self.begun[0] - 1
        assert self.index[key] == self.filled, (key, self.uses[self.filled])
        self.filled += 1
        ins.then_inc(self.full_sem, 1)

    def wait(self, engine, key):
        engine.wait_ge(self.full_sem, self.index[key] + 1)
        return self.at(key)

    def free(self, ins, key):
        n = self.index[key]
        engine = self.uses[n][1]
        self.released[engine] = self.released.get(engine, 0) + 1
        assert self.released[engine] == self.rank[n], (key, engine)
        ins.then_inc(self.freed[engine], 1)


STEPS = [(0, 4 * g, 4) for g in range(4)] + [(1, 2 * n, 2) for n in range(8)]
ROOTS = [("norm", 0), "meta", ("ret", 0), ("ret", 1), ("norm", 1), ("norm", 2), ("norm", 3), ("norm", 5),
         ("norm", 4),         ("go", 1), ("go", 2), ("norm", 6), ("norm", 7)]


HALF_STEP = 8


def nsa_order():
    order = [("S", 0), ("S", 1), ("N", 0), ("N", 1), ("C", 0), ("G", 0)]
    for i in range(len(STEPS)):
        order += [("T", i)] + [("G", i + 1)] * (i < 3)
        if i + 2 < len(STEPS):
            order.append(("S", i + 2))
        order.append(("O", i))
        if i == HALF_STEP:
            order.append(("H", 0))
        if i + 2 < len(STEPS):
            order.append(("N", i + 2))
    return order


def main_uses():
    u = [(("rqk", n), "dve") for n in range(8)]
    u += [(("rv", c, t), "act") for c in range(4) for t in range(TT)]
    u += [(("rg", c, t), "dve") for c in range(4) for t in range(TT)]
    u += [(("ro", c, t), "dve") for c in range(2) for t in range(TT)]

    def ple(n):
        return [(("emb", n, c, t), "act") for c in range(2) for t in range(TT)] + \
               [(("pg", n, c, t), "act") for c in range(2) for t in range(TT)]

    u += ple(0)
    u += [(("kvA", n), "act") for n in range(8)]
    u += [(("kvB", n, t), "act") for n in range(2) for t in range(TT)]
    for n in range(8):
        u += [(("bg", n - 4), "act")] * (n in (4, 5)) + [(("nq", n), "act")]
    for kind, i in nsa_order():
        if kind == "S":
            u += [(("s", i), "act"), (("w", i), "act")]
        elif kind == "G":
            u += [(("ng", i, t), "dve") for t in range(TT)]
    u += [(("no", c, t), "dve") for c in range(2) for t in range(TT)]
    u += ple(1)
    u += [("gb", "act"), ("ga", "dve"), ("ff", "dve")]
    u += [(("gin", j), "act") for j in range(12)]
    u += [(("fin", j), "act") for j in range(8)]
    u += [(("fv", c), "act") for c in range(3)]
    u += [(("gz", t), "dve") for t in range(TT)]
    u += [(("mo", c, t), "dve") for c in range(2) for t in range(TT)]
    for n in range(11):
        u += [(("fg", n), "dve"), (("fu", n), "dve")]
    u += [(("dn", c, t), "dve") for c in range(2) for t in range(TT)]
    return u


def tr_uses(name, first, n=4):
    return [((name, f), "dve") for f in range(first, first + n)]


def aux_uses():
    u = tr_uses("xT_ret", 0) + [("meta", "dve")]
    u += [(("rs", h), "dve") for h in range(RH)]
    for h in range(RH):
        u += [(("rpv", h, t), "act") for t in range(TT)]
    u += tr_uses("yT0", 0) + tr_uses("yT1", 4)
    u += tr_uses("xT_ple0", 0)
    u += tr_uses("xT_kv", 0)
    u += [(("cmp", n), "dve") for n in range(2)]
    u += [(("hT", n), "dve") for n in range(2)] + [(("c2", n), "dve") for n in range(2)]
    for kind, i in nsa_order():
        if kind == "C":
            u += [(("cs", b), "dve") for b in range(TT)]
        elif kind == "T":
            u += [(("sT", i), "dve"), (("wT", i), "act"), (("cT", i), "dve")]
        elif kind == "O":
            u += [(("o", i), "dve")]
        elif kind == "H":
            u += tr_uses("oT0", 0)
    u += tr_uses("oT1", 4)
    u += tr_uses("xT_ple1", 0)
    u += tr_uses("xT_attn", 0)
    u += [("ss", "dve")] + [(("rb", j), "dve") for j in range(8)]
    u += [("tok", "dve")]
    for c in range(3):
        u += [(("bc", c), "act" if c else "dve"), (("kk", c), "dve")]
        if c:
            u += [(("qk", c), "dve")]
        u += [(("kt", c), "dve"), (("vt", c), "dve")]
    u += gdn_fox_uses()
    u += tr_uses("mT0", 0, 2)
    u += tr_uses("xT_ffn", 0)
    return u


def level_chunks(n):
    return [c for c in (1, 2, 0) if 2 * LEVELS[n] <= CHUNKS[c][1]]


def last_level(n, c):
    return 2 * LEVELS[n] == CHUNKS[c][1]


def gdn_fox_order():
    order = [("Fs", 0)]
    for n in range(len(LEVELS)):
        order += [("Lz", n, c) for c in level_chunks(n)] + [("Ft", n)]
        order += [("Lx", n, c) for c in level_chunks(n)] + [("Fo", n), ("Fs", n + 1)]
    order += [("W", 1), ("W", 2), ("V", 0), ("Ft", 7), ("V", 1), ("Fo", 7), ("H", 0), ("V", 2)]
    return order


def gdn_fox_uses():
    u = []
    for kind, *at in gdn_fox_order():
        n = at[0]
        if kind == "Lz":
            u += [(("z", *at), "act")]
        elif kind == "Lx":
            u += ([] if last_level(*at) else [(("x", *at), "dve")]) + [(("y", *at), "dve")]
        elif kind == "Fs":
            u += [(("fs", n), "act")]
        elif kind == "Ft":
            u += [(("fT", n), "act"), (("fm", n), "dve")]
        elif kind == "Fo":
            u += [(("fo", n), "act")]
        elif kind == "W":
            u += [(("gw", n), "act")]
        elif kind == "H":
            u += tr_uses("mT1", 2, 2)
        else:
            u += [(("vn", n), "act")] + [(("go", n), "act")] * (n > 0) + [(("st", n), "dve")] * (n < 2)
    return u


R1, R2, R3, R4 = 0, 4096, 8192, 12288
GIN_TILES = [4, 5, 6, 7, 0, 1, 2, 3, 8, 9, 10, 11]
RAW_W = TM + 3
C_OFF = [0, 4 * M, 4 * M + 4 * P]
C_ALL = 4 * M + 8 * P
CMP_K, CMP_V = 4 * CMP_ROWS, 5 * CMP_ROWS
LEVEL_LIST = [(n, c) for n in range(len(LEVELS)) for c in level_chunks(n)]


def two_models_kernel(nc, x, meta, weights, side, params, tabs, ret_tabs, p_t, gains, out):
    ctx = ExitStack()
    with ctx:
        one_pass = {}

        def sb(name, cols, parts=False):
            buf = ctx.enter_context(nc.sbuf_tensor(name, [P, cols], F32))
            if parts:
                one_pass[buf.name] = nc.alloc_sbuf_tensor_at(f"{name}_parts", [P, cols], F32R,
                                                             offset=nc.sbuf_base - 4 * cols)
            return buf

        def as_r(ap):
            return bass.AP(tensor=one_pass[ap.tensor.name], offset=ap.offset, ap=ap.ap)

        def value_of(ap):
            return as_r(ap).bitcast(F32)

        sems = {}

        def sem(name):
            if name not in sems:
                sems[name] = ctx.enter_context(nc.semaphore(name))
            return sems[name]

        ring = sb("ring", RING * UNIT, True)
        high = sb("high", HIGH * UNIT, True)
        gates_high = sb("gates_high", KD * 16, True)
        side_sb = sb("side_sb", NSIDE, True)
        tab = sb("tab", NTAB)
        par = sb("par", NPARAM)
        h = sb("h", TT * D)
        xn = sb("xn", TT * D, True)
        xT = sb("xT", KD * TM, True)
        xT2 = sb("xT2", KD * TM, True)
        R = sb("R", 4 * 4096, True)
        PTb = sb("PTb", 4096, True)
        G1 = sb("G1", 2 * D)
        tmp = sb("tmp", 1024)
        diag = sb("diag", TT * P)
        nw = sb("nw", 1024)
        Pf = sb("Pf", 832)
        PfT = sb("PfT", 1280)
        small = sb("small", 544)
        psum = ctx.enter_context(nc.psum_tensor("psum", [P, 8, 512], F32))

        freed = {e: sem(f"main_read_by_{e}") for e in ("act", "dve")}
        begun = [0]
        main = Banks(psum, 0, main_uses(), sem("main_filled"), freed, begun)
        freed = {e: sem(f"aux_read_by_{e}") for e in ("act", "dve")}
        aux = Banks(psum, 4, aux_uses(), sem("aux_filled"), freed, begun)

        at = [0]

        def cols(n):
            at[0] += n
            assert at[0] <= 544
            return small[:, at[0] - n:at[0]]

        sums = cols(32)
        rstd = cols(16)
        var = cols(2)
        power = cols(1)
        msum = cols(3)
        bn, mv, rrs, nmr = cols(24), cols(16), cols(8), cols(8)
        half_gn = cols(17)
        bgt = cols(96)
        nmx, esum, esc = cols(96), cols(96), cols(96)
        tk, g3, e3, be = nmx[:, 0:24], nmx[:, 24:60], esum[:, 0:36], esum[:, 36:48]
        hb, fnm, fsum, frs = esum[:, 48:60], esc[:, 0:16], esc[:, 16:32], esc[:, 32:48]
        gss, grs = esc[:, 48:56], esc[:, 64:72]
        cst = cols(32)

        ident = tab[:, TB_ID:TB_ID + P]
        ident_b = ctx.enter_context(nc.sbuf_tensor("ident_b", [P, P], BF16))[:, :]
        causal_b = ctx.enter_context(nc.sbuf_tensor("causal_b", [P, P], BF16))[:, :]

        def param(name, n=0, rows=P):
            return par[0:rows, PARAM[name] + n:PARAM[name] + n + 1]

        def hrow(t, c=0, n=D):
            return h[:, t * D + c:t * D + c + n]

        def xnrow(t):
            return xn[:, t * D:(t + 1) * D]

        def spread(ap, inner):
            return ap.unsqueeze(2).to_broadcast([ap.shape[0], ap.shape[1], inner])

        def over(ap, outer):
            return ap.unsqueeze(1).to_broadcast([ap.shape[0], outer, ap.shape[1]])

        def kt_cols(buf, kt, c0, n, width=TM, base=0):
            return buf[:, base + kt * width + c0:base + kt * width + c0 + n]

        def into_x(kt):
            return kt_cols(xT, kt, M, T), kt_cols(xT2, kt, M, T)

        def into_kv(kt):
            return kt_cols(xT, kt, M, T), R[:, R4 + kt * T:R4 + (kt + 1) * T]

        def into_nsa(kt):
            return kt_cols(xT2, kt, M, T), PTb[:, 2048 + kt * T:2048 + (kt + 1) * T]

        def into_out(kt):
            return R[:, R1 + kt * T:R1 + (kt + 1) * T], R[:, R2 + kt * T:R2 + (kt + 1) * T]

        def into_out1(kt):
            return R[:, R1 + kt * T:R1 + (kt + 1) * T], R[:, R3 + kt * T:R3 + (kt + 1) * T]

        class Marks:

            def __init__(self, engine, name):
                self.engine, self.sem, self.n = engine, sem(name), 0

            def then_wait(self, ins):
                self.n += 1
                ins.then_inc(self.sem, 1)
                self.engine.wait_ge(self.sem, self.n)

        def wait_read(engine, banks, key):
            n = banks.index[key]
            engine.wait_ge(banks.freed[banks.uses[n][1]], banks.rank[n])

        turns = []

        def turned(name, banks, *readers):
            for place, gain in readers:
                for f in banks:
                    turns.append(((name, f), [(kt, place(kt), gain(kt)) for kt in (2 * f, 2 * f + 1)],
                                  place is readers[-1][0]))

        def gain_of(name):
            return lambda kt: param(name, kt)

        turned("xT_ret", range(4), (into_x, gain_of("ret_norm")))
        for half in range(2):
            turned(f"yT{half}", range(4 * half, 4 * half + 4), (into_out, lambda kt: half_gn[:, kt:kt + 1]))
        turned("xT_ple0", range(4), (into_x, gain_of("ple_norm0")))
        turned("xT_kv", range(4), (into_kv, gain_of("kv_norm")), (into_nsa, gain_of("nsa_norm")))
        for half in range(2):
            turned(f"oT{half}", range(4 * half, 4 * half + 4), (into_out1, lambda kt: 0.5))
        turned("xT_ple1", range(4), (into_x, gain_of("ple_norm1")))
        turned("xT_attn", range(4), (into_x, gain_of("attn_norm_w_2")))
        turned("mT1", (2, 3), (into_x, lambda kt: 1.0))
        turned("mT0", (0, 1), (into_x, lambda kt: half_gn[:, 16:17]))
        turned("xT_ffn", range(4), (into_x, gain_of("ffn_norm_w_2")))

        def turned_high(act, name, wait):
            for key, parts, frees in turns:
                if key[0] == name:
                    bank = wait(aux, key)
                    if name == "xT_kv" and frees:
                        act.wait_ge(sem("kv_low"), key[1] + 1)
                    for n, (kt, (hi, _), g) in enumerate(parts):
                        ins = act.activation(as_r(hi), bank[:, n * T:(n + 1) * T], ACT.Copy, scale=g)
                    ins.then_inc(sem("turned_high"), 1)

        def turned_low(dve, name, wait):
            for n_turn, (key, parts, frees) in enumerate(turns):
                if key[0] == name:
                    bank = wait(aux, key)
                    dve.wait_ge(sem("turned_high"), n_turn + 1)
                    for n, (kt, (hi, lo), g) in enumerate(parts):
                        ins = dve.scalar_tensor_tensor(as_r(lo), bank[:, n * T:(n + 1) * T], g, value_of(hi),
                                                       ALU.mult,
                                                       ALU.subtract)
                    if frees:
                        aux.free(ins, key)
                    else:
                        ins.then_inc(sem("kv_low"), 1)

        def split_units(engine, split, ahead):
            done = [0]

            def up_to(u):
                while done[0] <= min(u, NU - 1):
                    if IS_SPLIT[done[0]]:
                        split(done[0])
                    done[0] += 1

            def wait(banks, key):
                up_to(banks.unit[key] + ahead)
                return banks.wait(engine, key)

            def after_read(banks, key):
                up_to(banks.unit[key] + ahead)
                wait_read(engine, banks, key)

            return wait, after_read, up_to

        def blocks(n):
            size = CMP_L * CMP_ROWS
            hi = R[:, R2 + 2048:R2 + 2048 + size] if n == 0 else R[:, R1:R1 + size]
            return hi, (R[:, R4 + 2048:R4 + 2048 + size] if n == 0 else xn[:, 0:size])

        def hidden(k, part):
            return R[:, (part * 22 + k) * T:(part * 22 + k + 1) * T]

        RV, RK, KDEC = (R, R1), (R, R1 + 1536), (G1, 0)
        SM = {}
        for n, (name, rows) in enumerate([("ga", 4), ("la", 4), ("gc", 4), ("beta", 4), ("ff", 8), ("lf", 8), ("ones", 8)]):
            SM[name] = R[0:rows, R4 + 1024 + n * TM:R4 + 1024 + (n + 1) * TM]
        SM["negc"] = R[0:8, R3 + 8 * TM + 1536:R3 + 9 * TM + 1536]
        SM["r8"] = xn[0:8, 0:TM]

        block = ctx.enter_context(nc.Block())

        @block.sync
        def _(sp):
            def load(name, dst, src):
                sp.dma_start(dst, src).then_inc(sem(name), 16)

            for t in range(TT):
                load(f"x_in{t}", hrow(t), x[t * P:(t + 1) * P, :])
            load("ident_in", ident, tabs[:, TB_ID:TB_ID + P])
            load("par_in", par[:, :], params)

            def unit(slot, src):
                sp.dma_start(ring[:, slot * UNIT:(slot + 1) * UNIT], src).then_inc(sem(f"unit_in{slot}"), 16)

            for u in range(2):
                unit(u, weights[u])
            load("ret_in", R[:, R4:R4 + NRT], ret_tabs)
            for u in range(2, RING):
                unit(u, weights[u])
            load("meta_in", R[0:M, R3:R3 + D], meta)
            load("tab_in", tab[:, P:NTAB], tabs[:, P:NTAB])
            load("pT_in", G1[:, D:2 * D], p_t)
            load("side_in", side_sb[:, :], side)
            load("gain1_in", G1[:, 0:D], gains[0:1, :].to_broadcast([P, D]))
            rounds = weights[0:NU // RING * RING].rearrange("(g r) p c -> g r p c", r=RING)
            swiglu = UNITS.index(("w_gate_2", "A", 0, 0)) // RING

            def stream(first, end):
                with sp.Fori(first, end) as g:
                    for slot in range(RING):
                        sp.wait_ge(sem("units_used"), g * RING + (slot - RING + 1))
                        unit(slot, rounds[g, slot])

            stream(1, swiglu)
            main.wait(sp, ("emb", 1, 1, 1))
            load("gain2_in", G1[:, D:2 * D], gains[1:2, :].to_broadcast([P, D]))
            stream(swiglu, NU // RING)
            for u in range(NU // RING * RING, NU):
                sp.wait_ge(sem("units_used"), u - RING + 1)
                unit(u % RING, weights[u])
            for t in range(TT):
                sp.wait_ge(sem("out_rows"), t + 1)
                sp.dma_start(out[t * P:(t + 1) * P, :], xnrow(t)).then_inc(sem("stored"), 16)
            sp.wait_ge(sem("stored"), 16 * TT)

        @block.tensor
        def _(pe):
            narrow = []

            def mm(out, lhsT, rhs, first, last):
                return pe.matmul(out, lhsT, rhs, start=first, stop=last, skip_group_check=True)

            def parts3(product, out, lhsT, rhs, first, last):
                product(out, as_r(lhsT[0]), as_r(rhs[0]), first, False)
                if narrow:
                    narrow.pop(0)()
                product(out, as_r(lhsT[1]), as_r(rhs[0]), False, False)
                if narrow:
                    narrow.pop(0)()
                return product(out, as_r(lhsT[0]), as_r(rhs[1]), False, last)

            def next_unit(k):
                u = begun[0]
                begun[0] += 1
                if IS_SPLIT[u]:
                    pe.wait_ge(sem("units_low"), SPLITS[u])
                else:
                    pe.wait_ge(sem(f"unit_in{u % RING}"), 16 * (u // RING + 1))
                first = [u > 0]

                def product(*args):
                    ins = mm(*args)
                    if first[0]:
                        ins.then_inc(sem("units_used"), 1)
                    first[0] = False
                    return ins

                low = ring[:, u % RING * UNIT:(u % RING + 1) * UNIT].rearrange("p (k c) -> p k c", k=k)
                hi = high[:, u % HIGH * UNIT:(u % HIGH + 1) * UNIT].rearrange("p (k c) -> p k c", k=k)
                return lambda i, c: (hi[:, i, c], low[:, i, c]), product

            def project_a(keys, src, c0, n):
                w, product = next_unit(KD)
                for f in range(2):
                    key = keys[f * (len(keys) - 1)]
                    base = f * n if len(keys) == 1 else 0
                    if f == 0 or len(keys) == 2:
                        bank = main.open(pe, key)
                    for k in range(KD):
                        x_k = src(k, c0, n)
                        ins = parts3(product, bank[:, base:base + n], w(k, slice(f * P, (f + 1) * P)), x_k,
                                     k == 0, k == KD - 1)
                    if f == 1 or len(keys) == 2:
                        main.full(ins, key)

            def project_b(keys, src, rows, kt, ready=None):
                banks = [main.open(pe, key) for key in keys]
                for k0 in range(0, kt, 4):
                    if ready:
                        ready(k0)
                    w, product = next_unit(4)
                    for n, bank in enumerate(banks):
                        c0, m = rows[n]
                        for k in range(4):
                            x_k = src(k0 + k, c0, m)
                            ins = parts3(product, bank[0:m, :], x_k, w(k, slice(0, 512)), k0 + k == 0,
                                         k0 + k == kt - 1)
                        if k0 + 4 == kt:
                            main.full(ins, keys[n])

            def turn(name, f, src):
                bank = aux.open(pe, (name, f))
                for k in range(2):
                    for t in range(TT):
                        ins = pe.transpose(bank[:, k * T + t * P:k * T + (t + 1) * P], src(2 * f + k, t), ident)
                aux.full(ins, (name, f))

            def turn_norm(name, n, src=h):
                for f in range(4):
                    bank = aux.open(pe, (name, f))
                    for k in range(2):
                        for t in range(TT):
                            if f + k == 0:
                                pe.wait_ge(sem("diag_ready"), 2 * n + t + 1)
                            c0 = t * D + (2 * f + k) * P
                            ins = mm(bank[:, k * T + t * P:k * T + (t + 1) * P], src[:, c0:c0 + P],
                                     diag[:, t * P:(t + 1) * P], True, True)
                    aux.full(ins, (name, f))

            pending = {}

            def need(place, name, n):
                for f in range(n):
                    pending[place, f] = name

            def tile_ready(place, k):
                name = pending.pop((place, k // 2), None)
                if name and place == "kv":
                    pe.wait_ge(sem("kv_low"), k // 2 + 1)
                elif name:
                    wait_read(pe, aux, (name, k // 2))

            def source(place, into):
                def tile_of(k, c0, n):
                    tile_ready(place, k)
                    return tuple(part[:, c0:c0 + n] for part in into(k))
                return tile_of

            def x_src(k, c0, n):
                tile_ready("x", k)
                return kt_cols(xT, k, c0, n), kt_cols(xT2, k, c0, n)

            kv_src = source("kv", into_kv)
            nsa_src = source("nsa", into_nsa)
            out_src = source("out", into_out)
            out1_src = source("out", into_out1)

            rows = [(M, P), (M + P, P)]
            rows0 = [(0, P), (P, P)]

            turn_norm("xT_ret", 0)
            need("x", "xT_ret", 4)
            for n in range(8):
                project_a([("rqk", n)], x_src, M, T)
            pe.wait_ge(sem("meta_rows"), 1)
            bank = aux.open(pe, "meta")
            for kt in range(KD):
                ins = pe.transpose(bank[:, kt * M:(kt + 1) * M], R[0:M, R3 + kt * P:R3 + (kt + 1) * P], ident[0:M, 0:M])
            aux.full(ins, "meta")
            project_b([("rv", 0, t) for t in range(TT)], x_src, rows, KD)

            def qk_tile(which, hd, half, c0, n):
                return kt_cols(R, which * 8 + hd * 2 + half, c0, n, T, R1)

            pe.wait_ge(sem("rotated"), 8)
            for hd in range(RH):
                bank = aux.open(pe, ("rs", hd))
                for half in range(2):
                    mm(bank[:, 0:T], qk_tile(1, hd, half, 0, P), qk_tile(0, hd, half, 0, T), half == 0, half == 1)
                for half in range(2):
                    ins = mm(bank[:, T:T + P], qk_tile(1, hd, half, P, P), qk_tile(0, hd, half, P, P),
                             half == 0, half == 1)
                aux.full(ins, ("rs", hd))
            for c in range(1, 4):
                project_b([("rv", c, t) for t in range(TT)], x_src, rows, KD)

            def retention_values(hd):
                wait_read(pe, aux, ("rs", hd))
                for t in range(TT):
                    wait_read(pe, main, ("rv", hd, t))
                st = PTb[:, hd * 384:(hd + 1) * 384]
                v0 = R[:, R2 + hd * 512:R2 + (hd + 1) * 512]
                v1 = R[:, R2 + 2048 + hd * 512:R2 + 2048 + (hd + 1) * 512]
                bank = aux.open(pe, ("rpv", hd, 0))
                aux.full(mm(bank, st[:, 0:P], v0, True, True), ("rpv", hd, 0))
                bank = aux.open(pe, ("rpv", hd, 1))
                mm(bank, st[:, P:T], v0, True, False)
                aux.full(mm(bank, st[:, T:T + P], v1, False, True), ("rpv", hd, 1))

            def turn_half(name, half, base):
                for f in range(4 * half, 4 * half + 4):
                    turn(f"{name}{half}", f, lambda kt, t: R[:, base + t * 2048 + kt * P:base + t * 2048 + (kt + 1) * P])
                    pending["out", f] = f"{name}{half}"

            for half in range(2):
                for hd in (2 * half, 2 * half + 1):
                    retention_values(hd)
                for c in (2 * half, 2 * half + 1):
                    project_b([("rg", c, t) for t in range(TT)], x_src, rows, KD)
                    if c == 2:
                        pe.wait_ge(sem("ret_y"), 4)
                        turn_half("yT", 0, R3)

            def last_half(name, base, wait_rows):
                def ready(k0):
                    if k0 == 8:
                        wait_rows()
                        turn_half(name, 1, base)
                return ready

            project_b([("ro", 0, t) for t in range(TT)], out_src, rows0, 16,
                      last_half("yT", R3, lambda: pe.wait_ge(sem("ret_y"), 8)))
            project_b([("ro", 1, t) for t in range(TT)], out_src, rows0, 16)

            def ple(n, norm):
                pe.wait_ge(sem("pT_in"), 16)
                w, product = next_unit(2)
                for c in range(2):
                    for t in range(TT):
                        bank = main.open(pe, ("emb", n, c, t))
                        for k in range(2):
                            c0 = D + (n * 2 + k) * T + t * P
                            _, w_k = w(k, slice(c * 512, (c + 1) * 512))
                            ins = product(bank, G1[:, c0:c0 + P], w_k, k == 0, k == 1)
                        main.full(ins, ("emb", n, c, t))
                turn_norm(f"xT_ple{n}", norm)
                need("x", f"xT_ple{n}", 4)
                for c in range(2):
                    project_b([("pg", n, c, t) for t in range(TT)], x_src, rows, KD)

            ple(0, 1)

            turn_norm("xT_kv", 2)
            need("kv", "xT_kv", 4)
            need("nsa", "xT_kv", 4)
            for n in range(8):
                project_a([("kvA", n)], kv_src, 0, T)
            for n in range(2):
                project_b([("kvB", n, t) for t in range(TT)], kv_src, rows0, KD)
            def first_layer(n, quarter):
                if quarter == 0:
                    pe.wait_ge(sem("blocks_low"), n + 1)
                    bank = aux.open(pe, ("cmp", n))
                bank = aux.at(("cmp", n))
                w, product = next_unit(8)
                hi, lo = blocks(n)
                for k in range(8):
                    place = quarter * 8 + k
                    at_ = slice(place * CMP_ROWS, (place + 1) * CMP_ROWS)
                    ins = parts3(product, bank[0:CMP_ROWS, 0:256], (hi[:, at_], lo[:, at_]), w(k, slice(0, 256)),
                                 place == 0, place == CMP_L - 1)
                if quarter == 3:
                    aux.full(ins, ("cmp", n))

            def second_layer():
                pe.wait_ge(sem("side_in"), 16)
                for n in range(2):
                    wait_read(pe, aux, ("cmp", n))
                    bank = aux.open(pe, ("hT", n))
                    for k in range(2):
                        c0 = n * 512 + 256 + k * P
                        ins = pe.transpose(bank[:, k * CMP_ROWS:(k + 1) * CMP_ROWS], tmp[0:CMP_ROWS, c0:c0 + P],
                                           ident[0:CMP_ROWS, 0:CMP_ROWS])
                    aux.full(ins, ("hT", n))
                wait_read(pe, aux, ("hT", 0))
                bank = aux.open(pe, ("c2", 0))
                for k in range(2):
                    ins = mm(bank[:, 0:CMP_ROWS], side_sb[:, SIDE_W2K + k * P:SIDE_W2K + (k + 1) * P],
                             Pf[:, k * CMP_ROWS:(k + 1) * CMP_ROWS], k == 0, k == 1)
                aux.full(ins, ("c2", 0))
                wait_read(pe, aux, ("hT", 1))
                bank = aux.open(pe, ("c2", 1))
                for g in range(NSA_G):
                    for k in range(2):
                        c0 = 2 * CMP_ROWS + k * CMP_ROWS + g * CMP_N
                        ins = mm(bank[0:CMP_N, g * P:(g + 1) * P], Pf[:, c0:c0 + CMP_N],
                                 side_sb[:, SIDE_W2V + k * P:SIDE_W2V + (k + 1) * P], k == 0, k == 1)
                aux.full(ins, ("c2", 1))
            def branch_gates(t):
                bank = main.open(pe, ("bg", t))
                for k in range(KD):
                    for part in range(2):
                        def product(k=k, part=part):
                            ins = mm(bank[:, 0:48], value_of(nsa_src(k, *rows0[t])[part]),
                                     side_sb[:, SIDE_BG + k * 48:SIDE_BG + (k + 1) * 48],
                                     k + part == 0, part == 1 and k == KD - 1)
                            if part == 1 and k == KD - 1:
                                main.full(ins, ("bg", t))
                        narrow.append(product)

            for kind, n in query_order():
                if kind == "c":
                    first_layer(n // 4, n % 4)
                elif kind == "q":
                    if n in (4, 5):
                        branch_gates(n - 4)
                    project_a([("nq", n)], nsa_src, 0, T)
                else:
                    second_layer()

            def q_tile(hd, b):
                return kt_cols(R, hd, b * P, P, T, R3)

            def nsa_compressed():
                wait_read(pe, aux, ("c2", 1))
                for b in range(TT):
                    bank = aux.open(pe, ("cs", b))
                    for hd in range(NSA_H):
                        def score(b=b, hd=hd, bank=bank):
                            c0 = CMP_K + hd // NSA_HPG * CMP_N
                            ins = mm(bank[:, hd * CMP_N:(hd + 1) * CMP_N], q_tile(hd, b), Pf[:, c0:c0 + CMP_N],
                                     True, True)
                            if hd == NSA_H - 1:
                                aux.full(ins, ("cs", b))
                        narrow.append(score)

            wait_read(pe, main, ("kvB", 1, 1))
            wait_read(pe, main, ("nq", 7))
            pe.wait_ge(sem("masks"), 1)

            def nsa_scores(i):
                b, h0, nh = STEPS[i]
                kt = b + 1
                for key, base in ((("s", i), R1 + 2048), (("w", i), R1 + 3072)):
                    bank = main.open(pe, key)
                    for n in range(nh):
                        k0 = base + (h0 + n) // NSA_HPG * T
                        c0 = n * kt * P
                        mm(bank[:, c0:c0 + kt * P], q_tile(h0 + n, b), R[:, k0:k0 + kt * P], True, False)
                        ins = mm(bank[:, c0 + b * P:c0 + kt * P], ident_b, causal_b, False, True)
                    main.full(ins, key)

            def nsa_turn(i):
                b, h0, nh = STEPS[i]
                kt = b + 1
                slot = i % 2
                pe.wait_ge(sem("nsa_p"), i + 1)
                for key, base in ((("sT", i), 0), (("wT", i), 512)):
                    bank = aux.open(pe, key)
                    for n in range(4):
                        c0 = R2 + 2048 + slot * 1024 + base + n * P
                        ins = pe.transpose(bank[:, n * P:(n + 1) * P], R[:, c0:c0 + P], ident)
                    aux.full(ins, key)
                pe.wait_ge(sem("cmp_p"), b + 1)
                bank = aux.open(pe, ("cT", i))
                for n in range(nh):
                    c0 = b * 240 + (h0 + n) * CMP_N
                    ins = pe.transpose(bank[0:CMP_N, n * P:(n + 1) * P], xn[:, c0:c0 + CMP_N], ident)
                aux.full(ins, ("cT", i))

            def nsa_values(i):
                b, h0, nh = STEPS[i]
                kt = b + 1
                slot = i % 2
                bank = aux.open(pe, ("o", i))
                for key in ("sT", "wT", "cT"):
                    wait_read(pe, aux, (key, i))
                for n in range(nh):
                    g = (h0 + n) // NSA_HPG
                    o = bank[:, n * P:(n + 1) * P]
                    mm(o, nw[0:CMP_N, slot * 512 + n * P:slot * 512 + (n + 1) * P],
                       Pf[0:CMP_N, CMP_V + g * P:CMP_V + (g + 1) * P], True, False)
                    for br in range(2):
                        for k in range(kt):
                            c0 = slot * 1024 + br * 512 + (n * kt + k) * P
                            v0 = R2 + br * 1024 + k * 512 + g * P
                            ins = mm(o, PTb[:, c0:c0 + P], R[:, v0:v0 + P], False, br == 1 and k == kt - 1)
                aux.full(ins, ("o", i))

            for kind, i in nsa_order():
                if kind == "S":
                    nsa_scores(i)
                elif kind == "C":
                    nsa_compressed()
                elif kind == "G":
                    project_b([("ng", i, t) for t in range(TT)], nsa_src, rows0, KD)
                    assert not narrow
                elif kind == "T":
                    nsa_turn(i)
                elif kind == "O":
                    nsa_values(i)
                elif kind == "H":
                    wait_read(pe, aux, ("o", HALF_STEP - 1))
                    turn_half("oT", 0, R4)
            project_b([("no", 0, t) for t in range(TT)], out1_src, rows0, 16,
                      last_half("oT", R4, lambda: wait_read(pe, aux, ("o", len(STEPS) - 1))))
            project_b([("no", 1, t) for t in range(TT)], out1_src, rows0, 16)
            ple(1, 3)

            turn_norm("xT_attn", 4, xn)
            need("x", "xT_attn", 4)
            wait_read(pe, aux, "meta")
            pe.wait_ge(sem("gates_low"), 1)
            for key, c0, n in (("gb", 0, 4), ("ga", 4, 4), ("ff", 8, 8)):
                bank = main.open(pe, key)
                for k in range(KD):
                    w0 = k * 16 + c0
                    w_k = gates_high[:, w0:w0 + n], side_sb[:, SIDE_G2 + w0:SIDE_G2 + w0 + n]
                    ins = parts3(mm, bank[0:n, 0:TM], w_k, x_src(k, 0, TM), k == 0, k == KD - 1)
                main.full(ins, key)
            for u in range(6):
                project_a([("gin", 2 * u), ("gin", 2 * u + 1)], x_src, 0, TM)
            for u in range(4):
                project_a([("fin", 2 * u), ("fin", 2 * u + 1)], x_src, 0, TM)

            def ch(j, c0, n):
                return kt_cols(R, j, c0, n, TM, R2)

            pe.wait_ge(sem("squares"), 1)
            bank = aux.open(pe, "ss")
            for j in range(8):
                ins = mm(bank[0:8, 0:TM], tab[:, TB_ONE + 7 - j:TB_ONE + 15 - j], PTb[:, j * TM:(j + 1) * TM],
                         j == 0, j == 7)
            aux.full(ins, "ss")
            project_b([("fv", c) for c in range(3)], x_src, [(0, M)] + rows, KD)
            pe.wait_ge(sem("qk_factor"), 1)
            for j in range(8):
                bank = aux.open(pe, ("rb", j))
                aux.full(mm(bank[:, 0:TM], ident[0:8, j:j + 1].to_broadcast([8, P]), SM["r8"], True, True), ("rb", j))
            pe.wait_ge(sem("scans"), 4)
            bank = aux.open(pe, "tok")
            for c, (t0, n) in enumerate(CHUNKS):
                for i, src in enumerate(("gc", "beta")):
                    ins = pe.transpose(bank[0:n, c * 8 + i * 4:c * 8 + i * 4 + 4], SM[src][:, t0:t0 + n],
                                       ident[0:4, 0:4])
            aux.full(ins, "tok")
            project_b([("gz", t) for t in range(TT)], x_src, rows, KD)

            wait_read(pe, aux, ("rb", 7))
            pe.wait_ge(sem("conv_silu"), 12)
            for c, (t0, n) in enumerate(CHUNKS):
                bank = aux.open(pe, ("bc", c))
                for hd in range(GH):
                    ins = mm(bank[:, hd * n:(hd + 1) * n], ident[0:4, hd:hd + 1].to_broadcast([4, P]),
                             SM["gc"][:, t0:t0 + n], True, True)
                aux.full(ins, ("bc", c))
                bank = aux.open(pe, ("kk", c))
                for hd in range(GH):
                    ins = mm(bank[0:n, hd * n:(hd + 1) * n], ch(4 + hd, t0, n), ch(4 + hd, t0, n), True, True)
                aux.full(ins, ("kk", c))
                if c:
                    bank = aux.open(pe, ("qk", c))
                    for hd in range(GH):
                        ins = mm(bank[0:n, hd * n:(hd + 1) * n], ch(4 + hd, t0, n), ch(hd, t0, n), True, True)
                    aux.full(ins, ("qk", c))
                for key, j0 in (("kt", 4), ("vt", 8)):
                    bank = aux.open(pe, (key, c))
                    for hd in range(GH):
                        ins = pe.transpose(bank[0:n, hd * P:(hd + 1) * P], ch(j0 + hd, t0, n), ident)
                    aux.full(ins, (key, c))

            def mat(buf, base, c, hd):
                n = CHUNKS[c][1]
                return buf[0:n, base + C_OFF[c] + hd * n:base + C_OFF[c] + (hd + 1) * n]

            def chunk_rows(base, c, hd):
                buf, b0 = base
                return buf[0:CHUNKS[c][1], b0 + c * 512 + hd * P:b0 + c * 512 + (hd + 1) * P]

            def fox_scores(hd):
                bank = aux.open(pe, ("fs", hd))
                p0, c0 = hd % 2 * FD, hd // 2 * TM
                at_ = 0
                for b in range(TT):
                    n = M + (b + 1) * P
                    o = bank[:, at_:at_ + n]
                    q0 = R3 + c0 + M + b * P
                    mm(o, R[p0:p0 + FD, q0:q0 + P], R[p0:p0 + FD, R3 + 4 * TM + c0:R3 + 4 * TM + c0 + n], True, False)
                    mm(o, ident[0:8, hd:hd + 1].to_broadcast([8, P]), SM["negc"][:, 0:n], False, False)
                    ins = mm(bank[:, at_ + n - P:at_ + n], ident_b, causal_b, False, True)
                    at_ += n
                aux.full(ins, ("fs", hd))

            def fox_turn(hd):
                p = Pf[:, hd % 2 * 416:hd % 2 * 416 + 416]
                wait_read(pe, aux, ("fs", hd))
                bank = aux.open(pe, ("fT", hd))
                for n, c0 in enumerate((M, P + 2 * M, 2 * P + 2 * M)):
                    ins = pe.transpose(bank[:, n * P:(n + 1) * P], p[:, c0:c0 + P], ident)
                aux.full(ins, ("fT", hd))
                bank = aux.open(pe, ("fm", hd))
                for n, c0 in enumerate((0, P + M)):
                    ins = pe.transpose(bank[0:M, n * P:(n + 1) * P], p[:, c0:c0 + M], ident)
                aux.full(ins, ("fm", hd))

            def fox_values(hd):
                wait_read(pe, aux, ("fT", hd))
                wait_read(pe, aux, ("fm", hd))
                slot = hd % 2 * 640
                bank = aux.open(pe, ("fo", hd))

                def v(c, m):
                    v0 = R3 + 8 * TM + c * 512 + hd * FD
                    return R[0:m, v0:v0 + FD]

                for b in range(TT):
                    o = bank[:, b * FD:(b + 1) * FD]
                    mm(o, PfT[0:M, slot + 384 + b * P:slot + 384 + (b + 1) * P], v(0, M), True, False)
                    for k in range(b + 1):
                        ins = mm(o, PfT[:, slot + (b + k) * P:slot + (b + k + 1) * P], v(1 + k, P), False, k == b)
                aux.full(ins, ("fo", hd))

            state, v_new = R1 + 3072, R1 + 3584
            pe.wait_ge(sem("fox_c"), 1)
            wait_read(pe, main, ("fv", 2))
            pe.wait_ge(sem("xy_init"), 6)
            def turn_mix(half):
                for f in (2 * half, 2 * half + 1):
                    turn(f"mT{half}", f, lambda kt, t: R[:, R4 + 1024 + t * D + kt * P:R4 + 1024 + t * D + (kt + 1) * P])
                    pending["x", f] = f"mT{half}"

            for kind, *key in gdn_fox_order():
                if kind == "H":
                    wait_read(pe, aux, ("fo", FH - 1))
                    turn_mix(1)
                elif kind == "Fs":
                    fox_scores(key[0])
                elif kind == "Ft":
                    fox_turn(key[0])
                elif kind == "Fo":
                    fox_values(key[0])
                elif kind == "Lz":
                    lv, c = key
                    pe.wait_ge(sem("level_part"), LEVEL_LIST.index((lv, c)) + 1)
                    if lv:
                        wait_read(pe, aux, ("y", lv - 1, c))
                    n = CHUNKS[c][1]
                    bank = aux.open(pe, ("z", lv, c))
                    for hd in range(GH):
                        ins = mm(bank[0:n, hd * n:(hd + 1) * n], mat(xT2, 0, c, hd), mat(PTb, C_ALL, c, hd), True, True)
                    aux.full(ins, ("z", lv, c))
                elif kind == "Lx":
                    lv, c = key
                    wait_read(pe, aux, ("z", lv, c))
                    n = CHUNKS[c][1]
                    if not last_level(lv, c):
                        bank = aux.open(pe, ("x", lv, c))
                        for hd in range(GH):
                            ins = mm(bank[0:n, hd * n:(hd + 1) * n], mat(xT2, C_ALL, c, hd), mat(PTb, 0, c, hd),
                                     True, True)
                        aux.full(ins, ("x", lv, c))
                    bank = aux.open(pe, ("y", lv, c))
                    for hd in range(GH):
                        ins = mm(bank[0:n, hd * n:(hd + 1) * n], mat(PTb, 0, c, hd), mat(xT2, C_ALL, c, hd), True, True)
                    aux.full(ins, ("y", lv, c))
                elif kind == "W":
                    c = key[0]
                    wait_read(pe, aux, ("y", len(LEVELS) - 1, c))
                    bank = aux.open(pe, ("gw", c))
                    for hd in range(GH):
                        ins = mm(bank[:, hd * P:(hd + 1) * P], chunk_rows(RK, c, hd), mat(PTb, C_ALL, c, hd), True, True)
                    aux.full(ins, ("gw", c))
                else:
                    c = key[0]
                    t0, n = CHUNKS[c]
                    if c:
                        wait_read(pe, aux, ("st", c - 1))
                        wait_read(pe, aux, ("gw", c))
                    else:
                        wait_read(pe, aux, ("y", 3, 0))
                    bank = aux.open(pe, ("vn", c))
                    for hd in range(GH):
                        o = bank[0:n, hd * P:(hd + 1) * P]
                        ins = mm(o, mat(PTb, C_ALL, c, hd), chunk_rows(RV, c, hd), True, c == 0)
                        if c:
                            w0 = (c - 1) * 512 + hd * P
                            ins = mm(o, nw[:, w0:w0 + P], R[:, state + hd * P:state + (hd + 1) * P], False, True)
                    aux.full(ins, ("vn", c))
                    wait_read(pe, aux, ("vn", c))
                    if c:
                        bank = aux.open(pe, ("go", c))
                        for hd in range(GH):
                            o = bank[:, hd * P:(hd + 1) * P]
                            mm(o, ch(hd, t0, n), R[:, state + hd * P:state + (hd + 1) * P], True, False)
                            k0 = R4 + 3072 + (c - 1) * 512 + hd * P
                            ins = mm(o, R[:, k0:k0 + P], R[:, v_new + hd * P:v_new + (hd + 1) * P], False, True)
                        aux.full(ins, ("go", c))
                    if c < 2:
                        bank = aux.open(pe, ("st", c))
                        for hd in range(GH):
                            ins = mm(bank[:, hd * P:(hd + 1) * P], chunk_rows(KDEC, c, hd),
                                     R[0:n, v_new + hd * P:v_new + (hd + 1) * P], True, True)
                        aux.full(ins, ("st", c))

            banks = {(c, t): main.open(pe, ("mo", c, t)) for c in range(2) for t in range(TT)}
            for half in (1, 0):
                if half == 0:
                    pe.wait_ge(sem("mix_ready"), 2)
                    turn_mix(0)
                for c in range(2):
                    w, product = next_unit(4)
                    for t in range(TT):
                        for k in range(4):
                            ins = parts3(product, banks[c, t], x_src(4 * half + k, *rows[t]), w(k, slice(0, 512)),
                                         half == 1 and k == 0, half == 0 and k == 3)
                        if half == 0:
                            main.full(ins, ("mo", c, t))
            turn_norm("xT_ffn", 5)
            need("x", "xT_ffn", 4)
            for n in range(11):
                project_a([("fg", n)], x_src, M, T)
                project_a([("fu", n)], x_src, M, T)

            def hidden_src(k, t):
                return tuple(hidden(k, part)[:, t * P:(t + 1) * P] for part in range(2))

            banks = {(c, t): main.open(pe, ("dn", c, t)) for c in range(2) for t in range(TT)}
            for c in range(2):
                for k0 in range(0, 20, 4):
                    if c == 0:
                        pe.wait_ge(sem("hidden_low"), k0 // 2 + 2)
                    w, product = next_unit(4)
                    for t in range(TT):
                        for k in range(4):
                            parts3(product, banks[c, t], hidden_src(k0 + k, t), w(k, slice(0, 512)), k0 + k == 0, False)
            pe.wait_ge(sem("hidden_low"), 11)
            w, product = next_unit(2)
            for c in range(2):
                for t in range(TT):
                    for k in range(2):
                        ins = parts3(product, banks[c, t], hidden_src(20 + k, t), w(k, slice(c * 512, (c + 1) * 512)),
                                     False, k == 1)
                    main.full(ins, ("dn", c, t))
            assert begun[0] == NU

        @block.scalar
        def _(act):
            own = Marks(act, "act_step")

            def split_high(u):
                act.wait_ge(sem(f"unit_in{u % RING}"), 16 * (u // RING + 1))
                if u >= HIGH:
                    act.wait_ge(sem("units_used"), u - HIGH + 1)
                act.copy(as_r(high[:, u % HIGH * UNIT:(u % HIGH + 1) * UNIT]),
                         ring[:, u % RING * UNIT:(u % RING + 1) * UNIT]).then_inc(sem("units_high"), 1)

            wait, after_read, split_up_to = split_units(act, split_high, HIGH - 1)

            def square(n, c, t, src, trash):
                part = slice(t * D + c * 512, t * D + (c + 1) * 512)
                ins = act.activation(trash[:, part], src[:, part], ACT.Square, scale=float(D) ** -0.5,
                                     accum_out=sums[:, 4 * n + 2 * c + t:4 * n + 2 * c + t + 1])
                if c + t == 2:
                    ins.then_inc(sem("norm_sums"), 1)

            def norm_stats(n, wait_rows):
                for c in range(2):
                    for t in range(TT):
                        wait_rows(c, t)
                        square(n, c, t, h, xn)

            def high_parts(name):
                turned_high(act, name, wait)

            gates = [0]

            def gate_tanh(key, before):
                i = gates[0]
                gates[0] += 1
                bank = wait(main, key)
                if before:
                    after_read(main, before)
                act.activation(tmp[:, i % 2 * 512:i % 2 * 512 + 512], bank, ACT.Tanh, scale=0.5).then_inc(
                    sem("gate_tanh"), 1)

            norm_stats(0, lambda c, t: act.wait_ge(sem(f"x_in{t}"), 16))
            act.wait_ge(sem("par_in"), 16)
            split_up_to(1)
            high_parts("xT_ret")
            act.wait_ge(sem("meta_in"), 16)
            act.activation(xn[0:M, 0:D], R[0:M, R3:R3 + D], ACT.Square, scale=float(D) ** -0.5,
                           accum_out=msum[0:M, 0:1]).then_inc(sem("meta_sum"), 1)
            for c in range(4):
                for t in range(TT):
                    key = ("rv", c, t)
                    bank = wait(main, key)
                    main.free(act.copy(R[:, R2 + t * 2048 + c * 512:R2 + t * 2048 + (c + 1) * 512], bank), key)
            act.wait_ge(sem("rotated"), 8)
            seq = [("rg", c, t) for c in range(4) for t in range(TT)]
            act.wait_ge(sem("half_gn"), 1)
            for half in range(2):
                wait(aux, ("rpv", 2 * half + 1, 1))
                act.wait_ge(sem("ret_norm"), half + 1)
                for i in range(4 * half, 4 * half + 4):
                    key = ("rpv", i // 2, i % 2)
                    bank = wait(aux, key)
                    if i >= 4:
                        act.wait_ge(sem("ret_y"), i - 3)
                    aux.free(act.activation(xn[:, i % 4 * 512:(i % 4 + 1) * 512], bank, ACT.Identity,
                                            scale=rrs[:, i:i + 1], bias=nmr[:, i:i + 1]), key)
                for i in range(4 * half, 4 * half + 4):
                    gate_tanh(seq[i], seq[i - 2] if i >= 2 else None)
                    if i == 5:
                        high_parts("yT0")
            high_parts("yT1")

            def ple(n, norm, wait_rows):
                norm_stats(norm, wait_rows)
                for c in range(2):
                    for t in range(TT):
                        key = ("emb", n, c, t)
                        bank = wait(main, key)
                        c0 = R2 + t * D + c * 512
                        main.free(act.activation(R[:, c0:c0 + 512], bank, ACT.Copy, scale=0.5), key)
                high_parts(f"xT_ple{n}")
                for i in range(4):
                    key = ("pg", n, i // 2, i % 2)
                    bank = wait(main, key)
                    if i >= 2:
                        act.wait_ge(sem("h_ready"), 4 * n + i - 1)
                    main.free(act.activation(tmp[:, i % 2 * 512:i % 2 * 512 + 512], bank, ACT.Tanh, scale=0.5), key)

            ple(0, 1, lambda c, t: after_read(main, ("ro", c, t)))

            act.wait_ge(sem("side_in"), 16)
            act.copy(as_r(gates_high[:, :]), side_sb[:, SIDE_G2:SIDE_G2 + KD * 16]).then_inc(sem("gates_high"), 1)

            norm_stats(2, lambda c, t: act.wait_ge(sem("h_ready"), 2 * c + t + 1))
            high_parts("xT_kv")

            def blocks_high(n):
                act.wait_ge(sem("blocks_ready"), n + 1)
                hi, lo = blocks(n)
                act.copy(as_r(hi), lo).then_inc(sem("blocks_high"), 1)

            for n in range(8):
                key = ("kvA", n)
                bank = wait(main, key)
                main.free(act.copy(R[:, R1 + n * 512:R1 + (n + 1) * 512], bank), key)
                if n in (5, 7):
                    blocks_high(n // 2 - 2)
            for n in range(2):
                for t in range(TT):
                    key = ("kvB", n, t)
                    bank = wait(main, key)
                    c0 = R2 + n * D + t * 512
                    main.free(act.copy(R[:, c0:c0 + 512], bank), key)
            def gelu(n):
                bank = wait(aux, ("cmp", n))[0:CMP_ROWS, 0:256]
                g = tmp[0:CMP_ROWS, n * 512:n * 512 + 256]
                act.activation(g, bank, ACT.Square).then_inc(sem("gelu_square"), 1)
                act.wait_ge(sem("gelu_in"), n + 1)
                act.activation(g, g, ACT.Tanh, scale=float(np.sqrt(2.0 / np.pi))).then_inc(sem("gelu_tanh"), 1)

            for n in range(8):
                if n in (3, 6):
                    gelu(n // 3 - 1)
                if n in (4, 5):
                    key = ("bg", n - 4)
                    bank = wait(main, key)
                    main.free(act.activation(bgt[:, (n - 4) * 48:(n - 3) * 48], bank[:, 0:48], ACT.Tanh, scale=0.5), key)
                key = ("nq", n)
                bank = wait(main, key)
                main.free(act.activation(R[:, R3 + n * 512:R3 + (n + 1) * 512], bank, ACT.Copy, scale=float(P) ** -0.5), key)
            seq = [("ng", c, t) for c in range(4) for t in range(TT)]
            for kind, i in nsa_order():
                if kind == "S":
                    b, h0, nh = STEPS[i]
                    n_keys = (b + 1) * P
                    for br, name in enumerate(("s", "w")):
                        bank = wait(main, (name, i))
                        act.wait_ge(sem("nsa_max"), 2 * i + br + 1)
                        for n in range(nh):
                            c0 = R2 + 2048 + i % 2 * 1024 + br * 512 + n * n_keys
                            col = i * 8 + br * nh + n
                            ins = act.activation(R[:, c0:c0 + n_keys], bank[:, n * n_keys:(n + 1) * n_keys], ACT.Exp,
                                                 bias=nmx[:, col:col + 1], accum_out=esum[:, col:col + 1])
                        main.free(ins, (name, i))
                elif kind == "H":
                    high_parts("oT0")
                elif kind == "C":
                    for b in range(TT):
                        after_read(aux, ("cs", b))
                        act.wait_ge(sem("cmp_shifted"), b + 1)
                        cx = xn[:, b * 240:(b + 1) * 240]
                        act.activation(cx, cx, ACT.Exp).then_inc(sem("cmp_exp"), 1)
                elif kind == "G":
                    for t in range(TT):
                        k = 2 * i + t
                        gate_tanh(seq[k], seq[k - 2] if k >= 2 else None)
                elif kind == "T":
                    bank = wait(aux, ("wT", i))
                    c0 = i % 2 * 1024 + 512
                    aux.free(act.copy(PTb[:, c0:c0 + 512], bank), ("wT", i))
            high_parts("oT1")
            ple(1, 3, lambda c, t: after_read(main, ("no", c, t)))

            for c in range(2):
                for t in range(TT):
                    act.wait_ge(sem("h_ready"), 4 + 2 * c + t + 1)
                    square(4, c, t, h, R[:, R4:R4 + TT * D])
                    act.wait_ge(sem("gained"), 2 * c + t + 1)
                    square(5, c, t, xn, R[:, R3:R3 + TT * D])
            high_parts("xT_attn")
            bank = wait(main, "gb")
            main.free(act.activation(SM["beta"], bank[0:4, 0:TM], ACT.Tanh, scale=0.5), "gb")
            act.activation(cst[0:4, 0:1], param("a_log_2", 0, 4), ACT.Exp).then_inc(sem("a_exp"), 1)

            def conv_tanh(jj):
                act.wait_ge(sem("conv_done"), jj + 1)
                if jj >= 2:
                    act.wait_ge(sem("conv_silu"), jj - 1)
                c0 = R2 + GIN_TILES[jj] * TM
                act.activation(tmp[:, jj % 2 * 512:jj % 2 * 512 + TM], R[:, c0:c0 + TM], ACT.Tanh, scale=0.5).then_inc(
                    sem("conv_tanh"), 1)

            for jj in range(12):
                bank = wait(main, ("gin", jj))
                c0 = R1 + GIN_TILES[jj] * RAW_W + 3
                act.copy(R[:, c0:c0 + TM], bank[:, 0:TM])
                j = GIN_TILES[jj]
                main.free(act.activation(R[:, R2 + j * TM:R2 + (j + 1) * TM], bank[:, 0:TM], ACT.Copy,
                                         scale=param("conv_w_2", 36 + j)), ("gin", jj))
                if jj:
                    conv_tanh(jj - 1)
            conv_tanh(11)

            def fox_in(j):
                bank = wait(main, ("fin", j))
                main.free(act.activation(R[:, R3 + j * TM:R3 + (j + 1) * TM], bank[:, 0:TM], ACT.Copy,
                                         scale=float(FD) ** -0.5 if j < 4 else 1.0), ("fin", j))

            for j in range(4):
                fox_in(j)
            act.wait_ge(sem("conv_silu"), 8)
            act.activation(PTb[:, 0:8 * TM], R[:, R2:R2 + 8 * TM], ACT.Square).then_inc(sem("squares"), 1)
            for j in range(4, 8):
                fox_in(j)
            after_read(main, "ff")
            act.activation(SM["la"], SM["ga"], ACT.Abs)
            own.then_wait(act.activation(SM["lf"], SM["ff"], ACT.Abs))
            act.activation(SM["la"], SM["la"], ACT.Exp, scale=-1.0)
            own.then_wait(act.activation(SM["lf"], SM["lf"], ACT.Exp, scale=-1.0))
            act.activation(SM["la"], SM["la"], ACT.Ln, bias=1.0)
            act.activation(SM["lf"], SM["lf"], ACT.Ln, bias=1.0).then_inc(sem("soft_logs"), 1)
            after_read(aux, "ss")
            act.activation(SM["r8"], SM["r8"], ACT.Sqrt).then_inc(sem("qk_root"), 1)
            for c in range(3):
                m = CHUNKS[c][1]
                bank = wait(main, ("fv", c))
                c0 = R3 + 8 * TM + c * 512
                main.free(act.copy(R[0:m, c0:c0 + 512], bank[0:m, :]), ("fv", c))
            for t in range(TT):
                if t == 0:
                    act.wait_ge(sem("conv_silu"), 12)
                gate_tanh(("gz", t), None)

            for c, (t0, n) in enumerate(CHUNKS):
                act.wait_ge(sem("log_decays"), c + 1)
                act.activation(e3[0:n, c * 12:(c + 1) * 12], g3[0:n, c * 12:(c + 1) * 12], ACT.Exp).then_inc(
                    sem("decays_small"), 1)
                if c:
                    act.wait_ge(sem("bc_read"), c)
                    if c == 2:
                        act.wait_ge(sem("q_scaled"), 1)
                    aux.free(act.activation(xn[:, 1536:2048], aux.at(("bc", c)), ACT.Exp), ("bc", c))
                act.wait_ge(sem("clamped"), c + 1)
                if c:
                    act.activation(xn[0:n, 1024:1024 + 4 * n], xn[0:n, 1024:1024 + 4 * n], ACT.Exp)
                act.activation(xn[0:n, 512:512 + 4 * n], xn[0:n, 512:512 + 4 * n], ACT.Exp, scale=-1.0).then_inc(
                    sem("decay_ready"), 1)

            for kind, *key in gdn_fox_order():
                if kind == "H":
                    high_parts("mT1")
                elif kind == "Lz":
                    lv, c = key
                    n = CHUNKS[c][1]
                    bank = wait(aux, ("z", lv, c))
                    c0 = C_ALL + C_OFF[c]
                    aux.free(act.copy(xT2[0:n, c0:c0 + 4 * n], bank[0:n, 0:4 * n]), ("z", lv, c))
                elif kind == "Fs":
                    hd = key[0]
                    bank = wait(aux, ("fs", hd))
                    act.wait_ge(sem("fox_max"), hd + 1)
                    at_ = 0
                    for b in range(TT):
                        n = M + (b + 1) * P
                        c0 = hd % 2 * 416 + at_
                        ins = act.activation(Pf[:, c0:c0 + n], bank[:, at_:at_ + n], ACT.Exp,
                                             bias=fnm[:, 2 * hd + b:2 * hd + b + 1],
                                             accum_out=fsum[:, 2 * hd + b:2 * hd + b + 1])
                        at_ += n
                    aux.free(ins, ("fs", hd))
                elif kind == "Ft":
                    hd = key[0]
                    bank = wait(aux, ("fT", hd))
                    aux.free(act.copy(PfT[:, hd % 2 * 640:hd % 2 * 640 + 384], bank[:, 0:384]), ("fT", hd))
                elif kind == "Fo":
                    hd = key[0]
                    bank = wait(aux, ("fo", hd))
                    act.wait_ge(sem("fox_recip"), hd + 1)
                    for b in range(TT):
                        c0 = R4 + 1024 + b * D + 512 + hd * FD
                        ins = act.activation(R[:, c0:c0 + FD], bank[:, b * FD:(b + 1) * FD], ACT.Copy,
                                             scale=frs[:, 2 * hd + b:2 * hd + b + 1])
                    aux.free(ins, ("fo", hd))
                elif kind == "W":
                    c = key[0]
                    bank = wait(aux, ("gw", c))
                    aux.free(act.activation(nw[:, (c - 1) * 512:c * 512], bank, ACT.Copy, scale=-1.0), ("gw", c))
                elif kind == "V":
                    c = key[0]
                    n = CHUNKS[c][1]
                    bank = wait(aux, ("vn", c))
                    aux.free(act.copy(R[0:n, R1 + 3584:R1 + 4096], bank[0:n, :]), ("vn", c))
                    if c:
                        bank = wait(aux, ("go", c))
                        if c == 2:
                            act.wait_ge(sem("mix_ready"), 1)
                        aux.free(act.copy(tmp[:, 512:1024], bank), ("go", c))
                        after_read(aux, ("go", c))
                        act.activation(tmp[:, 0:512], tmp[:, 512:1024], ACT.Square).then_inc(sem("go_square"), 1)
            high_parts("mT0")
            norm_stats(6, lambda c, t: after_read(main, ("mo", c, t)))
            high_parts("xT_ffn")

            def hidden_high(n):
                after_read(main, ("fu", n))
                act.copy(as_r(R[:, n * 512:(n + 1) * 512]), R[:, 22 * T + n * 512:22 * T + (n + 1) * 512]).then_inc(
                    sem("hidden_high"), 1)

            for n in range(11):
                gate_tanh(("fg", n), ("fg", n - 2) if n >= 2 else None)
                if n:
                    hidden_high(n - 1)
            hidden_high(10)
            norm_stats(7, lambda c, t: after_read(main, ("dn", c, t)))

        @block.vector
        def _(dve):
            own = Marks(dve, "dve_step")

            def low_part(hi, value):
                return dve.tensor_tensor(as_r(value), value, value_of(hi), ALU.subtract)

            def split_low(u):
                dve.wait_ge(sem("units_high"), SPLITS[u])
                low_part(high[:, u % HIGH * UNIT:(u % HIGH + 1) * UNIT],
                         ring[:, u % RING * UNIT:(u % RING + 1) * UNIT]).then_inc(sem("units_low"), 1)

            wait, after_read, split_up_to = split_units(dve, split_low, HIGH - 1)

            def low_parts(name):
                turned_low(dve, name, wait)

            def roots(n):
                dve.wait_ge(sem("roots"), ROOTS.index(("norm", n)) + 1)

            def inverse_roots(name, ins):
                ins.then_inc(sem("root_in"), 1)
                dve.wait_ge(sem("roots"), ROOTS.index(name) + 1)

            def to_diagonal(n):
                for t in range(TT):
                    dve.tensor_scalar(diag[:, t * P:(t + 1) * P], ident, rstd[:, 2 * n + t:2 * n + t + 1], None,
                                      ALU.mult).then_inc(sem("diag_ready"), 1)

            def norm(n):
                roots(n)
                to_diagonal(n)

            def add_to_h(keys):
                for key in keys:
                    _, c, t = key
                    bank = wait(main, key)
                    main.free(dve.tensor_tensor(hrow(t, c * 512, 512), hrow(t, c * 512, 512), bank, ALU.add), key)

            gates = [0]

            def gate(key, dst):
                i = gates[0]
                gates[0] += 1
                bank = wait(main, key)
                dve.wait_ge(sem("gate_tanh"), i + 1)
                main.free(dve.scalar_tensor_tensor(dst, tmp[:, i % 2 * 512:i % 2 * 512 + 512], 1.0, bank, ALU.add,
                                                   ALU.mult), key)

            dve.wait_ge(sem("ident_in"), 16)
            norm(0)
            dve.wait_ge(sem("par_in"), 16)
            dve.tensor_scalar(half_gn, par[:, PARAM["ret_gn"]:PARAM["ret_gn"] + 17], 0.5, None, ALU.mult).then_inc(
                sem("half_gn"), 1)
            low_parts("xT_ret")
            split_up_to(1)
            dve.wait_ge(sem("roots"), ROOTS.index("meta") + 1)
            dve.tensor_scalar(R[0:M, R3:R3 + D], R[0:M, R3:R3 + D], msum[0:M, 1:2], None, ALU.mult).then_inc(
                sem("meta_rows"), 1)
            dve.wait_ge(sem("tab_in"), 16)
            dve.tensor_copy(ident_b, ident)
            dve.tensor_copy(causal_b, tab[:, TB_CAUSAL:TB_CAUSAL + P]).then_inc(sem("masks"), 1)

            dve.wait_ge(sem("ret_in"), 16)
            cos, sin = R[:, R4 + RT_COS:R4 + RT_COS + T], R[:, R4 + RT_SIN:R4 + RT_SIN + T]
            for n in range(8):
                key = ("rqk", n)
                bank = wait(main, key).rearrange("p (f t) -> p f t", f=2)
                ta, tb = tmp[:, 0:512], tmp[:, 512:1024]
                if n:
                    dve.wait_ge(sem("rotated"), n)
                dve.tensor_tensor(ta.rearrange("p (f t) -> p f t", f=2), bank, over(cos, 2), ALU.mult)
                main.free(dve.tensor_tensor(tb.rearrange("p (f t) -> p f t", f=2), bank, over(sin, 2), ALU.mult), key)
                after_read(main, key)
                c0 = R1 + n * 512
                dve.tensor_tensor(R[:, c0:c0 + T], ta[:, 0:T], tb[:, T:2 * T], ALU.subtract)
                dve.tensor_tensor(R[:, c0 + T:c0 + 2 * T], tb[:, 0:T], ta[:, T:2 * T], ALU.add).then_inc(
                    sem("rotated"), 1)
            bank = wait(aux, "meta")
            for kt in range(KD):
                ins = dve.tensor_scalar(as_r(kt_cols(xT, kt, 0, M)), bank[:, kt * M:(kt + 1) * M],
                                        param("attn_norm_w_2", kt), None, ALU.mult)
            own.then_wait(ins)
            for kt in range(KD):
                ins = dve.scalar_tensor_tensor(as_r(kt_cols(xT2, kt, 0, M)), bank[:, kt * M:(kt + 1) * M],
                                               param("attn_norm_w_2", kt), value_of(kt_cols(xT, kt, 0, M)), ALU.mult,
                                               ALU.subtract)
            aux.free(ins, "meta")
            for hd in range(RH):
                key = ("rs", hd)
                bank = wait(aux, key)
                decay = R[:, R4 + RT_DECAY + hd * T:R4 + RT_DECAY + (hd + 1) * T]
                dve.tensor_tensor(PTb[:, hd * 384:hd * 384 + T], bank[:, 0:T], decay, ALU.mult)
                aux.free(dve.tensor_tensor(PTb[:, hd * 384 + T:(hd + 1) * 384], bank[:, T:T + P], decay[:, 0:P],
                                           ALU.mult), key)
            for half in range(2):
                for i in range(4 * half, 4 * half + 4):
                    bank = wait(aux, ("rpv", i // 2, i % 2))
                    ins = dve.bn_stats(bn[:, i % 4 * 6:(i % 4 + 1) * 6], bank)
                own.then_wait(ins)
                for i in range(4 * half, 4 * half + 4):
                    ins = dve.bn_aggr(mv[:, 2 * i:2 * i + 2], bn[:, i % 4 * 6:(i % 4 + 1) * 6])
                inverse_roots(("ret", half), ins)
                four = slice(4 * half, 4 * half + 4)
                dve.scalar_tensor_tensor(nmr[:, four], mv.rearrange("p (i c) -> p i c", c=2)[:, four, 0], -1.0,
                                         rrs[:, four], ALU.mult, ALU.mult).then_inc(sem("ret_norm"), 1)
                for c in (2 * half, 2 * half + 1):
                    for t in range(TT):
                        gate(("rg", c, t), R[:, R3 + t * 2048 + c * 512:R3 + t * 2048 + (c + 1) * 512])
                    if c == 2:
                        low_parts("yT0")
            low_parts("yT1")
            add_to_h([("ro", c, t) for c in range(2) for t in range(TT)])

            def ple(n, norm_n):
                if n == 1:
                    dve.wait_ge(sem("gain1_in"), 16)
                norm(norm_n)
                low_parts(f"xT_ple{n}")
                after_read(main, ("emb", n, 1, 1))
                for i in range(4):
                    c, t = i // 2, i % 2
                    after_read(main, ("pg", n, c, t))
                    g = tmp[:, i % 2 * 512:i % 2 * 512 + 512]
                    c0 = R2 + t * D + c * 512
                    own.then_wait(dve.scalar_tensor_tensor(g, g, 1.0, R[:, c0:c0 + 512], ALU.add, ALU.mult))
                    dve.tensor_tensor(hrow(t, c * 512, 512), hrow(t, c * 512, 512), g, ALU.add).then_inc(
                        sem("h_ready"), 1)
                    if n == 1:
                        dve.wait_ge(sem("h_ready"), 4 * n + i + 1)
                        dve.tensor_tensor(xn[:, t * D + c * 512:t * D + (c + 1) * 512], hrow(t, c * 512, 512),
                                          G1[:, c * 512:(c + 1) * 512], ALU.mult).then_inc(sem("gained"), 1)

            ple(0, 1)

            norm(2)
            low_parts("xT_kv")
            for n in range(2):
                split_up_to(main.unit["kvA", 5 + 2 * n] + HIGH - 1)
                dve.wait_ge(sem("blocks_high"), n + 1)
                low_part(*blocks(n)).then_inc(sem("blocks_low"), 1)
            dve.wait_ge(sem("gates_high"), 1)
            low_part(gates_high[:, :], side_sb[:, SIDE_G2:SIDE_G2 + KD * 16]).then_inc(sem("gates_low"), 1)
            for n in range(2):
                bank = wait(aux, ("cmp", n))[0:CMP_ROWS, 0:256]
                g = tmp[0:CMP_ROWS, n * 512:n * 512 + 256]
                dve.wait_ge(sem("gelu_square"), n + 1)
                own.then_wait(dve.tensor_scalar(g, g, 0.044715, 1.0, ALU.mult, ALU.add))
                dve.tensor_tensor(g, g, bank, ALU.mult).then_inc(sem("gelu_in"), 1)
                dve.wait_ge(sem("gelu_tanh"), n + 1)
                aux.free(dve.scalar_tensor_tensor(tmp[0:CMP_ROWS, n * 512 + 256:n * 512 + 512], g, 1.0, bank, ALU.add,
                                                   ALU.mult), ("cmp", n))
            for n in range(2):
                bank = wait(aux, ("hT", n))
                aux.free(dve.tensor_copy(Pf[:, n * 120:(n + 1) * 120], bank[:, 0:120]), ("hT", n))
            bank = wait(aux, ("c2", 0))
            aux.free(dve.tensor_scalar(Pf[:, CMP_K:CMP_K + CMP_ROWS], bank[:, 0:CMP_ROWS], 0.5, None, ALU.mult), ("c2", 0))
            bank = wait(aux, ("c2", 1))
            aux.free(dve.tensor_scalar(Pf[0:CMP_N, CMP_V:CMP_V + 512], bank[0:CMP_N, :], 0.5, None, ALU.mult), ("c2", 1))
            after_read(main, ("bg", 1))
            own.then_wait(dve.tensor_scalar(bgt, bgt, 1.0, 0.5, ALU.add, ALU.mult))

            def heads(ap):
                return ap.rearrange("p (h n) -> p h n", h=NSA_H)

            for kind, i in nsa_order():
                if kind == "S":
                    b, h0, nh = STEPS[i]
                    for br, name in enumerate(("s", "w")):
                        bank = wait(main, (name, i))
                        c0 = i * 8 + br * nh
                        dve.tensor_reduce(nmx[:, c0:c0 + nh], bank.rearrange("p (h n) -> p h n", h=nh), AX, ALU.max,
                                          negate=True).then_inc(sem("nsa_max"), 1)
                elif kind == "H":
                    low_parts("oT0")
                elif kind == "C":
                    for b in range(TT):
                        cx = xn[:, b * 240:(b + 1) * 240]
                        bank = wait(aux, ("cs", b))
                        mask = tab[:, TB_CMP + b * CMP_N:TB_CMP + (b + 1) * CMP_N]
                        aux.free(dve.tensor_tensor(heads(cx), heads(bank[:, 0:240]), over(mask, NSA_H), ALU.add), ("cs", b))
                        after_read(aux, ("cs", b))
                        own.then_wait(dve.tensor_reduce(cst[:, b * 16:(b + 1) * 16], heads(cx), AX, ALU.max))
                        dve.tensor_tensor(heads(cx), heads(cx), spread(cst[:, b * 16:(b + 1) * 16], CMP_N),
                                          ALU.subtract).then_inc(sem("cmp_shifted"), 1)
                    for b in range(TT):
                        cx = xn[:, b * 240:(b + 1) * 240]
                        cs = cst[:, b * 16:(b + 1) * 16]
                        dve.wait_ge(sem("cmp_exp"), b + 1)
                        own.then_wait(dve.tensor_reduce(cs, heads(cx), AX, ALU.add))
                        own.then_wait(dve.reciprocal(cs, cs))
                        own.then_wait(dve.scalar_tensor_tensor(
                            cs, cs, tab[:, TB_ROW + b:TB_ROW + b + 1],
                            bgt[:, b * 48:(b + 1) * 48].rearrange("p (h c) -> p h c", c=3)[:, :, 0], ALU.mult, ALU.mult))
                        dve.tensor_tensor(heads(cx), heads(cx), spread(cs, CMP_N), ALU.mult).then_inc(sem("cmp_p"), 1)
                elif kind == "N":
                    b, h0, nh = STEPS[i]
                    after_read(main, ("w", i))
                    sc = esc[:, i * 8:i * 8 + 2 * nh]
                    own.then_wait(dve.reciprocal(sc, esum[:, i * 8:i * 8 + 2 * nh]))
                    g = bgt[:, b * 48 + h0 * 3:b * 48 + (h0 + nh) * 3].rearrange("p (n c) -> p c n", c=3)[:, 1:3, :]
                    sc = sc.rearrange("p (c n) -> p c n", c=2)
                    dve.tensor_tensor(sc, sc, g, ALU.mult).then_inc(sem("nsa_scale"), 1)
                elif kind == "G":
                    for t in range(TT):
                        gate(("ng", i, t), R[:, R4 + t * 2048 + i * 512:R4 + t * 2048 + (i + 1) * 512])
                elif kind == "T":
                    b, h0, nh = STEPS[i]
                    slot = i % 2
                    bank = wait(aux, ("sT", i))
                    aux.free(dve.tensor_copy(PTb[:, slot * 1024:slot * 1024 + 512], bank), ("sT", i))
                    bank = wait(aux, ("cT", i))
                    aux.free(dve.tensor_copy(nw[0:CMP_N, slot * 512:slot * 512 + nh * P], bank[0:CMP_N, 0:nh * P]),
                             ("cT", i))
                else:
                    b, h0, nh = STEPS[i]
                    bank = wait(aux, ("o", i))
                    after_read(main, ("ng", h0 // NSA_HPG, b))
                    y = R[:, R4 + b * 2048 + h0 * P:R4 + b * 2048 + (h0 + nh) * P]
                    aux.free(dve.tensor_tensor(y, y, bank[:, 0:nh * P], ALU.mult), ("o", i))
            low_parts("oT1")
            add_to_h([("no", c, t) for c in range(2) for t in range(TT)])
            ple(1, 3)

            roots(5)
            to_diagonal(5)
            low_parts("xT_attn")
            roots(4)
            for t in range(TT):
                dve.tensor_scalar(hrow(t), xnrow(t), rstd[:, 8 + t:9 + t], None, ALU.mult).then_inc(sem("x2_ready"), 1)
            raw = R[:, R1:R1 + 12 * RAW_W].rearrange("p (j t) -> p j t", j=12)
            dve.memset(raw[:, :, 0:3], 0.0)
            own.then_wait(dve.memset(SM["ones"], 1.0))
            for key, rows_, name, bias in (("ga", 4, "ga", "dt_bias_2"), ("ff", 8, "ff", "fgate_b_2")):
                bank = wait(main, key)
                main.free(dve.tensor_scalar(SM[name], bank[0:rows_, 0:TM], param(bias, 0, rows_), None, ALU.add), key)
            after_read(main, "gb")
            dve.tensor_scalar(SM["beta"], SM["beta"], 1.0, 0.5, ALU.add, ALU.mult).then_inc(sem("scans"), 1)

            def conv(jj):
                j = GIN_TILES[jj]
                after_read(main, ("gin", jj))
                y = R[:, R2 + j * TM:R2 + (j + 1) * TM]
                for k in range(3):
                    ins = dve.scalar_tensor_tensor(y, raw[:, j, k:k + TM], param("conv_w_2", 12 * k + j), y, ALU.mult,
                                                   ALU.add)
                    if k < 2:
                        own.then_wait(ins)
                ins.then_inc(sem("conv_done"), 1)

            def silu(jj):
                j = GIN_TILES[jj]
                y = R[:, R2 + j * TM:R2 + (j + 1) * TM]
                dve.wait_ge(sem("conv_tanh"), jj + 1)
                dve.scalar_tensor_tensor(y, tmp[:, jj % 2 * 512:jj % 2 * 512 + TM], 1.0, y, ALU.add,
                                         ALU.mult).then_inc(sem("conv_silu"), 1)

            for jj in range(12):
                conv(jj)
                if jj:
                    silu(jj - 1)
            silu(11)
            dve.wait_ge(sem("a_exp"), 1)
            own.then_wait(dve.tensor_scalar(cst[0:4, 1:2], cst[0:4, 0:1], -1.0, None, ALU.mult))
            split_up_to(main.unit["fin", 7] + HIGH - 1)
            dve.wait_ge(sem("soft_logs"), 1)
            dve.scalar_tensor_tensor(SM["la"], SM["ga"], 0.0, SM["la"], ALU.max, ALU.add)
            own.then_wait(dve.scalar_tensor_tensor(SM["lf"], SM["ff"], 0.0, SM["lf"], ALU.min, ALU.subtract))
            own.then_wait(dve.tensor_scalar(SM["la"], SM["la"], cst[0:4, 1:2], None, ALU.mult))
            for t0, n in CHUNKS:
                dve.tensor_tensor_scan(SM["gc"][:, t0:t0 + n], SM["ones"][0:4, 0:n], SM["la"][:, t0:t0 + n], 0.0,
                                       ALU.mult, ALU.add).then_inc(sem("scans"), 1)
            own.then_wait(dve.tensor_tensor_scan(SM["ff"], SM["ones"], SM["lf"], 0.0, ALU.mult, ALU.add))
            dve.tensor_scalar(SM["negc"], SM["ff"], -1.0, None, ALU.mult).then_inc(sem("fox_c"), 1)
            bank = wait(aux, "ss")
            aux.free(dve.tensor_scalar(SM["r8"], bank[0:8, 0:TM], 0.25, EPS, ALU.mult, ALU.add), "ss")
            dve.wait_ge(sem("qk_root"), 1)
            dve.reciprocal(SM["r8"], SM["r8"]).then_inc(sem("qk_factor"), 1)
            dve.wait_ge(sem("conv_silu"), 12)
            for j in range(8):
                bank = wait(aux, ("rb", j))
                y = R[:, R2 + j * TM:R2 + (j + 1) * TM]
                aux.free(dve.scalar_tensor_tensor(y, y, 0.5 * float(P) ** -0.5 if j < 4 else 0.5, bank[:, 0:TM],
                                                  ALU.mult, ALU.mult), ("rb", j))
            bank = wait(aux, "tok")
            dve.tensor_copy(tk[0:M, 0:8], bank[0:M, 0:8])
            aux.free(dve.tensor_copy(tk[:, 8:24], bank[:, 8:24]), "tok")
            for t in range(TT):
                gate(("gz", t), R[:, R4 + t * 512:R4 + (t + 1) * 512])

            after_read(aux, "tok")
            for c, (t0, n) in enumerate(CHUNKS):
                def four(ap, w=None):
                    return ap.rearrange("p (h n) -> p h n", h=GH)

                gc, beta = tk[0:n, c * 8:c * 8 + 4], tk[0:n, c * 8 + 4:c * 8 + 8]
                d, d1, d2 = (xn[0:n, s * 512:s * 512 + 4 * n] for s in range(3))
                bank = wait(aux, ("bc", c))
                own.then_wait(dve.tensor_copy(g3[:, c * 12 + 8:c * 12 + 12], four(bank[:, 0:4 * n])[:, :, n - 1]))
                ins = dve.tensor_tensor(four(d), four(bank[0:n, 0:4 * n]), spread(gc, n), ALU.subtract)
                if c:
                    ins.then_inc(sem("bc_read"), 1)
                    dve.wait_ge(sem("bc_read"), c)
                else:
                    aux.free(ins, ("bc", c))
                    after_read(aux, ("bc", c))
                dve.tensor_copy(g3[0:n, c * 12:c * 12 + 4], gc)
                dve.tensor_tensor(g3[0:n, c * 12 + 4:c * 12 + 8], g3[0:n, c * 12 + 8:c * 12 + 12], gc,
                                  ALU.subtract).then_inc(sem("log_decays"), 1)
                if c:
                    dve.tensor_tensor(four(d2), four(d), over(tab[0:n, TB_INCL:TB_INCL + n], GH), ALU.min)
                dve.tensor_tensor(four(d1), four(d), over(tab[0:n, TB_STRICT:TB_STRICT + n], GH), ALU.max).then_inc(
                    sem("clamped"), 1)
                dve.wait_ge(sem("decays_small"), c + 1)
                dve.tensor_tensor(be[0:n, c * 4:c * 4 + 4], beta, e3[0:n, c * 12:c * 12 + 4], ALU.mult)
                own.then_wait(dve.tensor_scalar(hb[0:n, c * 4:c * 4 + 4], beta, 0.5, None, ALU.mult))
                dve.wait_ge(sem("decay_ready"), c + 1)
                own.then_wait(dve.tensor_tensor(four(d1), four(d1), spread(beta, n), ALU.mult))
                bank = wait(aux, ("kk", c))
                a0 = 2 * C_ALL + C_OFF[c]
                aux.free(dve.tensor_tensor(PTb[0:n, a0:a0 + 4 * n], d1, bank[0:n, 0:4 * n], ALU.mult), ("kk", c))
                if c:
                    bank = wait(aux, ("qk", c))
                    k0 = R4 + 3072 + (c - 1) * 512
                    aux.free(dve.tensor_tensor(R[:, k0:k0 + 512], d2, bank, ALU.mult), ("qk", c))
                    after_read(aux, ("bc", c))
                    q = R[:, R2:R2 + 12 * TM].rearrange("p (j t) -> p j t", j=12)[:, 0:4, t0:t0 + n]
                    dve.tensor_tensor(q, q, four(xn[:, 1536:2048]), ALU.mult).then_inc(sem("q_scaled"), 1)

                def rows_of(base):
                    buf, b0 = base
                    return four(buf[0:n, b0 + c * 512:b0 + (c + 1) * 512])

                bank = four(wait(aux, ("kt", c))[0:n, :])
                if c < 2:
                    dve.tensor_tensor(rows_of(KDEC), bank, spread(e3[0:n, c * 12 + 4:c * 12 + 8], P), ALU.mult)
                aux.free(dve.tensor_tensor(rows_of(RK), bank, spread(be[0:n, c * 4:c * 4 + 4], P), ALU.mult), ("kt", c))
                bank = four(wait(aux, ("vt", c))[0:n, :])
                aux.free(dve.tensor_tensor(rows_of(RV), bank, spread(hb[0:n, c * 4:c * 4 + 4], P), ALU.mult), ("vt", c))

            state = R[:, R1 + 3072:R1 + 3584]
            for kind, *key in gdn_fox_order():
                if kind == "H":
                    low_parts("mT1")
                elif kind == "Lx":
                    lv, c = key
                    n = CHUNKS[c][1]
                    by = wait(aux, ("y", lv, c))
                    if not last_level(lv, c):
                        bx = aux.at(("x", lv, c))
                        X = PTb[0:n, C_OFF[c]:C_OFF[c] + 4 * n]
                        aux.free(dve.tensor_tensor(X, X, bx[0:n, 0:4 * n], ALU.subtract), ("x", lv, c))
                    Y = PTb[0:n, C_ALL + C_OFF[c]:C_ALL + C_OFF[c] + 4 * n]
                    aux.free(dve.tensor_tensor(Y, Y, by[0:n, 0:4 * n], ALU.subtract), ("y", lv, c))
                elif kind == "Fs":
                    hd = key[0]
                    bank = wait(aux, ("fs", hd))
                    dve.tensor_reduce(fnm[:, 2 * hd:2 * hd + 1], bank[:, 0:P + M], AX, ALU.max, negate=True)
                    dve.tensor_reduce(fnm[:, 2 * hd + 1:2 * hd + 2], bank[:, P + M:3 * P + 2 * M], AX, ALU.max,
                                      negate=True).then_inc(sem("fox_max"), 1)
                elif kind == "Ft":
                    hd = key[0]
                    after_read(aux, ("fs", hd))
                    dve.reciprocal(frs[:, 2 * hd:2 * hd + 2], fsum[:, 2 * hd:2 * hd + 2]).then_inc(sem("fox_recip"), 1)
                    bank = wait(aux, ("fm", hd))
                    c0 = hd % 2 * 640 + 384
                    aux.free(dve.tensor_copy(PfT[0:M, c0:c0 + 256], bank[0:M, 0:256]), ("fm", hd))
                elif kind == "V":
                    c = key[0]
                    if c == 0:
                        aux.free(dve.tensor_copy(state, wait(aux, ("st", 0))), ("st", 0))
                    if c == 1:
                        wait(aux, ("go", 1))
                        s3 = state.rearrange("p (h n) -> p h n", h=GH)
                        own.then_wait(dve.tensor_tensor(s3, s3, spread(e3[:, c * 12 + 8:c * 12 + 12], P), ALU.mult))
                        bank = wait(aux, ("st", 1))
                        aux.free(dve.tensor_tensor(state, state, bank, ALU.add), ("st", 1))
                    if c:
                        dve.wait_ge(sem("go_square"), c)
                        s4 = slice(4 * c - 4, 4 * c)
                        own.then_wait(dve.tensor_reduce(gss[:, s4], tmp[:, 0:512].rearrange("p (h n) -> p h n", h=GH), AX,
                                                        ALU.add))
                        inverse_roots(("go", c), dve.tensor_scalar(gss[:, s4], gss[:, s4], 1.0 / P, None, ALU.mult))
                        on = tmp[:, 512:1024]
                        on3 = on.rearrange("p (h n) -> p h n", h=GH)
                        own.then_wait(dve.tensor_tensor(on3, on3, spread(grs[:, s4], P), ALU.mult))
                        m0 = R4 + 1024 + (c - 1) * D
                        dve.tensor_tensor(R[:, m0:m0 + 512], on, R[:, R4 + (c - 1) * 512:R4 + c * 512],
                                          ALU.mult).then_inc(sem("mix_ready"), 1)
            low_parts("mT0")
            add_to_h([("mo", c, t) for c in range(2) for t in range(TT)])
            norm(6)
            low_parts("xT_ffn")

            def hidden_low(n):
                dve.wait_ge(sem("hidden_high"), n + 1)
                low_part(R[:, n * 512:(n + 1) * 512], R[:, 22 * T + n * 512:22 * T + (n + 1) * 512]).then_inc(
                    sem("hidden_low"), 1)

            for n in range(11):
                a = xn[:, n % 2 * 512:n % 2 * 512 + 512]
                gate(("fg", n), a)
                after_read(main, ("fg", n))
                bank = wait(main, ("fu", n))
                product = R[:, 22 * T + n * 512:22 * T + (n + 1) * 512]
                main.free(dve.scalar_tensor_tensor(product, a, 0.5, bank, ALU.mult, ALU.mult), ("fu", n))
                if n:
                    hidden_low(n - 1)
            hidden_low(10)
            add_to_h([("dn", c, t) for c in range(2) for t in range(TT)])
            roots(7)
            dve.wait_ge(sem("gain2_in"), 16)
            for t in range(TT):
                dve.scalar_tensor_tensor(xnrow(t), hrow(t), rstd[:, 14 + t:15 + t], G1[:, D:2 * D], ALU.mult,
                                         ALU.mult).then_inc(sem("out_rows"), 1)

        @block.gpsimd
        def _(pool):
            own = Marks(pool, "pool_step")

            own.then_wait(pool.memset(power, -0.5))

            def inverse_root(dst, src):
                own.then_wait(pool.tensor_scalar(dst, src, EPS, None, ALU.add))
                rows, n = dst.shape
                return pool.tensor_tensor(dst, dst, power[0:rows, :].to_broadcast([rows, n]), ALU.pow)

            def signal(name, ins):
                assert ROOTS.index(name) == rooted[0]
                rooted[0] += 1
                ins.then_inc(sem("roots"), 1)

            rooted, asked = [0], [0]

            def root_for_vector(name, dst, src):
                asked[0] += 1
                pool.wait_ge(sem("root_in"), asked[0])
                signal(name, inverse_root(dst, src))

            def mean_squares(n):
                pool.wait_ge(sem("norm_sums"), n + 1)
                own.then_wait(pool.tensor_tensor(var, sums[:, 4 * n:4 * n + 2], sums[:, 4 * n + 2:4 * n + 4], ALU.add))

            def norm(n):
                mean_squares(n)
                signal(("norm", n), inverse_root(rstd[:, 2 * n:2 * n + 2], var))

            norm(0)
            pool.wait_ge(sem("meta_sum"), 1)
            signal("meta", inverse_root(msum[0:M, 1:2], msum[0:M, 0:1]))
            for i in range(8):
                if i % 4 == 0:
                    four = slice(i, i + 4)
                    root_for_vector(("ret", i // 4), rrs[:, four], mv.rearrange("p (i c) -> p i c", c=2)[:, four, 1])
                hd, t = i // 2, i % 2
                wait_read(pool, aux, ("rpv", hd, t))
                wait_read(pool, main, ("rg", hd, t))
                y = R[:, R3 + t * 2048 + hd * 512:R3 + t * 2048 + (hd + 1) * 512]
                pool.tensor_tensor(y, y, xn[:, i % 4 * 512:(i % 4 + 1) * 512], ALU.mult).then_inc(sem("ret_y"), 1)
            norm(1)
            norm(2)
            for n, name in enumerate(("cmp_pe_k", "cmp_pe_v")):
                wait_read(pool, main, ("kvA", 2 * n + 1))
                src = R[:, R1 + n * D:R1 + (n + 1) * D].rearrange("p (g m l) -> p l g m", g=NSA_G, l=CMP_STRIDE)
                for o in range(2):
                    _, lo = blocks(n)
                    dst = lo[:, o * CMP_STRIDE * CMP_ROWS:(o + 1) * CMP_STRIDE * CMP_ROWS].rearrange("p (l g m) -> p l g m", g=NSA_G, m=CMP_N)
                    p0 = PARAM[name] + o * CMP_STRIDE
                    pe_cols = par[:, p0:p0 + CMP_STRIDE].unsqueeze(2).unsqueeze(3).to_broadcast(
                        [P, CMP_STRIDE, NSA_G, CMP_N])
                    ins = pool.tensor_tensor(dst, src[:, :, :, o:o + CMP_N], pe_cols, ALU.add)
                ins.then_inc(sem("blocks_ready"), 1)
            for i, (b, h0, nh) in enumerate(STEPS):
                pool.wait_ge(sem("nsa_scale"), i + 1)
                c0 = R2 + 2048 + i % 2 * 1024
                p = R[:, c0:c0 + 1024].rearrange("p (h n) -> p h n", h=2 * nh)
                pool.tensor_tensor(p, p, spread(esc[:, i * 8:i * 8 + 2 * nh], 1024 // (2 * nh)), ALU.mult).then_inc(
                    sem("nsa_p"), 1)
            norm(3)
            r1, r2 = rstd[:, 8:10], rstd[:, 10:12]
            mean_squares(4)
            own.then_wait(pool.tensor_scalar(r1, var, EPS, None, ALU.add))
            own.then_wait(pool.tensor_scalar(r2, r1, EPS, None, ALU.mult))
            mean_squares(5)
            own.then_wait(pool.tensor_tensor(r2, r2, var, ALU.add))
            exponent = power.to_broadcast([P, 2])
            signal(("norm", 5), pool.tensor_tensor(r2, r2, exponent, ALU.pow))
            signal(("norm", 4), pool.tensor_tensor(r1, r1, exponent, ALU.pow))
            aux.wait(pool, "ss")
            for c, (t0, n) in enumerate(CHUNKS):
                for base in (0, C_ALL):
                    c0 = base + C_OFF[c]
                    pool.tensor_copy(PTb[0:n, c0:c0 + 4 * n].rearrange("p (h n) -> p h n", h=GH),
                                     over(ident[0:n, 0:n], GH)).then_inc(sem("xy_init"), 1)
            for lv, c in LEVEL_LIST:
                n = CHUNKS[c][1]
                wait_read(pool, aux, ("kk", c))
                main.wait(pool, ("gz", 1))
                if lv:
                    aux.wait(pool, ("z", lv - 1, c))
                a0, m0 = 2 * C_ALL + C_OFF[c], TB_LEVEL + lv * P
                pool.tensor_tensor(xT2[0:n, C_OFF[c]:C_OFF[c] + 4 * n].rearrange("p (h n) -> p h n", h=GH),
                                   PTb[0:n, a0:a0 + 4 * n].rearrange("p (h n) -> p h n", h=GH),
                                   over(tab[0:n, m0:m0 + n], GH), ALU.mult).then_inc(sem("level_part"), 1)
            for c in (1, 2):
                s4 = slice(4 * c - 4, 4 * c)
                root_for_vector(("go", c), grs[:, s4], gss[:, s4])
            norm(6)
            norm(7)


_INS = ["x", "meta", "weights", "side", "params", "tabs", "ret_tabs", "p_t", "gains"]


def kernel(**inputs):
    import numpy as _np
    import concourse.bacc as _bacc
    from concourse import mybir as _mybir
    from concourse.bass_utils import run_bass_kernel_spmd as _run

    a = {k: _np.asarray(v) for k, v in inputs.items()}
    w = {}
    for name in ("ret_w_in", "ret_w_out", "nsa_w_in", "nsa_w_out", "w_in_2", "w_out_2", "w_gate_2", "w_up_2", "w_down_2"):
        w[name] = a[name][0]
    for name in ("kv_w", "cmp_w1_k", "cmp_w1_v"):
        w[name] = a[name]
    for i in range(2):
        w[f"ple_w_gate{i}"], w[f"ple_w_emb{i}"] = a["ple_w_gate"][i], a["ple_w_emb"][i]

    def tiles(m, k0, kt, c0, n):
        return m[k0 * P:(k0 + kt) * P, c0:c0 + n].reshape(kt, P, n).transpose(1, 0, 2).reshape(P, kt * n)

    shape_of = {"A": (8, 256), "B": (4, 512), "E": (2, 1024), "C": (8, 256)}
    weights = _np.empty((NU, P, UNIT), _np.float32)
    for u, (name, kind, k0, c0) in enumerate(UNITS):
        kt, n = shape_of[kind]
        weights[u] = tiles(w[name], k0, kt, c0, n)
    side = _np.concatenate([
        tiles(w["nsa_w_in"], 0, KD, 4096, 48),
        tiles(_np.concatenate([w["w_in_2"][:, 2048:2056], w["w_in_2"][:, 3592:3600]], 1), 0, KD, 0, 16),
        tiles(a["cmp_w2_k"], 0, 2, 0, P), tiles(a["cmp_w2_v"], 0, 2, 0, P)], 1)

    def columns(v):
        return v.reshape(-1, P).T

    def column(v):
        out = _np.zeros((P, 1), _np.float32)
        out[:v.size, 0] = v.reshape(-1)
        return out

    params = _np.concatenate([
        columns(a["ret_norm"][0]), columns(a["kv_norm"]), columns(a["nsa_norm"][0]), columns(a["ple_norm"][0]),
        columns(a["ple_norm"][1]), columns(a["attn_norm_w_2"][0]), columns(a["ffn_norm_w_2"][0]),
        columns(a["ret_gn"][0]), columns(a["gdn_norm_w_2"][0]), a["cmp_pe_k"].T, a["cmp_pe_v"].T,
        columns(a["conv_w_2"][0].reshape(-1)), column(a["a_log_2"]), column(a["dt_bias_2"]), column(a["fgate_b_2"])], 1)
    p_t = _np.concatenate([tiles(_np.ascontiguousarray(a["p"][i, 0].T), 0, 2, 0, T) for i in range(2)], 1)
    tabs, ret_tabs = tables()
    arrays = {
        "x": a["x"][0], "meta": a["meta_tokens_2"], "weights": weights, "side": side, "params": params,
        "tabs": tabs, "ret_tabs": ret_tabs, "p_t": p_t,
        "gains": _np.stack([a["final_norm"], a["final_norm_w_2"]]),
    }
    nc = _bacc.Bacc("TRN2", target_bir_lowering=False, num_devices=1)
    args, feed = [], {}
    for name in _INS:
        feed[f"in_{name}"] = _np.ascontiguousarray(arrays[name])
        args.append(nc.dram_tensor(f"in_{name}", feed[f"in_{name}"].shape, _mybir.dt.from_np(feed[f"in_{name}"].dtype),
                                   kind="ExternalInput").ap())
    args.append(nc.dram_tensor("out_0", (T, D), F32, kind="ExternalOutput").ap())
    two_models_kernel(nc, *args)
    r = _run(nc, [feed], core_ids=[0])
    return r.results[0]["out_0"].reshape(1, T, D)
```
